# Optimizing a Trainium2 kernel written in Bass

```python
import math
import jax, jax.numpy as jnp
from jax import lax
import numpy as np

D_MODEL = 1024
BATCH = 1
SEQ = 512
DEPTH = 1

N_BRANCH = 4
D_MIX = D_MODEL // N_BRANCH
HEAD_A = 64
H_A = D_MIX // HEAD_A
LORA_W = 32
LORA_A = 32
LORA_V = 32
LORA_G = 64
LNX_EPS = 64e-5
CHUNK = 128
GROUP_B = 64
G_B = D_MIX // GROUP_B
CONV_K = 3
GROUP_D = 16
G_D = D_MIX // GROUP_D
N_STATE = 64
D_FF = 4 * D_MODEL
EPS = 1e-6
LN_EPS = 1e-5

A_COLS = 3 * D_MIX + LORA_W + LORA_A + LORA_G
B_COLS = 2 * D_MIX
C_COLS = 3 * D_MIX
D_COLS = D_MIX
GATE_COLS = N_BRANCH * D_MODEL
OFF_B = A_COLS
OFF_C = OFF_B + B_COLS
OFF_D = OFF_C + C_COLS
OFF_G = OFF_D + D_COLS
N_IN = OFF_G + GATE_COLS


def rms_norm(x, g):
    xf = x.astype(jnp.float32)
    return xf * lax.rsqrt(jnp.mean(xf * xf, axis=-1, keepdims=True) + EPS) * g.astype(jnp.float32)

def layer_norm(x, w, b, eps):
    xf = x.astype(jnp.float32)
    mu = jnp.mean(xf, axis=-1, keepdims=True)
    var = jnp.mean(jnp.square(xf - mu), axis=-1, keepdims=True)
    return (xf - mu) * lax.rsqrt(var + eps) * w.astype(jnp.float32) + b.astype(jnp.float32)

def shift_prev(p):
    return jnp.pad(p, ((0, 0), (1, 0), (0, 0)))[:, :-1]

def wkv7(r, w, k, v, a, b):
    bsz, _, nh, n = r.shape

    def step(state, inp):
        r_t, w_t, k_t, v_t, a_t, b_t = inp
        sa = jnp.einsum('bhij,bhj->bhi', state, a_t)
        state = (state * w_t[:, :, None, :] + sa[..., None] * b_t[:, :, None, :]
                 + v_t[..., None] * k_t[:, :, None, :])
        return state, jnp.einsum('bhij,bhj->bhi', state, r_t)

    xs = tuple(jnp.moveaxis(t, 1, 0) for t in (r, w, k, v, a, b))
    s0 = jnp.zeros((bsz, nh, n, n), jnp.float32)
    _, out = lax.scan(step, s0, xs)
    return jnp.moveaxis(out, 0, 1)

def rwkv7_mixer(p, v_first, v_mix, mu, w0, w2, a0, a2, g2, k_k, k_a, r_k, lnx_w, lnx_b, w_out):
    bsz, seq, _ = p.shape
    p = p + (shift_prev(p) - p) * mu
    r = p[..., :D_MIX]
    k = p[..., D_MIX:2 * D_MIX]
    v = p[..., 2 * D_MIX:3 * D_MIX]
    wd = p[..., 3 * D_MIX:3 * D_MIX + LORA_W]
    ad = p[..., 3 * D_MIX + LORA_W:3 * D_MIX + LORA_W + LORA_A]
    gd = p[..., 3 * D_MIX + LORA_W + LORA_A:]
    log_w = -jax.nn.softplus(-(w0 + jnp.tanh(wd) @ w2)) - 0.5
    decay = jnp.exp(-jnp.exp(log_w))
    if v_mix is None:
        v_first = v
    else:
        v0, v1, v2 = v_mix
        v = v + (v_first - v) * jax.nn.sigmoid(v0 + (v @ v1) @ v2)
    a = jax.nn.sigmoid(a0 + ad @ a2)
    g = jax.nn.sigmoid(gd) @ g2

    def heads(t):
        return t.reshape(bsz, seq, H_A, HEAD_A).astype(jnp.float32)

    kk = heads(k * k_k)
    kk = kk / jnp.maximum(jnp.sqrt(jnp.sum(kk * kk, axis=-1, keepdims=True)), 1e-12)
    k = k * (1.0 + (a - 1.0) * k_a)
    rh, kh, vh, ah = heads(r), heads(k), heads(v), heads(a)
    o = wkv7(rh, heads(decay), kh, vh, -kk, kk * ah)
    o = layer_norm(o, lnx_w.reshape(H_A, HEAD_A), lnx_b.reshape(H_A, HEAD_A), LNX_EPS)
    o = o + jnp.sum(rh * kh * r_k, axis=-1, keepdims=True) * vh
    return (o.reshape(bsz, seq, D_MIX) * g) @ w_out, v_first

def spatial_gating_mixer(p, ln_w, ln_b, w_s, b_s, w_out):
    bsz, seq, _ = p.shape
    z = jax.nn.gelu(p)
    u = z[..., :D_MIX]
    v = layer_norm(z[..., D_MIX:], ln_w, ln_b, LN_EPS)
    v = v.reshape(bsz, seq // CHUNK, CHUNK, G_B, GROUP_B)
    mask = jnp.tril(jnp.ones((CHUNK, CHUNK), jnp.float32))
    mixed = jnp.einsum('gts,bnsgc->bntgc', w_s * mask, v) + b_s.T[None, None, :, :, None]
    return (u * mixed.reshape(bsz, seq, D_MIX)) @ w_out

def short_conv_mixer(p, conv_w, w_out):
    seq = p.shape[1]
    bg = p[..., :D_MIX]
    cg = p[..., D_MIX:2 * D_MIX]
    xin = p[..., 2 * D_MIX:]
    zp = jnp.pad(cg * xin, ((0, 0), (CONV_K - 1, 0), (0, 0)))
    y = sum(conv_w[j] * zp[:, j:j + seq] for j in range(CONV_K))
    return (bg * y) @ w_out

def _complex_affine_combine(e1, e2):
    a1r, a1i, b1r, b1i = e1
    a2r, a2i, b2r, b2i = e2
    return (a2r * a1r - a2i * a1i,
            a2r * a1i + a2i * a1r,
            a2r * b1r - a2i * b1i + b2r,
            a2r * b1i + a2i * b1r + b2i)

def s5_mixer(u, a_re, a_im, b_re, b_im, c_re, c_im, d, log_dt, glu_w):
    f32 = jnp.float32
    bsz, seq, _ = u.shape
    u32 = u.astype(f32)
    ug = u32.reshape(bsz, seq, G_D, GROUP_D)
    lam_re = jnp.minimum(a_re.astype(f32), -1e-4)
    lam_im = a_im.astype(f32)
    dt = jnp.exp(log_dt.astype(f32))[:, None]
    mag = jnp.exp(lam_re * dt)
    ab_re = mag * jnp.cos(lam_im * dt)
    ab_im = mag * jnp.sin(lam_im * dt)
    den = lam_re * lam_re + lam_im * lam_im
    q_re = ((ab_re - 1.0) * lam_re + ab_im * lam_im) / den
    q_im = (ab_im * lam_re - (ab_re - 1.0) * lam_im) / den
    bb_re = q_re[..., None] * b_re - q_im[..., None] * b_im
    bb_im = q_re[..., None] * b_im + q_im[..., None] * b_re
    bu_re = jnp.einsum('gnc,bsgc->bsgn', bb_re, ug)
    bu_im = jnp.einsum('gnc,bsgc->bsgn', bb_im, ug)
    ar = jnp.broadcast_to(ab_re, bu_re.shape)
    ai = jnp.broadcast_to(ab_im, bu_im.shape)
    _, _, x_re, x_im = lax.associative_scan(_complex_affine_combine, (ar, ai, bu_re, bu_im), axis=1)
    y = (jnp.einsum('gcn,bsgn->bsgc', c_re, x_re) - jnp.einsum('gcn,bsgn->bsgc', c_im, x_im))
    y = y.reshape(bsz, seq, D_MIX) + d * u32
    h = jax.nn.gelu(y) @ glu_w
    return h[..., :D_MODEL] * jax.nn.sigmoid(h[..., D_MODEL:])

def first_inputs(seed: int = 0) -> dict:
    key = jax.random.key(seed)
    ks = iter(jax.random.split(key, 64))
    f32 = jnp.float32
    L = DEPTH

    def nrm(shape, scale):
        return scale * jax.random.normal(next(ks), shape, f32)

    def uni(shape, lo, hi):
        return jax.random.uniform(next(ks), shape, f32, lo, hi)

    return {
        'x': nrm((BATCH, SEQ, D_MODEL), 1.0),
        'c': nrm((BATCH, D_MODEL), 1.0),
        'ada_w': nrm((L, D_MODEL, 6 * D_MODEL), 0.5 * D_MODEL ** -0.5),
        'ada_b': nrm((L, 6 * D_MODEL), 0.02),
        'norm_mix_g': 1.0 + nrm((L, D_MODEL), 0.1),
        'w_in': nrm((L, D_MODEL, N_IN), D_MODEL ** -0.5),
        'rwkv_mu': uni((L, A_COLS), 0.0, 1.0),
        'rwkv_w0': uni((L, D_MIX), -6.0, -1.0),
        'rwkv_w2': nrm((L, LORA_W, D_MIX), 0.1),
        'rwkv_a0': nrm((L, D_MIX), 0.1),
        'rwkv_a2': nrm((L, LORA_A, D_MIX), 0.1),
        'rwkv_g2': nrm((L, LORA_G, D_MIX), LORA_G ** -0.5),
        'rwkv_v0': 1.0 + nrm((L - 1, D_MIX), 0.1),
        'rwkv_v1': nrm((L - 1, D_MIX, LORA_V), D_MIX ** -0.5),
        'rwkv_v2': nrm((L - 1, LORA_V, D_MIX), 0.1),
        'rwkv_kk': 0.85 + nrm((L, D_MIX), 0.1),
        'rwkv_ka': 1.0 + nrm((L, D_MIX), 0.1),
        'rwkv_rk': nrm((L, H_A, HEAD_A), 0.1),
        'rwkv_lnx_w': 1.0 + nrm((L, D_MIX), 0.1),
        'rwkv_lnx_b': nrm((L, D_MIX), 0.02),
        'rwkv_out': nrm((L, D_MIX, D_MODEL), D_MIX ** -0.5),
        'sg_ln_w': 1.0 + nrm((L, D_MIX), 0.1),
        'sg_ln_b': nrm((L, D_MIX), 0.02),
        'sg_ws': nrm((L, G_B, CHUNK, CHUNK), CHUNK ** -0.5),
        'sg_bs': 1.0 + nrm((L, G_B, CHUNK), 0.1),
        'sg_out': nrm((L, D_MIX, D_MODEL), D_MIX ** -0.5),
        'conv_w': nrm((L, CONV_K, D_MIX), CONV_K ** -0.5),
        'conv_out': nrm((L, D_MIX, D_MODEL), D_MIX ** -0.5),
        's5_a_re': -0.5 + nrm((L, G_D, N_STATE), 0.01),
        's5_a_im': jnp.pi * jnp.arange(N_STATE, dtype=f32)[None, None, :] + nrm((L, G_D, N_STATE), 0.01),
        's5_b_re': nrm((L, G_D, N_STATE, GROUP_D), (2 * GROUP_D) ** -0.5),
        's5_b_im': nrm((L, G_D, N_STATE, GROUP_D), (2 * GROUP_D) ** -0.5),
        's5_c_re': nrm((L, G_D, GROUP_D, N_STATE), (2 * N_STATE) ** -0.5),
        's5_c_im': nrm((L, G_D, GROUP_D, N_STATE), (2 * N_STATE) ** -0.5),
        's5_d': nrm((L, D_MIX), 1.0),
        's5_log_dt': uni((L, G_D), math.log(1e-3), math.log(1e-1)),
        's5_glu_w': nrm((L, D_MIX, 2 * D_MODEL), D_MIX ** -0.5),
        'w_o': nrm((L, D_MODEL, D_MODEL), D_MODEL ** -0.5),
        'norm_ffn_g': 1.0 + nrm((L, D_MODEL), 0.1),
        'ffn_w1': nrm((L, D_MODEL, D_FF), D_MODEL ** -0.5),
        'ffn_w2': nrm((L, D_FF, D_MODEL), D_FF ** -0.5),
        'final_g': 1.0 + nrm((D_MODEL,), 0.1),
    }

def first_block(x, c, ada_w, ada_b, norm_mix_g, w_in, rwkv_mu, rwkv_w0, rwkv_w2, rwkv_a0, rwkv_a2,
              rwkv_g2, rwkv_v0, rwkv_v1, rwkv_v2, rwkv_kk, rwkv_ka, rwkv_rk, rwkv_lnx_w, rwkv_lnx_b,
              rwkv_out, sg_ln_w, sg_ln_b, sg_ws, sg_bs, sg_out, conv_w, conv_out, s5_a_re, s5_a_im,
              s5_b_re, s5_b_im, s5_c_re, s5_c_im, s5_d, s5_log_dt, s5_glu_w, w_o, norm_ffn_g,
              ffn_w1, ffn_w2, final_g):
    in_dtype = x.dtype
    bsz, seq, _ = x.shape
    c_act = jax.nn.silu(c.astype(jnp.float32))
    v_first = None
    for l in range(DEPTH):
        mod = (c_act @ ada_w[l] + ada_b[l])[:, None, :]
        sh1, sc1, gt1, sh2, sc2, gt2 = jnp.split(mod, 6, axis=-1)

        h = rms_norm(x, norm_mix_g[l]) * (1.0 + sc1) + sh1
        p = h @ w_in[l]
        v_mix = None if l == 0 else (rwkv_v0[l - 1], rwkv_v1[l - 1], rwkv_v2[l - 1])
        y_a, v_first = rwkv7_mixer(p[..., :OFF_B], v_first, v_mix, rwkv_mu[l], rwkv_w0[l], rwkv_w2[l],
                                   rwkv_a0[l], rwkv_a2[l], rwkv_g2[l], rwkv_kk[l], rwkv_ka[l],
                                   rwkv_rk[l], rwkv_lnx_w[l], rwkv_lnx_b[l], rwkv_out[l])
        y_b = spatial_gating_mixer(p[..., OFF_B:OFF_C], sg_ln_w[l], sg_ln_b[l], sg_ws[l], sg_bs[l], sg_out[l])
        y_c = short_conv_mixer(p[..., OFF_C:OFF_D], conv_w[l], conv_out[l])
        y_d = s5_mixer(p[..., OFF_D:OFF_G], s5_a_re[l], s5_a_im[l], s5_b_re[l], s5_b_im[l],
                       s5_c_re[l], s5_c_im[l], s5_d[l], s5_log_dt[l], s5_glu_w[l])
        gates = jax.nn.sigmoid(p[..., OFF_G:]).reshape(bsz, seq, N_BRANCH, D_MODEL)
        merged = (gates[:, :, 0] * y_a + gates[:, :, 1] * y_b
                  + gates[:, :, 2] * y_c + gates[:, :, 3] * y_d)
        x = x + gt1 * (merged @ w_o[l])

        h = rms_norm(x, norm_ffn_g[l]) * (1.0 + sc2) + sh2
        x = x + gt2 * (jnp.square(jax.nn.relu(h @ ffn_w1[l])) @ ffn_w2[l])
    return rms_norm(x, final_g).astype(in_dtype)


DEPTH_2 = 2

HEAD_DIM = 64
N_HEADS_TOTAL = D_MODEL // HEAD_DIM
N_MEM_HEADS = 4
N_MIX_HEADS = N_HEADS_TOTAL - N_MEM_HEADS
D_MIX_2 = N_MIX_HEADS * HEAD_DIM
D_MEMQ = N_MEM_HEADS * HEAD_DIM
MEM_TOKENS = 256
D_FF_2 = 2816
CONV_WIDTH = 3
ROPE_THETA = 10000.0
Q_BLOCK = 128
DILATED_BRANCHES = ((128, 1), (512, 4), (2048, 16))
N_MIXERS = 2
N_A_LAYERS = (DEPTH_2 + 1) // 2
N_B_LAYERS = DEPTH_2 // 2
FOX_IN = 3 * D_MIX_2 + N_MIX_HEADS + D_MEMQ
DIL_IN = 3 * D_MIX_2 + D_MEMQ
NORM_EPS = 1e-6
NEG = -1e30


def rmsnorm(x, g):
    xf = x.astype(jnp.float32)
    y = xf * lax.rsqrt(jnp.mean(xf * xf, axis=-1, keepdims=True) + NORM_EPS)
    return (y * g.astype(jnp.float32)).astype(x.dtype)

def split_heads(t, n_heads):
    b, s, _ = t.shape
    return t.reshape(b, s, n_heads, HEAD_DIM).transpose(0, 2, 1, 3)

def merge_heads(t):
    b, h, s, d = t.shape
    return t.transpose(0, 2, 1, 3).reshape(b, s, h * d)

def rope_tables(seq):
    inv = 1.0 / (ROPE_THETA ** (jnp.arange(0, HEAD_DIM, 2, dtype=jnp.float32) / HEAD_DIM))
    ang = jnp.arange(seq, dtype=jnp.float32)[:, None] * inv[None, :]
    return jnp.cos(ang), jnp.sin(ang)

def apply_rope(x, cos, sin):
    x1, x2 = jnp.split(x.astype(jnp.float32), 2, axis=-1)
    y = jnp.concatenate([x1 * cos - x2 * sin, x2 * cos + x1 * sin], axis=-1)
    return y.astype(x.dtype)

def fox_attention(q, k, v, log_f):
    b, h, s, dh = q.shape
    c = lax.cumsum(log_f, axis=2)
    nb = s // Q_BLOCK
    scale = dh ** -0.5
    qb = q.reshape(b, h, nb, Q_BLOCK, dh).transpose(2, 0, 1, 3, 4)
    cb = c.reshape(b, h, nb, Q_BLOCK).transpose(2, 0, 1, 3)
    starts = jnp.arange(nb, dtype=jnp.int32) * Q_BLOCK
    kpos = jnp.arange(s, dtype=jnp.int32)

    def one_block(args):
        qi, ci, st = args
        sc = jnp.einsum('bhqd,bhkd->bhqk', qi, k, preferred_element_type=jnp.float32) * scale
        sc = sc + ci[..., :, None] - c[..., None, :]
        qpos = st + jnp.arange(Q_BLOCK, dtype=jnp.int32)
        sc = jnp.where(kpos[None, :] <= qpos[:, None], sc, NEG)
        p = jax.nn.softmax(sc, axis=-1)
        return jnp.einsum('bhqk,bhkd->bhqd', p.astype(v.dtype), v)

    out = lax.map(one_block, (qb, cb, starts))
    return out.transpose(1, 2, 0, 3, 4).reshape(b, h, s, dh)

def dilated_branch(q, k, v, window, dilation):
    b, h, s, dh = q.shape
    L = window // dilation
    chunk = dilation * L
    sp = -(-s // chunk) * chunk
    n = sp // dilation
    nb = n // L
    scale = dh ** -0.5

    def strided(t):
        t = jnp.pad(t, ((0, 0), (0, 0), (0, sp - s), (0, 0)))
        t = t.reshape(b, h, n, dilation, dh).transpose(0, 1, 3, 2, 4)
        return t.reshape(b, h, dilation, nb, L, dh)

    def with_prev(t):
        prev = jnp.pad(t, ((0, 0), (0, 0), (0, 0), (1, 0), (0, 0), (0, 0)))[:, :, :, :-1]
        return jnp.concatenate([prev, t], axis=4)

    qs = strided(q)
    kb = with_prev(strided(k))
    vb = with_prev(strided(v))
    sc = jnp.einsum('bhrnqd,bhrnkd->bhrnqk', qs, kb, preferred_element_type=jnp.float32) * scale
    a = jnp.arange(L, dtype=jnp.int32)
    cidx = jnp.arange(2 * L, dtype=jnp.int32)
    blk = jnp.arange(nb, dtype=jnp.int32)
    dist = a[:, None] + L - cidx[None, :]
    valid = (dist >= 0) & (dist <= L)
    valid = valid[None] & ((blk[:, None, None] > 0) | (cidx[None, None, :] >= L))
    sc = jnp.where(valid, sc, NEG)
    m = jnp.max(sc, axis=-1, keepdims=True)
    e = jnp.exp(sc - m)
    den = jnp.sum(e, axis=-1, keepdims=True)
    o = jnp.einsum('bhrnqk,bhrnkd->bhrnqd', (e / den).astype(v.dtype), vb)
    lse = (m + jnp.log(den))[..., 0]
    o = o.reshape(b, h, dilation, n, dh).transpose(0, 1, 3, 2, 4).reshape(b, h, sp, dh)[:, :, :s]
    lse = lse.reshape(b, h, dilation, n).transpose(0, 1, 3, 2).reshape(b, h, sp)[:, :, :s]
    return o, lse

def dilated_attention(q, k, v):
    outs, lses = [], []
    for window, dilation in DILATED_BRANCHES:
        o, lse = dilated_branch(q, k, v, window, dilation)
        outs.append(o)
        lses.append(lse)
    wts = jax.nn.softmax(jnp.stack(lses, axis=0), axis=0)
    return jnp.einsum('gbhs,gbhsd->bhsd', wts.astype(v.dtype), jnp.stack(outs, axis=0))

def memory_attention(qm, mem_n, w_mem_kv):
    km, vm = jnp.split(mem_n @ w_mem_kv, 2, axis=-1)
    km = split_heads(km, N_MEM_HEADS)
    vm = split_heads(vm, N_MEM_HEADS)
    sc = jnp.einsum('bhqd,bhkd->bhqk', qm, km, preferred_element_type=jnp.float32) * (HEAD_DIM ** -0.5)
    p = jax.nn.softmax(sc, axis=-1)
    return jnp.einsum('bhqk,bhkd->bhqd', p.astype(vm.dtype), vm)

def conv_ffn(xn, w_up, conv_w, conv_b, w_down):
    u = xn @ w_up
    s = u.shape[1]
    up = jnp.pad(u, ((0, 0), (CONV_WIDTH - 1, 0), (0, 0)))
    c = conv_b
    for j in range(CONV_WIDTH):
        c = c + conv_w[j] * up[:, j:j + s]
    val, gate = jnp.split(c, 2, axis=-1)
    return (jax.nn.silu(gate) * val) @ w_down

def second_inputs(seed: int = 0) -> dict:
    key = jax.random.key(seed)
    ks = jax.random.split(key, 16)
    f32 = jnp.float32
    nrm = lambda k, shape, scale: jax.random.normal(k, shape, f32) * scale
    forget_bias_init = 3.0
    return {
        'x': nrm(ks[0], (BATCH, SEQ, D_MODEL), 1.0),
        'mem': nrm(ks[1], (BATCH, MEM_TOKENS, D_MODEL), 1.0),
        'norm_mix': 1.0 + nrm(ks[2], (DEPTH_2, D_MODEL), 0.1),
        'norm_mem': 1.0 + nrm(ks[3], (DEPTH_2, D_MODEL), 0.1),
        'norm_ffn': 1.0 + nrm(ks[4], (DEPTH_2, D_MODEL), 0.1),
        'w_in_fox': nrm(ks[5], (N_A_LAYERS, D_MODEL, FOX_IN), D_MODEL ** -0.5),
        'b_forget': forget_bias_init + nrm(ks[6], (N_A_LAYERS, N_MIX_HEADS), 0.5),
        'w_in_dil': nrm(ks[7], (N_B_LAYERS, D_MODEL, DIL_IN), D_MODEL ** -0.5),
        'w_mem_kv': nrm(ks[8], (DEPTH_2, D_MODEL, 2 * D_MEMQ), D_MODEL ** -0.5),
        'w_out': nrm(ks[9], (DEPTH_2, D_MODEL, D_MODEL), D_MODEL ** -0.5),
        'w_up': nrm(ks[10], (DEPTH_2, D_MODEL, 2 * D_FF_2), D_MODEL ** -0.5),
        'conv_w': nrm(ks[11], (DEPTH_2, CONV_WIDTH, 2 * D_FF_2), CONV_WIDTH ** -0.5),
        'conv_b': nrm(ks[12], (DEPTH_2, 2 * D_FF_2), 0.02),
        'w_down': nrm(ks[13], (DEPTH_2, D_FF_2, D_MODEL), D_FF_2 ** -0.5),
        'norm_final': 1.0 + nrm(ks[14], (D_MODEL,), 0.1),
    }

def second_block(x, mem, norm_mix, norm_mem, norm_ffn, w_in_fox, b_forget, w_in_dil,
              w_mem_kv, w_out, w_up, conv_w, conv_b, w_down, norm_final):
    s = x.shape[1]
    cos, sin = rope_tables(s)
    h = x
    for layer in range(DEPTH_2):
        kind = layer % N_MIXERS
        slot = layer // N_MIXERS
        xn = rmsnorm(h, norm_mix[layer])
        mn = rmsnorm(mem, norm_mem[layer])
        if kind == 0:
            proj = xn @ w_in_fox[slot]
            q, k, v, f_logit, qm = jnp.split(
                proj, [D_MIX_2, 2 * D_MIX_2, 3 * D_MIX_2, 3 * D_MIX_2 + N_MIX_HEADS], axis=-1)
            log_f = jax.nn.log_sigmoid(
                (f_logit + b_forget[slot]).astype(jnp.float32)).transpose(0, 2, 1)
            mix = fox_attention(split_heads(q, N_MIX_HEADS), split_heads(k, N_MIX_HEADS),
                                split_heads(v, N_MIX_HEADS), log_f)
        else:
            proj = xn @ w_in_dil[slot]
            q, k, v, qm = jnp.split(proj, [D_MIX_2, 2 * D_MIX_2, 3 * D_MIX_2], axis=-1)
            qh = apply_rope(split_heads(q, N_MIX_HEADS), cos, sin)
            kh = apply_rope(split_heads(k, N_MIX_HEADS), cos, sin)
            mix = dilated_attention(qh, kh, split_heads(v, N_MIX_HEADS))
        mem_out = memory_attention(split_heads(qm, N_MEM_HEADS), mn, w_mem_kv[layer])
        heads = jnp.concatenate([mix, mem_out], axis=1)
        h = h + merge_heads(heads) @ w_out[layer]
        h = h + conv_ffn(rmsnorm(h, norm_ffn[layer]), w_up[layer], conv_w[layer],
                         conv_b[layer], w_down[layer])
    return rmsnorm(h, norm_final)


def setup_inputs(seed=0):
    out = dict(first_inputs(seed))
    for name, value in second_inputs(seed + 1).items():
        if name != "x":
            out[name + "_2"] = value
    return out


def reference(
    x, c, ada_w, ada_b, norm_mix_g, w_in, rwkv_mu, rwkv_w0, rwkv_w2, rwkv_a0, rwkv_a2, rwkv_g2,
    rwkv_v0, rwkv_v1, rwkv_v2, rwkv_kk, rwkv_ka, rwkv_rk, rwkv_lnx_w, rwkv_lnx_b, rwkv_out,
    sg_ln_w, sg_ln_b, sg_ws, sg_bs, sg_out, conv_w, conv_out, s5_a_re, s5_a_im, s5_b_re,
    s5_b_im, s5_c_re, s5_c_im, s5_d, s5_log_dt, s5_glu_w, w_o, norm_ffn_g, ffn_w1, ffn_w2,
    final_g, mem_2, norm_mix_2, norm_mem_2, norm_ffn_2, w_in_fox_2, b_forget_2, w_in_dil_2,
    w_mem_kv_2, w_out_2, w_up_2, conv_w_2, conv_b_2, w_down_2, norm_final_2,
):
    x = first_block(
        x, c, ada_w, ada_b, norm_mix_g, w_in, rwkv_mu, rwkv_w0, rwkv_w2, rwkv_a0, rwkv_a2,
        rwkv_g2, rwkv_v0, rwkv_v1, rwkv_v2, rwkv_kk, rwkv_ka, rwkv_rk, rwkv_lnx_w, rwkv_lnx_b,
        rwkv_out, sg_ln_w, sg_ln_b, sg_ws, sg_bs, sg_out, conv_w, conv_out, s5_a_re, s5_a_im,
        s5_b_re, s5_b_im, s5_c_re, s5_c_im, s5_d, s5_log_dt, s5_glu_w, w_o, norm_ffn_g, ffn_w1,
        ffn_w2, final_g,
    )
    return second_block(
        x, mem_2, norm_mix_2, norm_mem_2, norm_ffn_2, w_in_fox_2, b_forget_2, w_in_dil_2,
        w_mem_kv_2, w_out_2, w_up_2, conv_w_2, conv_b_2, w_down_2, norm_final_2,
    )


_drawn_inputs = setup_inputs


def setup_inputs(seed=0):
    import zlib

    import numpy as np

    out = dict(_drawn_inputs(seed))
    spreads = {}
    factors = {'rwkv_w2': 8.0,
     'rwkv_a0': 8.0,
     'rwkv_kk': 2.952,
     'rwkv_ka': 2.771,
     'rwkv_lnx_w': 5.404,
     'rwkv_lnx_b': 8.0,
     'sg_ln_w': 5.601,
     'sg_ln_b': 8.0,
     'sg_bs': 3.898,
     's5_a_re': 64.0,
     's5_a_im': 64.0,
     's5_b_re': 64.0,
     's5_b_im': 64.0,
     's5_c_re': 64.0,
     's5_c_im': 64.0,
     's5_log_dt': 64.0,
     'norm_mem_2': 4.68,
     'conv_b_2': 2.759}
    for name, (base, spread) in spreads.items():
        noise = np.random.default_rng([zlib.crc32(name.encode()), seed]).standard_normal(out[name].shape)
        drawn = base * np.exp(spread * noise) if base else spread * noise
        out[name] = __import__('jax').numpy.asarray(drawn.astype(out[name].dtype))
    for name, factor in factors.items():
        out[name] = (out[name] * factor).astype(out[name].dtype)
    return out
```

```python
from contextlib import ExitStack

import numpy as np

import concourse.bass as bass
from concourse import mybir
from concourse.alu_op_type import AluOpType as ALU

F32 = mybir.dt.float32
F32R = mybir.dt.float32r
ACT = mybir.ActivationFunctionType
AX = mybir.AxisListType

P = 128
T = 512
D = 1024
KT = D // P
DM = 256
H_A, HD = 4, 64
C = 32
NCK = T // C
NB = 4
FF_GROUPS = 4096 // D
FF2 = 2816 // P
FF2_GROUPS = [8, 8, 6]
NH, NMH = 12, 4
MT = 256
QB = T // P
S5T = 8

RAW, SPLIT, BANKS, ADA = 2, 2, 4, 4

N_MIX = 6 + 4 + 2 + 7
N_FOX, N_DIL = 21, 20
N_KV = 4

EPS, LN_EPS, LNX_EPS = 1e-6, 1e-5, 64e-5
NEG = -1e30
PI = float(np.pi)
PI_IN = 3.1415925
TWO_PI = [6.28125, 0.0019350051879882812, 3.019916e-07]
ROUND = 1.5 * 2.0 ** 23


def branch_pieces():
    return [("conv", 1), ("sg", 1), ("s5", 2), ("rwkv", 1)]


def vec_columns():
    sizes = [("c", 8), ("ada_b", 48), ("g_mix", 8), ("mu", 7), ("w0", 2), ("a0", 2), ("kk", 2), ("ka", 2), ("rk", 2),
             ("sg_w", 2), ("sg_b", 2), ("conv_w", 6), ("s5_d", 2), ("a_re", 8), ("a_im", 8), ("log_dt", 8),
             ("g_ffn", 8), ("g_final1", 8), ("g_mix2", 16), ("g_mem2", 16), ("g_ffn2", 16), ("b_f", 1),
             ("cw2", 2 * 3 * 44), ("cb2", 2 * 44), ("g_final", 8), ("lnx_w", 64), ("lnx_b", 64)]
    at, cols = 0, {}
    for name, n in sizes:
        cols[name] = (at, n)
        at += n
    return cols, at


VEC, NVEC = vec_columns()


def const_columns():
    sizes = [("ident", 128), ("ones", 128), ("hsum", 128), ("lt", 64), ("gt", 64), ("ge", 64),
             ("stack", 64), ("sum32", 32), ("hm", 2), ("rot", 128)]
    at, cols = 0, {}
    for name, n in sizes:
        cols[name] = (at, n)
        at += n
    return cols, at


CON, NCON = const_columns()


X_DONE = [8 + 8 * FF_GROUPS + 8, 8 + 8 * FF_GROUPS + 8 + 8 + 24]

UNITS = [(h, b, (b + 1) * P, b * (b + 1) // 2 * P) for h in range(NH) for b in range(QB)] + \
        [(NH + h, b, MT, 0) for h in range(NMH) for b in range(QB)]


class Counts:

    def __init__(self):
        self.value = {}

    def next(self, name, by=1):
        self.value[name] = self.value.get(name, 0) + by
        return self.value[name]

    def turn(self, i, per):
        self.start = dict(self.value)
        for name, n in per.items():
            self.value[name] = self.value.get(name, 0) + i * n

    def leave(self, turns, per):
        for name, n in per.items():
            self.value[name] = self.start.get(name, 0) + turns * n


def build(nc, A, out):
    n_mix = N_MIX
    n_block1 = n_mix + 8 * NB + 10 + 8 + 2 * 8 * FF_GROUPS
    pieces = n_block1 + sum(n + N_KV + 8 + 2 * FF2 + 8 * len(FF2_GROUPS) for n in (N_FOX, N_DIL))
    with ExitStack() as ctx:
        def sb(name, shape, dt=F32):
            return ctx.enter_context(nc.sbuf_tensor(name, shape, dt))

        sems = {}

        def S(name):
            if name not in sems:
                sems[name] = ctx.enter_context(nc.semaphore(name))
            return sems[name]

        raw = sb("raw", [P, RAW, D])
        w_hi = sb("w_hi", [P, SPLIT, D], F32R)
        w_lo = sb("w_lo", [P, SPLIT, D], F32R)
        zero = sb("zero", [P, 1])
        x = sb("x", [P, KT, T])
        h_hi = sb("h_hi", [P, KT, T], F32R)
        h_lo = sb("h_lo", [P, KT, T], F32R)
        g_hi = sb("g_hi", [P, KT, T], F32R)
        g_lo = sb("g_lo", [P, KT, T], F32R)
        work = sb("work", [P, 6, T])
        vec = sb("vec", [P, NVEC])
        con = sb("con", [P, NCON])
        mod = sb("mod", [P, 48])
        small = sb("small", [P, 40, 8])
        ARENA = 21504
        arena = sb("arena", [P, ARENA])
        ps = [ctx.enter_context(nc.psum_tensor(f"ps{i}", [P, T], F32)) for i in range(8)]
        PA, PB, PC, PD = ps[4:]

        a_dram = nc.dram_tensor("pair_scores", (H_A, C, NCK, C), F32, kind="Internal").ap()
        t_dram = nc.dram_tensor("pair_inverse", (2, H_A, NCK, C // 2, C), F32, kind="Internal").ap()

        def V(name, i=0, n=None):
            at, size = VEC[name]
            return vec[:, at + i:at + i + (n or 1)]

        def K(name):
            at, size = CON[name]
            return con[:, at:at + size]

        def place(sizes, at=0):
            parts = {}
            for name, shape in sizes:
                n = int(np.prod(shape))
                assert at + n <= ARENA, (name, at + n)
                flat = arena[:, at:at + n]
                if len(shape) == 2:
                    flat = flat.rearrange("p (a b) -> p a b", a=shape[0])
                elif len(shape) == 3:
                    flat = flat.rearrange("p (a b c) -> p a b c", a=shape[0], b=shape[1])
                elif len(shape) == 4:
                    flat = flat.rearrange("p (a b c d) -> p a b c d", a=shape[0], b=shape[1], c=shape[2])
                parts[name] = flat
                at += n
            parts["end"] = at
            return parts

        merge_m = place([("sig", (8, T)), ("merged", (8, T)), ("tmp", (2, T))])
        ada_m = place([("ada", (ADA, D))], at=ARENA - ADA * D)
        conv_m = place([("bg", (2, T)), ("cg", (2, T)), ("z", (2, T)), ("y", (2, T))])
        sg_m = place([("z", (4, T)), ("mu", (T,)), ("d", (2, T)), ("sq", (2, T)), ("std", (T,)), ("rstd", (T,)),
                      ("vn", (2, T)), ("vt", (2, 4, P)), ("ws", (4, P)), ("wsm", (4, P)), ("bs", (2, P)),
                      ("mix", (2, T)), ("caus", (P,))], at=4096)
        s5_m = place([("u", (2, T)), ("ct", (8, T)), ("st", (8, T)), ("b_in", (2, 8, 16)), ("bb", (2, 8, 16)),
                      ("m8", (8, 8)), ("c_in", (2, 2, P)), ("bpad", (2, 8, P)), ("bt", (2, 8, P)), ("cc", (2, 8, P)),
                      ("w", (6, T)), ("y", (T,))])
        s5_w2 = arena[:, s5_m["end"] - 7 * T - 2048 * 2 - 2048:]
        rw_pad = place([("a", (2, NCK, 2, C)), ("b", (2, NCK, 2, C)), ("k", (2, NCK, 2, C)), ("r", (2, NCK, 2, C)),
                        ("g", (2, T)), ("bonus", (2, T))])
        rw_pad["all"] = arena[:, 0:4 * 2 * NCK * 2 * C]
        base_at = rw_pad["end"]
        rw_in = place([("r", (2, T)), ("k", (2, T)), ("v", (2, T)), ("m", (T,)), ("lw", (2, T)), ("a", (2, T)),
                       ("kk", (2, T)), ("cum", (2, T)), ("e", (2, T))], at=base_at)
        rw_bd = place([("ab", (NCK, 64)), ("akT", (NCK, 64)), ("vt", (NCK, 64)), ("rbT", (NCK, 64)),
                       ("rkT", (NCK, 64)), ("tT", (NCK, 64)), ("kt", (NCK, P))], at=base_at)
        rw_sol = place([("as", (C, C)), ("z", (C // 2, C)), ("o", (NCK, 64))],
                       at=max(rw_in["end"], rw_bd["end"]))
        at_m = place([("q", (NH + NMH, T)), ("k", (NH, T)), ("km", (NMH, MT)), ("v", (QB, NH * HD)), 
                      ("p", (2, T)), ("pt", (QB, T))])
        rw_sol["prod"] = work[:, 4, :]
        at_m["vm"] = work[:, 5, :].rearrange("p (a b) -> p a b", a=2)
        mem_in = at_m["pt"].rearrange("p a b -> p (a b)").rearrange("p (k t) -> p k t", k=KT)
        rope_t = arena[:, at_m["end"] - 4 * T - 2 * T:at_m["end"] - 4 * T].rearrange("p (a b) -> p a b", a=2)
        cv_m = place([("cv", (2, T)), ("cg", (2, T)), ("sg", (2, T)), ("t", (2, T))])
        ff_m = place([("r", (2, T)), ("s", (2, T))])
        rw_bt = rw_pad["k"].rearrange("p a n h c -> p (a n h c)").rearrange("p (n c) -> p n c", n=NCK)
        state = work[:, 2, 0:4 * HD].rearrange("p (a b c) -> p a b c", a=2, b=2)
        chain_y = work[:, 3, 0:2 * HD].rearrange("p (a b) -> p a b", a=2)


        block = ctx.enter_context(nc.Block())
        lora = work[:, 5, 0:DM]
        masks = work[:, 0:3, :].rearrange("p a b -> p (a b)")[:, 0:(QB * (QB + 1) // 2) * P]

        def mn(pair, k):
            return pair[:, k // 2, MT * (k % 2):MT * (k % 2) + MT]


        @block.sync
        def _(sp):
            sp.dma_start(vec[:], A["vec"]).then_inc(S("vec_in"), 16)
            sp.dma_start(con[:], A["con"]).then_inc(S("con_in"), 16)
            ada = ada_m["ada"]
            for q in range(ADA):
                sp.dma_start(ada[:, q, :], A["ada"][q]).then_inc(S(f"ada_in{q}"), 16)
            sp.dma_start(x[:], A["xT"]).then_inc(S("x_in"), 16)
            for q in range(RAW):
                if q < pieces:
                    sp.dma_start(raw[:, q, :], A["w"][q]).then_inc(S(f"raw_in{q}"), 16)
            for q in range(ADA, 16):
                sp.wait_ge(S("ada_used"), q - ADA + 1)
                sp.dma_start(ada[:, q % ADA, :], A["ada"][q]).then_inc(S(f"ada_in{q % ADA}"), 16)
            def stream_to(a, b):
                def one(q, n, slot):
                    sp.wait_ge(S("w_split"), q - RAW + 1)
                    sp.dma_start(raw[:, slot, :], n).then_inc(S(f"raw_in{slot}"), 16)
                while a < b and (a % RAW or b - a < RAW):
                    one(a, A["w"][a], a % RAW)
                    a += 1
                turns = (b - a) // RAW
                if turns == 1:
                    for k in range(RAW):
                        one(a + k, A["w"][a + k], k)
                elif turns > 1:
                    w = A["w"][0:pieces // RAW * RAW].rearrange("(g s) p n -> g s p n", s=RAW)
                    with sp.Fori(a // RAW, a // RAW + turns) as g:
                        for k in range(RAW):
                            one(g * RAW + k, w[bass.ds(g, 1), k].rearrange("a p n -> (a p) n"), k)
                a += turns * RAW
                while a < b:
                    one(a, A["w"][a], a % RAW)
                    a += 1

            stream_to(RAW, 6 + 4)
            sp.wait_ge(S("ada_used"), 16)
            sp.dma_start(sg_m["ws"], A["sg_ws"]).then_inc(S("sg_in"), 16)
            sp.dma_start(sg_m["bs"], A["sg_bs"]).then_inc(S("sg_in"), 16)
            sp.dma_start(sg_m["caus"], A["caus"]).then_inc(S("sg_in"), 16)
            stream_to(10, 12)
            sp.wait_ge(S("sg_y"), 2)
            for name, key in (("b_in", "s5_b"), ("m8", "s5_m8"), ("c_in", "s5_c")):
                sp.dma_start(s5_m[name], A[key]).then_inc(S("s5_in"), 16)
            stream_to(12, n_mix + RAW)
            sp.wait_ge(S("s5_y"), 2)
            sp.dma_start(lora, A["lora"]).then_inc(S("lora_in"), 16)
            sp.wait_ge(S("ab_scores"), 2)
            ab = rw_bd["ab"]
            for h in range(H_A):
                sp.dma_start(a_dram[h], ab[C * h:C * h + C, :, C * (h % 2):C * (h % 2) + C]).then_inc(S("a_out"), 16)
            sp.wait_ge(S("a_out"), 16 * H_A)
            for half in range(2):
                for h in range(H_A):
                    at = 64 * half + NCK * h
                    sp.dma_start(rw_sol["as"][at:at + NCK], a_dram[h].rearrange("t n s -> n t s")).then_inc(S("a_in"), 16)
            sp.dma_start(rw_sol["z"], A["eye"].rearrange("p (c t) -> p c t", t=C)).then_inc(S("a_in"), 16)
            sp.wait_ge(S("solved"), C - 1)
            sp.dma_start(t_dram.rearrange("a h n c t -> (a h n) (c t)"),
                         rw_sol["z"].rearrange("p c t -> p (c t)")).then_inc(S("t_out"), 16)
            sp.wait_ge(S("t_out"), 16)
            sp.wait_ge(S("tT_clear"), 1)
            for half in range(2):
                for h in range(H_A):
                    at = C * h + C // 2 * half
                    sp.dma_start(rw_bd["tT"][at:at + C // 2, :, C * (h % 2):C * (h % 2) + C],
                                 t_dram[half, h].rearrange("n c t -> c n t")).then_inc(S("tT_in"), 16)
            stream_to(n_mix + RAW, n_mix + 8 * NB + 10)
            sp.wait_ge(S("merge_done"), 1)
            for q in range(16, 48):
                if q >= 16 + ADA:
                    sp.wait_ge(S("ada_used"), q - ADA + 1)
                sp.dma_start(ada_m["ada"][:, q % ADA, :], A["ada"][q]).then_inc(S(f"ada_in{q % ADA}"), 16)
            stream_to(n_mix + 8 * NB + 10, n_block1)
            first = n_block1
            for layer, n_in in ((0, N_FOX), (1, N_DIL)):
                sp.wait_ge(S("x_done"), X_DONE[layer])
                sp.dma_start(mem_in, A["memT"]).then_inc(S("mem_in"), 16)
                stream_to(first, first + 2)
                if layer:
                    sp.wait_ge(S("h_ready"), 8 * 5)
                    sp.dma_start(work[:, 2:4, :], A["rope"]).then_inc(S("rope_in"), 16)
                    stream_to(first + 2, first + 14)
                    sp.wait_ge(S("rope_done"), 12)
                    sp.dma_start(masks, A["mask_dil"]).then_inc(S("mask_in"), 16)
                    stream_to(first + 14, first + n_in + N_KV)
                else:
                    stream_to(first + 2, first + n_in + N_KV)
                    sp.wait_ge(S("forget_sum"), 1)
                    sp.dma_start(at_m["k"][HD:HD + 1, :, :], work[0:NH, 4, :]).then_inc(S("forget_in"), 16)
                    sp.wait_ge(S("forget_in"), 16)
                    sp.dma_start(masks, A["mask_fox"]).then_inc(S("mask_in"), 16)
                last = first + n_in + N_KV + 8 + 2 * FF2 + 24
                stream_to(first + n_in + N_KV, last)
                first = last
            sp.wait_ge(S("result"), KT)
            sp.dma_start(out, arena[:, 0:KT * T].rearrange("p (k t) -> p k t", k=KT)).then_inc(S("stored"), 16)
            sp.wait_ge(S("stored"), 16)

        @block.gpsimd
        def _(pool):
            pool.memset(zero[:], 0.0).then_inc(S("zero_set"), 1)
            pool.wait_ge(S("zero_set"), 1)

            def split(q, slot, landed, free):
                pool.wait_ge(S(f"raw_in{slot}"), landed)
                if free is not None:
                    pool.wait_ge(S("w_used"), free)
                pool.tensor_tensor(w_hi[:, slot % SPLIT, :], raw[:, slot, :], zero[:].broadcast_to((P, D)), ALU.add).then_inc(S("w_high"), 1)
                pool.wait_ge(S("w_high"), q + 1)
                pool.tensor_tensor(w_lo[:, slot % SPLIT, :], raw[:, slot, :], w_hi[:, slot % SPLIT, :].bitcast(F32),
                                   ALU.subtract).then_inc(S("w_split"), 1)

            for q in range(min(RAW, pieces)):
                split(q, q, 16, None if q < SPLIT else q - SPLIT + 1)
            turns = pieces // RAW
            if turns > 1:
                with pool.Fori(1, turns) as g:
                    for k in range(RAW):
                        split(g * RAW + k, k, g * 16 + 16, g * RAW + (k - SPLIT + 1))
            for q in range(max(turns, 1) * RAW, pieces):
                split(q, q % RAW, 16 * (q // RAW + 1), q - SPLIT + 1)

        @block.vector
        def _(dve):
            n = Counts()

            def do(ins, name="dve_step"):
                ins.then_inc(S(name), 1)
                dve.wait_ge(S(name), n.next(name))

            def need(name, by=1):
                dve.wait_ge(S(name), n.next(name, by))

            def both_parts(hi, lo, src, name):
                do(dve.tensor_copy(hi, src))
                do(dve.tensor_tensor(lo, src, hi.bitcast(F32), ALU.subtract), name)

            def sum_squares(tiles, sq, acc):
                for k in range(tiles):
                    need("square")
                    if k == 0:
                        do(dve.tensor_copy(acc, sq(k)), "square_used")
                    else:
                        do(dve.tensor_tensor(acc, acc, sq(k), ALU.add), "square_used")
                n.value["squares_summed"] = n.value.get("squares_summed", 0)
                do(dve.tensor_scalar(acc, acc, 1.0, None, ALU.mult), "squares_summed")

            def norm(gain, shift=None):
                sum_squares(KT, lambda k: work[:, k % 2, :], work[:, 2, :])
                need("rms_ready")
                do(dve.reciprocal(work[:, 3, :], work[:, 3, :]))
                for k in range(KT):
                    t = work[:, 4 + k % 2, :]
                    do(dve.scalar_tensor_tensor(t, x[:, k, :], gain(k), work[:, 3, :], ALU.mult, ALU.mult))
                    if shift is not None:
                        do(dve.tensor_scalar(t, t, shift(k), None, ALU.add))
                    both_parts(h_hi[:, k, :], h_lo[:, k, :], t, "h_ready")

            def add_to_x(k, gate=None):
                need("tile")
                bank = ps[n.value["bank"] % BANKS]
                if gate is None:
                    do(dve.tensor_tensor(x[:, k, :], bank[:], x[:, k, :], ALU.add), "dve_freed")
                else:
                    do(dve.scalar_tensor_tensor(x[:, k, :], bank[:], gate, x[:, k, :], ALU.mult, ALU.add), "dve_freed")
                n.value["bank"] += 1

            n.value["bank"] = 0

            def tile():
                need("tile")
                n.value["bank"] += 1
                return ps[(n.value["bank"] - 1) % BANKS]

            def skip(tiles):
                n.next("tile", tiles)
                n.value["bank"] += tiles


            def vector_recurrence():
                v, bd, sol = rw_in, rw_bd, rw_sol
                keep = small[:, 24, 0:7]
                do(dve.tensor_scalar(keep, V("mu", 0, 7), -1.0, 1.0, ALU.mult, ALU.add))
                for i, dst in enumerate([v["r"][:, 0], v["r"][:, 1], v["k"][:, 0], v["k"][:, 1], v["v"][:, 0], v["v"][:, 1], v["m"]]):
                    bank = tile()
                    do(dve.tensor_scalar(dst, bank[:], keep[:, i:i + 1], None, ALU.mult))
                    do(dve.scalar_tensor_tensor(dst[:, 1:], bank[:, :T - 1], V("mu", i), dst[:, 1:], ALU.mult, ALU.add), "dve_freed")
                do(dve.memset(rw_pad["all"], 0.0), "rw_shifted")
                e, cum, lw, kk = v["e"], v["cum"], v["lw"], v["kk"]
                reset = e[:, 1, :]
                do(dve.memset(reset, 1.0))
                do(dve.memset(reset.rearrange("p (n t) -> p n t", t=C)[:, :, 0:1], 0.0))
                for k in range(2):
                    need("rw_decay")
                    do(dve.tensor_scalar(lw[:, k], lw[:, k], -float(np.exp(-0.5)), None, ALU.mult))
                    do(dve.tensor_tensor_scan(cum[:, k], reset, lw[:, k], 0.0, ALU.mult, ALU.add), "rw_cum")
                for k in range(2):
                    do(dve.tensor_scalar(kk[:, k], v["k"][:, k], V("kk", k), None, ALU.mult))
                    do(dve.tensor_tensor(e[:, k], kk[:, k], kk[:, k], ALU.mult), "rw_kk_square")
                for k in range(2):
                    need("rw_kk_sum")
                    do(dve.tensor_scalar(e[:, k], PA[:] if k == 0 else PB[:], 1e-24, None, ALU.max), "rw_kk_floor")
                for k in range(2):
                    need("rw_kk_norm")
                    do(dve.reciprocal(e[:, k], e[:, k]))
                    do(dve.tensor_tensor(kk[:, k], kk[:, k], e[:, k], ALU.mult))
                drop = small[:, 24, 0:2]
                do(dve.tensor_scalar(drop, V("ka", 0, 2), -1.0, 1.0, ALU.mult, ALU.add))
                for k in range(2):
                    need("rw_a")
                    do(dve.tensor_scalar(e[:, k], v["a"][:, k], V("ka", k), drop[:, k:k + 1], ALU.mult, ALU.add))
                    do(dve.tensor_tensor(v["k"][:, k], v["k"][:, k], e[:, k], ALU.mult))
                    do(dve.scalar_tensor_tensor(e[:, k], v["r"][:, k], V("rk", k), v["k"][:, k], ALU.mult, ALU.mult), "rw_rk")
                    do(dve.tensor_tensor(v["a"][:, k], v["a"][:, k], kk[:, k], ALU.mult))
                for k in range(2):
                    need("rw_rk_sum")
                    do(dve.tensor_tensor(rw_pad["bonus"][:, k], (PC if k == 0 else PD)[:], v["v"][:, k], ALU.mult))
                do(dve.memset(small[:, 39, :], 0.0), "rw_exp_go")
                half = lambda ap, g: ap[64 * g:64 * g + 64].rearrange("p (n t) -> p n t", t=C)
                pad = lambda name, k, g: rw_pad[name][64 * g:64 * g + 64, k, :, g, :]
                pc = small[:, 25:29, :].rearrange("p a b -> p (a b)").rearrange("p (k n) -> p k n", k=2)
                for k in range(2):
                    need("rw_exp")
                    for g in range(2):
                        do(dve.tensor_tensor(pad("r", k, g), half(v["r"][:, k], g), half(e[:, 0], g), ALU.mult))
                    do(dve.tensor_copy(pc[:, k, :], e[:, 0].rearrange("p (n t) -> p n t", t=C)[:, :, C - 1]))
                    do(dve.tensor_tensor(lw[:, k], cum[:, k], lw[:, k], ALU.subtract), "rw_before")
                    need("rw_exp")
                    for g in range(2):
                        do(dve.scalar_tensor_tensor(pad("a", k, g), half(kk[:, k], g), -1.0, half(e[:, 1], g), ALU.mult, ALU.mult))
                    need("rw_exp")
                    for g in range(2):
                        do(dve.tensor_tensor(pad("b", k, g), half(v["a"][:, k], g), half(e[:, 0], g), ALU.mult))
                        do(dve.tensor_tensor(pad("k", k, g), half(v["k"][:, k], g), half(e[:, 0], g), ALU.mult), "rw_padded")

                def bd_copy(dst, mask=None, per=8, name=None):
                    for q in range(NCK // per):
                        need("bd")
                        i = n.value["bd"] - 1
                        src = ps[4 + i % 4][:, 0:per * (T // per)].rearrange("p (n c) -> p n c", n=per)
                        d = dst[:, per * q:per * q + per, :]
                        if mask is None:
                            ins = dve.tensor_copy(d, src)
                        else:
                            ins = dve.tensor_tensor(d, src, mask.unsqueeze(1).broadcast_to((P, per, 64)), ALU.mult)
                        do(ins, "bd_used")

                bd_copy(bd["ab"], K("lt"))
                do(dve.memset(small[:, 39, :], 0.0), "ab_scores")
                do(dve.memset(small[:, 39, :], 0.0), "ab_scores")
                bd_copy(bd["akT"], K("gt"))
                bd_copy(bd["rkT"], K("ge"))
                bd_copy(bd["rbT"], K("ge"))
                do(dve.memset(bd["tT"], 0.0), "tT_clear")
                bd_copy(bd["kt"], per=4)
                do(dve.memset(rw_pad["k"].rearrange("p a n h c -> p (a n h c)"), 0.0))
                for k in range(2):
                    for g in range(2):
                        do(dve.tensor_copy(pad("k", k, g), half(v["v"][:, k], g)), "v_padded")
                bd_copy(bd["vt"])
                bd_copy(rw_bt, per=4)
                dve.wait_ge(S("a_in"), 16 * 9)
                a_m, z, prod = sol["as"], sol["z"], sol["prod"]
                do(dve.memset(a_m.rearrange("p t s -> p (t s)")[:, 0:C * C:C + 1], 1.0))
                for i in range(1, C):
                    pr = prod[:, 0:C // 2 * (i + 1)].rearrange("p (c j) -> p c j", j=i + 1)
                    do(dve.tensor_tensor(pr, z[:, :, 0:i + 1], a_m[:, i, 0:i + 1].unsqueeze(1).broadcast_to((P, C // 2, i + 1)), ALU.mult))
                    do(dve.tensor_reduce(z[:, :, i], pr, AX.X, ALU.add), "solved")
                do(dve.memset(state, 0.0), "state_set")
                for c in range(NCK):
                    for p in range(2):
                        do(dve.tensor_scalar(state[:, 1, p, :], state[:, 0, p, :], pc[:, p, c:c + 1], None, ALU.mult))
                    need("rec_y")
                    for p in range(2):
                        rows = slice(64 * p, 64 * p + 64)
                        do(dve.tensor_copy(chain_y[rows, 0, :], ps[4 + p][rows, 0:HD]), "rec_y_copied")
                    need("rec_sa")
                    for p in range(2):
                        rows = slice(64 * p, 64 * p + 64)
                        do(dve.tensor_copy(chain_y[rows, 1, :], ps[6 + p][rows, 0:HD]), "rec_sa_copied")
                    need("rec_o")
                    for p in range(2):
                        do(dve.scalar_tensor_tensor(state[:, 0, p, :], ps[4 + p][:, P:P + HD], pc[:, p, c:c + 1], state[:, 1, p, :],
                                                    ALU.mult, ALU.add), "state_set")
                need("rec_o_copied", 2 * NCK)
                o, sq = sol["o"], bd["ab"]
                mean, var = small[:, 29:31, :].rearrange("p a b -> p (a b)"), small[:, 31:33, :].rearrange("p a b -> p (a b)")
                spread = lambda s: s.unsqueeze(2).broadcast_to((P, NCK, HD))
                do(dve.tensor_reduce(mean, o, AX.X, ALU.add))
                do(dve.tensor_scalar(mean, mean, 1.0 / HD, None, ALU.mult))
                do(dve.tensor_tensor(o, o, spread(mean), ALU.subtract))
                do(dve.tensor_tensor(sq, o, o, ALU.mult))
                do(dve.tensor_reduce(var, sq, AX.X, ALU.add))
                do(dve.tensor_scalar(var, var, 1.0 / HD, LNX_EPS, ALU.mult, ALU.add), "rw_var")
                need("rw_std")
                do(dve.reciprocal(var, var))
                do(dve.tensor_tensor(o, o, spread(var), ALU.mult))
                at_w, at_b = VEC["lnx_w"][0], VEC["lnx_b"][0]
                over = lambda at: vec[:, at:at + HD].unsqueeze(1).broadcast_to((P, NCK, HD))
                do(dve.tensor_tensor(o, o, over(at_w), ALU.mult))
                do(dve.tensor_tensor(o, o, over(at_b), ALU.add))
                opad = rw_pad["a"].rearrange("p a n h c -> p (a n h c)").rearrange("p (n h i) -> p n h i", n=NCK, h=2)
                for g in range(2):
                    do(dve.tensor_scalar(opad[:, :, g, :], o, K("hm")[:, g:g + 1], None, ALU.mult), "o_padded")
                for k in range(2):
                    need("rw_o")
                    do(dve.tensor_tensor(rw_pad["bonus"][:, k], rw_pad["bonus"][:, k], ps[4 + k][:], ALU.add))
                    do(dve.tensor_tensor(rw_pad["bonus"][:, k], rw_pad["bonus"][:, k], rw_pad["g"][:, k], ALU.mult))
                    both_parts(g_hi[:, 6 + k, :], g_lo[:, 6 + k, :], rw_pad["bonus"][:, k], "rw_out")

            def vector_layer(layer):
                gm = lambda k: V("g_mix2", 8 * layer + k)
                norm(gm)
                dve.wait_ge(S("mem_in"), 16 * (layer + 1))
                sum_squares(KT, lambda k: work[:, 4, MT * (k % 2):MT * (k % 2) + MT], work[:, 5, 0:MT])
                need("rms_ready")
                do(dve.reciprocal(work[:, 5, MT:], work[:, 5, MT:]))
                for k in range(KT):
                    t = work[:, 4, MT * (k % 2):MT * (k % 2) + MT]
                    do(dve.scalar_tensor_tensor(t, mem_in[:, k, :], V("g_mem2", 8 * layer + k), work[:, 5, MT:], ALU.mult, ALU.mult))
                    both_parts(mn(g_hi, k), mn(g_lo, k), t, "mem_ready")
                q, km, kk = at_m["q"], at_m["km"], at_m["k"]
                do(dve.memset(q[HD:HD + 1, :, :], 1.0))
                for name, dst in (("q", q), ("k", kk)):
                    for i in range(NH // 2):
                        if layer == 0:
                            bank = tile()
                            for g in range(2):
                                do(dve.tensor_scalar(dst[0:HD, 2 * i + g, :], bank[64 * g:64 * g + 64, :],
                                                     HD ** -0.5 if name == "q" else 1.0, None, ALU.mult),
                                   "dve_freed" if g else "dve_step")
                        else:
                            skip(1)
                            if name == "q" and i == 0:
                                dve.wait_ge(S("rope_in"), 16)
                            need("rope_copied")
                            t, sw = rope_t[:, i % 2, :], ps[6 + i % 2]
                            need("rope_swapped")
                            u = work[:, 4, :]
                            do(dve.tensor_tensor(u, sw[:], work[:, 3, :], ALU.mult))
                            do(dve.tensor_tensor(t, t, work[:, 2, :], ALU.mult))
                            for g in range(2):
                                do(dve.tensor_tensor(dst[0:HD, 2 * i + g, :], t[64 * g:64 * g + 64, :], u[64 * g:64 * g + 64, :], ALU.add),
                                   "rope_done" if g else "dve_step")
                for i in range(NH // 2):
                    skip(1)
                    need("v_turned")
                    do(dve.tensor_copy(at_m["v"][:, :, P * i:P * i + P], ps[6 + i % 2][:].rearrange("p (a b) -> p a b", a=QB)), "v_taken")
                if layer == 0:
                    bank = tile()
                    f = lambda i: work[0:NH, i, :]
                    do(dve.tensor_scalar(f(0), bank[0:NH, :], V("b_f")[0:NH], None, ALU.add), "dve_freed")
                    do(dve.tensor_scalar(f(1), f(0), -1.0, None, ALU.mult))
                    do(dve.tensor_tensor(f(1), f(1), f(0), ALU.min), "forget_in_abs")
                    need("forget_log")
                    do(dve.tensor_scalar(f(0), f(0), 0.0, None, ALU.min))
                    do(dve.tensor_tensor(f(0), f(1), f(0), ALU.subtract))
                    do(dve.memset(f(2), 1.0))
                    do(dve.tensor_tensor_scan(f(4), f(2), f(0), 0.0, ALU.mult, ALU.add), "forget_sum")
                for i in range(NMH // 2):
                    bank = tile()
                    for g in range(2):
                        do(dve.tensor_scalar(q[0:HD, NH + 2 * i + g, :], bank[64 * g:64 * g + 64, :], HD ** -0.5, None, ALU.mult),
                           "dve_freed" if g else "dve_step")
                for i in range(NMH // 2):
                    bank = tile()
                    for g in range(2):
                        do(dve.tensor_copy(km[0:HD, 2 * i + g, :], bank[64 * g:64 * g + 64, 0:MT]), "dve_freed" if g else "dve_step")
                for i in range(NMH // 2):
                    skip(1)
                    need("v_turned")
                    do(dve.tensor_copy(at_m["vm"][:, :, P * i:P * i + P],
                                       ps[6 + i % 2][:, 0:MT].rearrange("p (a b) -> p a b", a=2)), "v_taken")
                dve.wait_ge(S("mask_in"), 16 * (layer + 1))
                for u, (head, qb, width, at) in enumerate(UNITS):
                    pr = at_m["p"][:, u % 2, 0:width]
                    if u >= 2:
                        dve.wait_ge(S("probs_turned"), len(UNITS) * layer + u - 1)
                    need("scores")
                    src = ps[4 + u % 2][:, 0:width]
                    top, rec = small[:, 33 + u % 2, 0:1], small[:, 33 + u % 2, 1:2]
                    if head < NH:
                        do(dve.tensor_tensor(pr, src, masks[:, at:at + width], ALU.add))
                        do(dve.tensor_reduce(top, pr, AX.X, ALU.max, negate=True), "score_top")
                    else:
                        do(dve.tensor_reduce(top, src, AX.X, ALU.max, negate=True), "score_top")
                    need("exped")
                    do(dve.reciprocal(rec, small[:, 33 + u % 2, 2:3]))
                    do(dve.tensor_scalar(pr, pr, rec, None, ALU.mult), "probs")
                    if qb == QB - 1:
                        need("head_hi")
                        rows = slice(64 * (head % 2), 64 * (head % 2) + 64)
                        do(dve.tensor_tensor(g_lo[rows, head // 2, :], PD[rows, :], g_hi[rows, head // 2, :].bitcast(F32), ALU.subtract), "heads")
                for k in range(KT):
                    bank = tile()
                    do(dve.tensor_tensor(x[:, k, :], bank[:], x[:, k, :], ALU.add), "x_done")
                norm(lambda k: V("g_ffn2", 8 * layer + k))
                for group in range(len(FF2_GROUPS)):
                    vector_ffn2(layer, group)

            def vector_ffn2(layer, group):
                j0 = sum(FF2_GROUPS[:group])
                for j in range(FF2_GROUPS[group]):
                    for side, c in ((0, cv_m["cv"]), (1, cv_m["cg"])):
                        bank = tile()
                        need("conv_first")
                        dst, w = c[:, j % 2, :], lambda tap: V("cw2", (3 * layer + tap) * 44 + 22 * side + j0 + j)
                        do(dve.scalar_tensor_tensor(dst[:, 1:], bank[:, :T - 1], w(1), dst[:, 1:], ALU.mult, ALU.add))
                        do(dve.scalar_tensor_tensor(dst[:, 2:], bank[:, :T - 2], w(0), dst[:, 2:], ALU.mult, ALU.add), "conv_summed")
                    need("conv_gate")
                    t = cv_m["t"][:, j % 2, :]
                    do(dve.tensor_tensor(t, cv_m["cv"][:, j % 2, :], cv_m["sg"][:, j % 2, :], ALU.mult), "conv_used")
                    both_parts(g_hi[:, j, :], g_lo[:, j, :], t, "hidden")
                for k in range(KT):
                    bank = tile()
                    do(dve.tensor_tensor(x[:, k, :], bank[:], x[:, k, :], ALU.add), "x_done")

            do(dve.memset(small[:, 38, 0:1], EPS), "eps_set")
            do(dve.memset(small[:, 38, 1:2], LN_EPS), "eps_set")
            dve.wait_ge(S("vec_in"), 16)
            dve.wait_ge(S("con_in"), 16)
            c_act = small[:, 0, :]
            need("silu_c")
            do(dve.tensor_tensor(c_act, V("c", 0, 8), small[:, 1, :], ALU.mult), "c_act")
            dve.wait_ge(S("ada_used"), 16)
            do(dve.tensor_tensor(mod[:, 0:16], PA[:, 0:16], V("ada_b", 0, 16), ALU.add))
            gain1 = small[:, 2, :]
            do(dve.scalar_tensor_tensor(gain1, mod[:, 8:16], 1.0, V("g_mix", 0, 8), ALU.add, ALU.mult))
            norm(lambda k: gain1[:, k:k + 1], lambda k: mod[:, k:k + 1])

            bg, cg, z, y = (conv_m[k] for k in ("bg", "cg", "z", "y"))
            for dst in (bg, cg):
                for k in range(2):
                    do(dve.tensor_copy(dst[:, k, :], tile()[:]), "dve_freed")
            for k in range(2):
                do(dve.tensor_tensor(z[:, k, :], tile()[:], cg[:, k, :], ALU.mult), "dve_freed")
            for k in range(2):
                cw = lambda j: V("conv_w", 2 * j + k)
                do(dve.tensor_scalar(y[:, k, :], z[:, k, :], cw(2), None, ALU.mult))
                for lag in (1, 2):
                    do(dve.scalar_tensor_tensor(y[:, k, lag:], z[:, k, :T - lag], cw(2 - lag), y[:, k, lag:], ALU.mult, ALU.add))
                do(dve.tensor_tensor(y[:, k, :], y[:, k, :], bg[:, k, :], ALU.mult))
                both_parts(g_hi[:, k, :], g_lo[:, k, :], y[:, k, :], "conv_y")

            skip(4)
            m = sg_m
            dve.wait_ge(S("sg_in"), 48)
            do(dve.tensor_tensor(m["wsm"], m["ws"], m["caus"].unsqueeze(1).broadcast_to((P, 4, P)), ALU.mult), "sg_w_masked")
            need("sg_mean")
            do(dve.tensor_scalar(m["mu"], PA[:], 1.0 / DM, None, ALU.mult))
            for k in range(2):
                do(dve.tensor_tensor(m["d"][:, k, :], m["z"][:, 2 + k, :], m["mu"], ALU.subtract))
                do(dve.tensor_tensor(m["sq"][:, k, :], m["d"][:, k, :], m["d"][:, k, :], ALU.mult), "sg_square")
            need("sg_std")
            do(dve.reciprocal(m["rstd"], m["std"]))
            for k in range(2):
                do(dve.tensor_tensor(m["d"][:, k, :], m["d"][:, k, :], m["rstd"], ALU.mult))
                do(dve.tensor_scalar(m["vn"][:, k, :], m["d"][:, k, :], V("sg_w", k), V("sg_b", k), ALU.mult, ALU.add), "sg_normed")
            for k in range(2):
                need("sg_mixed")
                mix = m["mix"][:, k, :].rearrange("p (n t) -> p n t", t=P)
                do(dve.tensor_tensor(mix, ps[4 + k][:].rearrange("p (n t) -> p n t", t=P),
                                     m["bs"][:, k, :].unsqueeze(1).broadcast_to((P, QB, P)), ALU.add))
                do(dve.tensor_tensor(m["mix"][:, k, :], m["mix"][:, k, :], m["z"][:, k, :], ALU.mult))
                both_parts(g_hi[:, 2 + k, :], g_lo[:, 2 + k, :], m["mix"][:, k, :], "sg_y")

            m = s5_m
            row = lambda i: small[:, i, :]
            lam, dt, e1, mag, th, kq, sn, sh, cs, ar, ai, den, am, qr, qi, t1, t2, pr, pi, t3 = (row(i) for i in range(3, 23))
            do(dve.tensor_scalar(lam, V("a_re", 0, 8), -1e-4, None, ALU.min))
            need("s5_dt")
            do(dve.tensor_tensor(e1, lam, dt, ALU.mult), "s5_e1")
            do(dve.tensor_tensor(th, V("a_im", 0, 8), dt, ALU.mult))
            do(dve.tensor_scalar(kq, th, 1.0 / (2 * PI), ROUND, ALU.mult, ALU.add))
            do(dve.tensor_scalar(kq, kq, ROUND, None, ALU.subtract))
            for part in TWO_PI:
                do(dve.scalar_tensor_tensor(th, kq, -part, th, ALU.mult, ALU.add))
            do(dve.tensor_scalar(th, th, PI_IN, -PI_IN, ALU.min, ALU.max), "s5_angle")
            need("s5_sines")
            do(dve.tensor_tensor(cs, sh, sh, ALU.mult))
            do(dve.tensor_scalar(cs, cs, -2.0, 1.0, ALU.mult, ALU.add))
            do(dve.tensor_tensor(ar, mag, cs, ALU.mult))
            do(dve.tensor_tensor(ai, mag, sn, ALU.mult))
            do(dve.tensor_tensor(den, lam, lam, ALU.mult))
            do(dve.tensor_tensor(t1, V("a_im", 0, 8), V("a_im", 0, 8), ALU.mult))
            do(dve.tensor_tensor(den, den, t1, ALU.add))
            do(dve.reciprocal(den, den))
            do(dve.tensor_scalar(am, ar, 1.0, None, ALU.subtract))
            do(dve.tensor_tensor(qr, am, lam, ALU.mult))
            do(dve.tensor_tensor(t1, ai, V("a_im", 0, 8), ALU.mult))
            do(dve.tensor_tensor(qr, qr, t1, ALU.add))
            do(dve.tensor_tensor(qr, qr, den, ALU.mult))
            do(dve.tensor_tensor(qi, ai, lam, ALU.mult))
            do(dve.tensor_tensor(t1, am, V("a_im", 0, 8), ALU.mult))
            do(dve.tensor_tensor(qi, qi, t1, ALU.subtract))
            do(dve.tensor_tensor(qi, qi, den, ALU.mult))
            dve.wait_ge(S("s5_in"), 48)
            wide = lambda v: v.unsqueeze(2).broadcast_to((P, S5T, 16))
            bb, b_in, tmp = m["bb"], m["b_in"], m["w"][:, 5, 0:128].rearrange("p (s c) -> p s c", s=S5T)
            for out_part, (qa, qb), op in ((0, (qr, qi), ALU.subtract), (1, (qi, qr), ALU.add)):
                do(dve.tensor_tensor(bb[:, out_part], b_in[:, 0], wide(qa), ALU.mult))
                do(dve.tensor_tensor(tmp, b_in[:, 1], wide(qb), ALU.mult))
                do(dve.tensor_tensor(bb[:, out_part], bb[:, out_part], tmp, op))
            m8 = m["m8"].unsqueeze(3).broadcast_to((P, S5T, 8, 16))
            for part in range(2):
                do(dve.tensor_tensor(m["bpad"][:, part].rearrange("p s (g c) -> p s g c", g=8),
                                     bb[:, part].unsqueeze(2).broadcast_to((P, S5T, 8, 16)), m8, ALU.mult), "s5_bpad")
            for s in range(S5T):
                for part, sign in ((0, 1.0), (1, -1.0)):
                    if s % 4 == 0:
                        need("s5_cT")
                    src = ps[6 + part][:, (s // 4) * P:(s // 4) * P + P]
                    do(dve.scalar_tensor_tensor(m["cc"][:, part, s].rearrange("p (g c) -> p g c", g=8),
                                                src.rearrange("p (g c) -> p g c", g=8), sign,
                                                m["m8"][:, s].unsqueeze(2).broadcast_to((P, 8, 16)), ALU.mult, ALU.mult), "s5_cc")
            ct, st = m["ct"], m["st"]
            do(dve.memset(ct[:, :, 0:1], 1.0))
            do(dve.memset(st[:, :, 0:1], 0.0))
            do(dve.tensor_copy(pr, cs))
            do(dve.tensor_copy(pi, sn))
            L = 1
            while L < T:
                cr = pr.unsqueeze(2).broadcast_to((P, S5T, L))
                ci = pi.unsqueeze(2).broadcast_to((P, S5T, L))
                tmp = m["w"].rearrange("p a b -> p (a b)")[:, 0:S5T * L].rearrange("p (s l) -> p s l", s=S5T)
                do(dve.tensor_tensor(ct[:, :, L:2 * L], ct[:, :, 0:L], cr, ALU.mult))
                do(dve.tensor_tensor(tmp, st[:, :, 0:L], ci, ALU.mult))
                do(dve.tensor_tensor(ct[:, :, L:2 * L], ct[:, :, L:2 * L], tmp, ALU.subtract))
                do(dve.tensor_tensor(st[:, :, L:2 * L], st[:, :, 0:L], cr, ALU.mult))
                do(dve.tensor_tensor(tmp, ct[:, :, 0:L], ci, ALU.mult))
                do(dve.tensor_tensor(st[:, :, L:2 * L], st[:, :, L:2 * L], tmp, ALU.add))
                do(dve.tensor_tensor(t1, pr, pr, ALU.mult))
                do(dve.tensor_tensor(t2, pi, pi, ALU.mult))
                do(dve.tensor_tensor(t3, pr, pi, ALU.mult))
                do(dve.tensor_tensor(pr, t1, t2, ALU.subtract))
                do(dve.tensor_scalar(pi, t3, 2.0, None, ALU.mult))
                L *= 2
            w = m["w"]
            for s in range(S5T):
                need("s5_bu", 2)
                re, im = ps[4][:], ps[5][:]
                if s > 0:
                    need("s5_read")
                cos, sin = ct[:, s, :], st[:, s, :]
                do(dve.tensor_tensor(w[:, 0, :], re, cos, ALU.mult))
                do(dve.tensor_tensor(w[:, 1, :], im, sin, ALU.mult))
                do(dve.tensor_tensor(w[:, 0, :], w[:, 0, :], w[:, 1, :], ALU.add))
                do(dve.tensor_tensor(w[:, 1, :], im, cos, ALU.mult))
                do(dve.tensor_tensor(w[:, 2, :], re, sin, ALU.mult), "s5_bu_used")
                do(dve.tensor_tensor(w[:, 1, :], w[:, 1, :], w[:, 2, :], ALU.subtract))
                decay = mag[:, s:s + 1].broadcast_to((P, T))
                do(dve.tensor_tensor_scan(w[:, 2, :], decay, w[:, 0, :], 0.0, ALU.mult, ALU.add))
                do(dve.tensor_tensor_scan(w[:, 3, :], decay, w[:, 1, :], 0.0, ALU.mult, ALU.add))
                do(dve.tensor_tensor(w[:, 0, :], w[:, 2, :], cos, ALU.mult))
                do(dve.tensor_tensor(w[:, 1, :], w[:, 3, :], sin, ALU.mult))
                do(dve.tensor_tensor(w[:, 4, :], w[:, 0, :], w[:, 1, :], ALU.subtract))
                do(dve.tensor_tensor(w[:, 0, :], w[:, 2, :], sin, ALU.mult))
                do(dve.tensor_tensor(w[:, 1, :], w[:, 3, :], cos, ALU.mult))
                do(dve.tensor_tensor(w[:, 5, :], w[:, 0, :], w[:, 1, :], ALU.add), "s5_states")
            skip(2)
            for k in range(2):
                if k == 0:
                    need("s5_read")
                do(dve.scalar_tensor_tensor(w[:, k, :], m["u"][:, k, :], V("s5_d", k), ps[6 + k][:], ALU.mult, ALU.add), "s5_sum")
                need("s5_gelu")
                both_parts(g_hi[:, 4 + k, :], g_lo[:, 4 + k, :], w[:, 2 + k, :], "s5_y")
            vector_recurrence()

            sig, merged, tmp = merge_m["sig"], merge_m["merged"], merge_m["tmp"]
            for b, (branch, per) in enumerate(branch_pieces()):
                for half in range(2):
                    skip(4)
                    for f in range(4 * half, 4 * half + 4):
                        if b == 0:
                            bank = tile()
                            need("gate")
                            do(dve.tensor_tensor(merged[:, f, :], bank[:], sig[:, f, :], ALU.mult), "dve_freed")
                        else:
                            bank = tile()
                            need("gate")
                            do(dve.tensor_tensor(tmp[:, 0, :], bank[:], sig[:, f, :], ALU.mult), "dve_freed")
                            if per == 2:
                                skip(1)
                                need("glu_gate")
                                do(dve.tensor_tensor(tmp[:, 0, :], tmp[:, 0, :], tmp[:, 1, :], ALU.mult), "glu_used")
                            do(dve.tensor_tensor(merged[:, f, :], merged[:, f, :], tmp[:, 0, :], ALU.add))
            for f in range(KT):
                both_parts(h_hi[:, f, :], h_lo[:, f, :], merged[:, f, :], "merged")
            do(dve.memset(small[:, 39, :], 0.0), "merge_done")
            dve.wait_ge(S("ada_used"), 48)
            do(dve.tensor_tensor(mod[:, 16:48], PA[:, 16:48], V("ada_b", 16, 32), ALU.add))
            gain2 = small[:, 23, :]
            do(dve.scalar_tensor_tensor(gain2, mod[:, 32:40], 1.0, V("g_ffn", 0, 8), ALU.add, ALU.mult))
            for k in range(KT):
                need("tile")
                bank = ps[n.value["bank"] % BANKS]
                n.value["bank"] += 1
                do(dve.scalar_tensor_tensor(x[:, k, :], bank[:], mod[:, 16 + k:17 + k], x[:, k, :], ALU.mult, ALU.add), "x_done")

            norm(lambda k: gain2[:, k:k + 1], lambda k: mod[:, 24 + k:25 + k])

            def ffn_group(i=None):
                for j in range(8):
                    skip(1)
                    need("hidden_relu")
                    r, s = ff_m["r"][:, j % 2, :], ff_m["s"][:, j % 2, :]
                    do(dve.tensor_tensor(s, r, r, ALU.mult), "relu_used")
                    both_parts(g_hi[:, j, :], g_lo[:, j, :], s, "hidden")
                for k in range(KT):
                    bank = tile()
                    do(dve.scalar_tensor_tensor(x[:, k, :], bank[:], mod[:, 40 + k:41 + k], x[:, k, :], ALU.mult, ALU.add), "x_done")

            for g in range(FF_GROUPS):
                ffn_group()
            sum_squares(KT, lambda k: work[:, k % 2, :], work[:, 2, :])
            need("rms_ready")
            do(dve.reciprocal(work[:, 3, :], work[:, 3, :]))
            for k in range(KT):
                do(dve.scalar_tensor_tensor(x[:, k, :], x[:, k, :], V("g_final1", k), work[:, 3, :], ALU.mult, ALU.mult), "x_done")
            for layer in range(2):
                vector_layer(layer)
            sum_squares(KT, lambda k: work[:, k % 2, :], work[:, 2, :])
            need("rms_ready")
            do(dve.reciprocal(work[:, 3, :], work[:, 3, :]))
            for k in range(KT):
                do(dve.scalar_tensor_tensor(arena[:, k * T:k * T + T], x[:, k, :], V("g_final", k), work[:, 3, :], ALU.mult, ALU.mult), "result")

        @block.scalar
        def _(act):
            n = Counts()
            n.value["bank"] = 0

            def do(ins, name="act_step"):
                ins.then_inc(S(name), 1)
                act.wait_ge(S(name), n.next(name))

            def need(name, by=1):
                act.wait_ge(S(name), n.next(name, by))

            def tile():
                need("tile")
                n.value["bank"] += 1
                return ps[(n.value["bank"] - 1) % BANKS]

            def skip(tiles):
                n.next("tile", tiles)
                n.value["bank"] += tiles

            def rms(tiles, src, sq, bank, dst, width):
                for k in range(tiles):
                    done = n.value.get("square", 0)
                    if done >= 2:
                        act.wait_ge(S("square_used"), done - 1)
                    do(act.activation(sq(k), src(k), ACT.Square), "square")
                need("squares_total")
                do(act.activation(dst, bank[:, 0:width], ACT.Sqrt, bias=small[:, 38, 0:1], scale=1.0 / D), "rms_ready")

            def rms_x():
                rms(KT, lambda k: x[:, k, :], lambda k: work[:, k % 2, :], PB, work[:, 3, :], T)

            def values(i, width, layer):
                bank = tile()
                if i >= 2:
                    act.wait_ge(S("v_turned"), 8 * layer + i - 1)
                elif layer:
                    act.wait_ge(S("rope_done"), 12)
                do(act.activation(rope_t[:, i % 2, 0:width], bank[:, 0:width], ACT.Copy), "v_copied")

            act.wait_ge(S("vec_in"), 16)
            do(act.activation(small[:, 1, :], V("c", 0, 8), ACT.Sigmoid), "silu_c")
            act.wait_ge(S("eps_set"), 2)
            act.wait_ge(S("x_in"), 16)
            rms_x()
            skip(6)
            m = sg_m
            for k in range(4):
                do(act.activation(m["z"][:, k, :], tile()[:], ACT.Gelu_apprx_tanh), "act_freed")
            need("sg_var")
            do(act.activation(m["std"], PB[:], ACT.Sqrt, bias=small[:, 38, 1:2], scale=1.0 / DM), "sg_std")
            for k in range(2):
                need("sg_turned")
                do(act.activation(m["vt"][:, k].rearrange("p n c -> p (n c)"), ps[6 + k][:], ACT.Copy), "sg_vt")
            m = s5_m
            row = lambda i: small[:, i, :]
            lam, dt, e1, mag, th, kq, sn, sh, cs = (row(i) for i in range(3, 12))
            act.wait_ge(S("sg_y"), 2)
            for k in range(2):
                do(act.activation(m["u"][:, k, :], tile()[:], ACT.Copy), "act_freed")
            do(act.activation(dt, V("log_dt", 0, 8), ACT.Exp), "s5_dt")
            need("s5_e1")
            do(act.activation(mag, e1, ACT.Exp))
            need("s5_angle")
            do(act.activation(sn, th, ACT.Sin))
            do(act.activation(sh, th, ACT.Sin, scale=0.5), "s5_sines")
            for part in range(2):
                need("s5_bT", 2)
                for half in range(2):
                    do(act.activation(m["bt"][:, part, 4 * half:4 * half + 4].rearrange("p s c -> p (s c)"), ps[4 + half][:], ACT.Copy),
                       "s5_bt")
            for k in range(2):
                need("s5_sum")
                do(act.activation(m["w"][:, 2 + k, :], m["w"][:, k, :], ACT.Gelu_apprx_tanh), "s5_gelu")
            v = rw_in
            act.wait_ge(S("lora_in"), 16)
            skip(7)
            need("rw_shifted")
            do(act.activation(v["m"][0:32, :], v["m"][0:32, :], ACT.Tanh), "rw_m")
            do(act.activation(v["m"][64:128, :], v["m"][64:128, :], ACT.Sigmoid), "rw_m")
            for k in range(2):
                need("rw_z")
                do(act.activation(v["lw"][:, k], ps[4 + k][:], ACT.Sigmoid, bias=V("w0", k)), "rw_decay")
            for k in range(2):
                need("rw_az")
                do(act.activation(v["a"][:, k], ps[6 + k][:], ACT.Sigmoid, bias=V("a0", k)), "rw_a")
            for k in range(2):
                need("rw_gz")
                do(act.activation(rw_pad["g"][:, k], ps[4 + k][:], ACT.Copy), "rw_g")
            for k in range(2):
                need("rw_kk_floor")
                do(act.activation(v["e"][:, k], v["e"][:, k], ACT.Sqrt), "rw_kk_norm")
            need("rw_exp_go")
            for k in range(2):
                if k:
                    act.wait_ge(S("rw_padded"), 2)
                do(act.activation(v["e"][:, 0], v["cum"][:, k], ACT.Exp), "rw_exp")
                need("rw_before")
                do(act.activation(v["e"][:, 1], v["lw"][:, k], ACT.Exp), "rw_exp")
                do(act.activation(v["e"][:, 0], v["cum"][:, k], ACT.Exp, scale=-1.0), "rw_exp")
            for c in range(NCK):
                need("rec_o")
                for p in range(2):
                    rows = slice(64 * p, 64 * p + 64)
                    at = P + HD
                    do(act.activation(rw_sol["o"][rows, c, :], ps[6 + p][rows, at:at + HD], ACT.Copy), "rec_o_copied")
            need("rw_var")
            do(act.activation(small[:, 31:33, :].rearrange("p a b -> p (a b)"), small[:, 31:33, :].rearrange("p a b -> p (a b)"),
                              ACT.Sqrt), "rw_std")
            sig, tmp = merge_m["sig"], merge_m["tmp"]
            act.wait_ge(S("rw_out"), 2)
            n.value["dve_freed"] = 6 + 7
            glu = 0
            for b, (branch, per) in enumerate(branch_pieces()):
                for half in range(2):
                    for f in range(4 * half, 4 * half + 4):
                        bank = tile()
                        if b:
                            act.wait_ge(S("dve_freed"), 13 + 8 * (b - 1) + f + 1)
                        do(act.activation(sig[:, f, :], bank[:], ACT.Sigmoid), "gate")
                    if per == 1:
                        skip(4)
                    else:
                        for f in range(4):
                            skip(1)
                            bank = tile()
                            if glu:
                                act.wait_ge(S("glu_used"), glu)
                            do(act.activation(tmp[:, 1, :], bank[:], ACT.Sigmoid), "glu_gate")
                            glu += 1
            skip(8)
            act.wait_ge(S("x_done"), 8)
            rms_x()
            for g in range(FF_GROUPS):
                for j in range(8):
                    bank = tile()
                    if 8 * g + j >= 2:
                        act.wait_ge(S("relu_used"), 8 * g + j - 1)
                    do(act.activation(ff_m["r"][:, j % 2, :], bank[:], ACT.Relu), "hidden_relu")
                skip(8)
            act.wait_ge(S("x_done"), 8 + 8 * FF_GROUPS)
            rms_x()
            for layer in range(2):
                act.wait_ge(S("x_done"), X_DONE[layer])
                rms_x()
                act.wait_ge(S("mem_in"), 16 * (layer + 1))
                act.wait_ge(S("h_ready"), (16, 16 + 16)[layer] + 8)
                rms(KT, lambda k: mem_in[:, k, :], lambda k: work[:, 4, MT * (k % 2):MT * (k % 2) + MT], PB, work[:, 5, MT:], MT)
                if layer == 0:
                    skip(12)
                else:
                    for i in range(12):
                        bank = tile()
                        if i >= 2:
                            act.wait_ge(S("rope_done"), i - 1)
                        do(act.activation(rope_t[:, i % 2, :], bank[:], ACT.Copy, scale=HD ** -0.5 if i < 6 else 1.0), "rope_copied")
                for i in range(6):
                    values(i, T, layer)
                if layer == 0:
                    skip(1)
                    need("forget_in_abs")
                    f = lambda i: work[0:NH, i, :]
                    do(act.activation(f(3), f(1), ACT.Exp))
                    do(act.activation(f(1), f(3), ACT.Ln, bias=1.0), "forget_log")
                skip(4)
                for i in range(2):
                    values(6 + i, MT, layer)
                for u, (head, qb, width, at) in enumerate(UNITS):
                    pr = at_m["p"][:, u % 2, 0:width]
                    small_u = small[:, 33 + u % 2, :]
                    need("score_top")
                    src = pr if head < NH else ps[4 + u % 2][:, 0:width]
                    do(act.activation(pr, src, ACT.Exp, bias=small_u[:, 0:1], accum_out=small_u[:, 2:3]), "exped")
                    need("probs_turned")
                    blocks = width // P
                    do(act.activation(at_m["pt"][:, 0:blocks, P * qb:P * qb + P], PC[:, 0:width].rearrange("p (a b) -> p a b", a=blocks),
                                      ACT.Copy), "probs_kept")
                    if qb == QB - 1:
                        need("head_out")
                        rows = slice(64 * (head % 2), 64 * (head % 2) + 64)
                        do(act.activation(g_hi[rows, head // 2, :], PD[rows, :], ACT.Copy), "head_hi")
                skip(8)
                act.wait_ge(S("x_done"), X_DONE[layer] + 8)
                rms_x()
                for group, width in enumerate(FF2_GROUPS):
                    j0 = sum(FF2_GROUPS[:group])
                    for j in range(width):
                        for side, c in ((0, cv_m["cv"]), (1, cv_m["cg"])):
                            bank = tile()
                            done = 22 * layer + j0 + j
                            if done >= 2:
                                act.wait_ge(S("conv_used"), done - 1)
                            at = (3 * layer + 2) * 44 + 22 * side + j0 + j
                            do(act.activation(c[:, j % 2, :], bank[:], ACT.Identity, scale=V("cw2", at),
                                              bias=V("cb2", 44 * layer + 22 * side + j0 + j)), "conv_first")
                        need("conv_summed", 2)
                        do(act.activation(cv_m["sg"][:, j % 2, :], cv_m["cg"][:, j % 2, :], ACT.Silu), "conv_gate")
                    skip(8)
            act.wait_ge(S("x_done"), X_DONE[1] + 8 + 24)
            rms_x()

        @block.tensor
        def _(pe):
            n = Counts()
            piece, t = [0], [0]
            freed = []

            def need(name, by=1):
                pe.wait_ge(S(name), n.next(name, by))

            def open_piece():
                pe.wait_ge(S("w_split"), piece[0] + 1)
                slot = piece[0] % SPLIT
                piece[0] += 1
                return slot

            def product(slot, blocks, hi, lo, owner, width=T, first_block=0, ready=None, first=True, close=True):
                if len(freed) >= BANKS:
                    pe.wait_ge(S(freed[-BANKS][0]), freed[-BANKS][1])
                bank = ps[t[0] % BANKS][:, 0:width]
                for k in range(blocks):
                    if ready is not None:
                        ready(k)
                    cols = slice(P * (first_block + k), P * (first_block + k) + P)
                    for i, (w, a) in enumerate(((w_hi, hi), (w_hi, lo), (w_lo, hi))):
                        mm = pe.matmul(bank, w[:, slot, cols], a(k), start=(k == 0 and i == 0), stop=(k == blocks - 1 and i == 2))
                        if first and k == 0 and i == 0 and piece[0] > 1:
                            mm.then_inc(S("w_used"), 1)
                mm.then_inc(S("tile"), 1)
                t[0] += 1
                freed.append((owner, n.next(owner)))

            of = lambda pair: (lambda k: pair[:, k, :])
            h = (of(h_hi), of(h_lo))

            def project(tiles, owner, operand=h, width=T, blocks=8, ready=None):
                for i in range(tiles):
                    slot = open_piece()
                    product(slot, blocks, *operand, owner if isinstance(owner, str) else owner[i], width,
                            ready=ready if i == 0 else None)

            def h_tile(k):
                need("h_ready")

            def modulation(a, b, bank):
                for q in range(a, b):
                    pe.wait_ge(S(f"ada_in{q % ADA}"), 16 * (q // ADA + 1))
                    for k in range(8):
                        mm = pe.matmul(bank[:, q:q + 1], ada_m["ada"][:, q % ADA, P * k:P * k + P], small[:, 0, k:k + 1],
                                       start=(k == 0), stop=(k == 7))
                    mm.then_inc(S("ada_used"), 1)

            def total_squares(acc, width=T):
                need("squares_summed")
                pe.matmul(PB[:, 0:width], K("ones"), acc, start=True, stop=True).then_inc(S("squares_total"), 1)

            def swap(i):
                pe.wait_ge(S("rope_copied"), i + 1)
                if i >= 2:
                    pe.wait_ge(S("rope_done"), i - 1)
                pe.matmul(ps[6 + i % 2][:], K("rot"), rope_t[:, i % 2, :], start=True, stop=True).then_inc(S("rope_swapped"), 1)

            def turn_values(i, width, layer):
                pe.wait_ge(S("v_copied"), 8 * layer + i + 1)
                if i >= 2:
                    pe.wait_ge(S("v_taken"), 8 * layer + i - 1)
                elif layer:
                    pe.wait_ge(S("rope_done"), 12)
                for b in range(width // P):
                    mm = pe.transpose(ps[6 + i % 2][:, P * b:P * b + P], rope_t[:, i % 2, P * b:P * b + P], K("ident"))
                mm.then_inc(S("v_turned"), 1)

            def attention(layer):
                before, heads = len(UNITS) * layer, (NH + NMH) * layer
                pe.wait_ge(S("v_taken"), 8 * (layer + 1))
                if layer == 0:
                    pe.wait_ge(S("forget_in"), 16)

                def scores(u):
                    head, qb, width, _ = UNITS[u]
                    if u >= 2:
                        pe.wait_ge(S("exped"), before + u - 1)
                    rows = HD + 1 if layer == 0 and head < NH else HD
                    keys = at_m["k"][0:rows, head, 0:width] if head < NH else at_m["km"][0:rows, head - NH, :]
                    pe.matmul(ps[4 + u % 2][:, 0:width], at_m["q"][0:rows, head, P * qb:P * qb + P], keys,
                              start=True, stop=True).then_inc(S("scores"), 1)

                scores(0)
                for u, (head, qb, width, _) in enumerate(UNITS):
                    if u + 1 < len(UNITS):
                        scores(u + 1)
                    pe.wait_ge(S("probs"), before + u + 1)
                    if u:
                        pe.wait_ge(S("probs_kept"), before + u)
                    for b in range(width // P):
                        mm = pe.transpose(PC[:, P * b:P * b + P], at_m["p"][:, u % 2, P * b:P * b + P], K("ident"))
                    mm.then_inc(S("probs_turned"), 1)
                    if qb == QB - 1:
                        pe.wait_ge(S("probs_kept"), before + u + 1)
                        if head:
                            pe.wait_ge(S("heads"), heads + head)
                        out_rows = slice(64 * (head % 2), 64 * (head % 2) + 64)
                        blocks = QB if head < NH else MT // P
                        for b in range(blocks):
                            q0 = P * b if head < NH else 0
                            values = at_m["v"][:, b, HD * head:HD * head + HD] if head < NH else \
                                at_m["vm"][:, b, HD * (head - NH):HD * (head - NH) + HD]
                            mm = pe.matmul(PD[out_rows, q0:T], values, at_m["pt"][:, b, q0:T], start=(b == 0), stop=(b == blocks - 1))
                        mm.then_inc(S("head_out"), 1)

            pe.wait_ge(S("con_in"), 16)
            need("c_act")
            modulation(0, 16, PA)
            total_squares(work[:, 2, :])
            project(10, ["dve_freed"] * 6 + ["act_freed"] * 4, ready=h_tile)
            project(2, "act_freed")

            m = sg_m
            pe.wait_ge(S("act_freed"), 4)
            for k in range(2):
                mm = pe.matmul(PA[:], K("ones"), m["z"][:, 2 + k, :], start=(k == 0), stop=(k == 1))
            mm.then_inc(S("sg_mean"), 1)
            for k in range(2):
                need("sg_square")
                mm = pe.matmul(PB[:], K("ones"), m["sq"][:, k, :], start=(k == 0), stop=(k == 1))
            mm.then_inc(S("sg_var"), 1)
            for k in range(2):
                need("sg_normed")
                for b in range(QB):
                    mm = pe.transpose(ps[6 + k][:, P * b:P * b + P], m["vn"][:, k, P * b:P * b + P], K("ident"))
                mm.then_inc(S("sg_turned"), 1)
            need("sg_w_masked")
            for k in range(2):
                need("sg_vt")
                for g in range(2):
                    for b in range(QB):
                        mm = pe.matmul(ps[4 + k][64 * g:64 * g + 64, P * b:P * b + P], m["vt"][:, k, b, 64 * g:64 * g + 64],
                                       m["wsm"][:, 2 * k + g, :], start=True, stop=True)
                mm.then_inc(S("sg_mixed"), 1)

            m = s5_m
            pe.wait_ge(S("s5_in"), 48)
            for k in range(2):
                for part in range(2):
                    if k == 1 and part == 0:
                        pe.wait_ge(S("s5_cc"), 8)
                    pe.transpose(ps[6 + part][:, P * k:P * k + P], m["c_in"][:, part, k, :], K("ident")).then_inc(S("s5_cT"), 1)
            for part in range(2):
                need("s5_bpad")
                if part == 1:
                    pe.wait_ge(S("s5_bt"), 2)
                pe.wait_ge(S("sg_y"), 2)
                for half in range(2):
                    for s in range(4):
                        mm = pe.transpose(ps[4 + half][:, P * s:P * s + P], m["bpad"][:, part, 4 * half + s, :], K("ident"))
                    mm.then_inc(S("s5_bT"), 1)
            pe.wait_ge(S("s5_bt"), 4)
            pe.wait_ge(S("act_freed"), 6)
            pe.wait_ge(S("s5_cc"), 16)
            for s in range(S5T):
                if s:
                    need("s5_bu_used")
                for part in range(2):
                    pe.matmul(ps[4 + part][:], m["bt"][:, part, s, :], m["u"][:, s // 4, :], start=True, stop=True).then_inc(S("s5_bu"), 1)
                need("s5_states")
                for part in range(2):
                    mm = pe.matmul(ps[6 + s // 4][:], m["cc"][:, part, s, :], m["w"][:, 4 + part, :],
                                   start=(s % 4 == 0 and part == 0), stop=(s % 4 == 3 and part == 1))
                mm.then_inc(S("s5_read"), 1)

            pe.wait_ge(S("s5_y"), 2)
            project(7, "dve_freed")
            v, bd = rw_in, rw_bd
            pe.wait_ge(S("lora_in"), 16)
            pe.wait_ge(S("rw_m"), 2)
            for rows, names, banks in ((slice(0, 32), "rw_z", (4, 5)), (slice(32, 64), "rw_az", (6, 7)), (slice(64, 128), "rw_gz", (4, 5))):
                for k in range(2):
                    if names == "rw_gz":
                        pe.wait_ge(S("rw_decay"), k + 1)
                    pe.matmul(ps[banks[k]][:], lora[rows, P * k:P * k + P], v["m"][rows, :], start=True, stop=True).then_inc(S(names), 1)
            for k in range(2):
                need("rw_kk_square")
                pe.wait_ge(S("rw_g"), k + 1)
                pe.matmul(ps[4 + k][:], K("hsum"), v["e"][:, k], start=True, stop=True).then_inc(S("rw_kk_sum"), 1)
            for k in range(2):
                need("rw_rk")
                pe.wait_ge(S("rw_a"), k + 1)
                pe.matmul(ps[6 + k][:], K("hsum"), v["e"][:, k], start=True, stop=True).then_inc(S("rw_rk_sum"), 1)
            pe.wait_ge(S("rw_padded"), 4)
            banks = [0]

            def blocks(lhs, rhs, width, per):
                for q in range(NCK // per):
                    i = banks[0]
                    if i >= 4:
                        pe.wait_ge(S("bd_used"), i - 3)
                    banks[0] += 1
                    for c in range(per):
                        for p in range(2):
                            mm = pe.matmul(ps[4 + i % 4][64 * p:64 * p + 64, width * c:width * c + width], lhs(p, per * q + c),
                                           rhs(p, per * q + c), start=True, stop=True)
                    mm.then_inc(S("bd"), 1)

            pad = lambda name: (lambda p, c: rw_pad[name][:, p, c].rearrange("a h t -> a (h t)"))
            blocks(pad("a"), pad("b"), 64, 8)
            blocks(pad("k"), pad("a"), 64, 8)
            blocks(pad("k"), pad("r"), 64, 8)
            blocks(pad("b"), pad("r"), 64, 8)
            blocks(pad("k"), lambda p, c: K("ident"), P, 4)
            pe.wait_ge(S("v_padded"), 4)
            blocks(pad("k"), lambda p, c: K("stack"), 64, 8)
            blocks(pad("b"), lambda p, c: K("ident"), P, 4)
            pe.wait_ge(S("tT_in"), 16 * 8)
            pe.wait_ge(S("bd_used"), 18)
            need("state_set")
            for c in range(NCK):
                if c:
                    need("state_set", 2)
                rows = [slice(0, 64), slice(64, 128)]
                for p in range(2):
                    pe.matmul(ps[4 + p][rows[p], 0:HD], bd["akT"][rows[p], c, :], bd["vt"][rows[p], c, :], start=True, stop=False)
                    mm = pe.matmul(ps[4 + p][rows[p], 0:HD], pad("a")(p, c), state[:, 0, p, :], start=False, stop=True)
                mm.then_inc(S("rec_y"), 1)
                need("rec_y_copied", 2)
                if c:
                    need("rec_o_copied", 2)
                for p in range(2):
                    mm = pe.matmul(ps[6 + p][rows[p], 0:HD], bd["tT"][rows[p], c, :], chain_y[rows[p], 0, :], start=True, stop=True)
                mm.then_inc(S("rec_sa"), 1)
                need("rec_sa_copied", 2)
                for p in range(2):
                    at = slice(P, P + HD)
                    pe.matmul(ps[4 + p][:, at], bd["kt"][rows[p], c, :], bd["vt"][rows[p], c, :], start=True, stop=False)
                    mm = pe.matmul(ps[4 + p][:, at], rw_bt[rows[p], c, :], chain_y[rows[p], 1, :], start=False, stop=True)
                for p in range(2):
                    at = slice(P + HD, P + 2 * HD)
                    pe.matmul(ps[6 + p][rows[p], at], pad("r")(p, c), state[:, 0, p, :], start=True, stop=False)
                    pe.matmul(ps[6 + p][rows[p], at], bd["rbT"][rows[p], c, :], chain_y[rows[p], 1, :], start=False, stop=False)
                    mm = pe.matmul(ps[6 + p][rows[p], at], bd["rkT"][rows[p], c, :], bd["vt"][rows[p], c, :], start=False, stop=True)
                mm.then_inc(S("rec_o"), 1)
            pe.wait_ge(S("o_padded"), 2)
            opad = rw_pad["a"].rearrange("p a n h c -> p (a n h c)").rearrange("p (n x) -> p n x", n=NCK)
            for p in range(2):
                rows = slice(64 * p, 64 * p + 64)
                for c in range(NCK):
                    mm = pe.matmul(ps[4 + p][:, C * c:C * c + C], opad[rows, c, :], K("sum32")[rows, :], start=True, stop=True)
                mm.then_inc(S("rw_o"), 1)

            for b, (branch, per) in enumerate(branch_pieces()):
                y = (lambda k, b=b: g_hi[:, 2 * b + k, :], lambda k, b=b: g_lo[:, 2 * b + k, :])
                for half in range(2):
                    project(4, "gate")
                    if b == 0 and half == 0:
                        pe.wait_ge(S("conv_y"), 2)
                    if b == 3 and half == 0:
                        pe.wait_ge(S("rw_out"), 2)
                    for q in range(per):
                        slot = open_piece()
                        for i in range(4):
                            product(slot, 2, *y, "glu_gate" if per == 2 and i % 2 else "dve_freed", first_block=2 * i, first=(i == 0))
            modulation(16, 48, PA)
            pe.wait_ge(S("merged"), 8)
            project(8, "x_done")
            g = (of(g_hi), of(g_lo))
            hidden = lambda k: need("hidden")
            total_squares(work[:, 2, :])
            for group in range(FF_GROUPS):
                project(8, "hidden_relu", ready=h_tile if group == 0 else None)
                project(8, "x_done", operand=g, ready=hidden)
            total_squares(work[:, 2, :])
            n.next("x_done", 8)
            for layer in range(2):
                total_squares(work[:, 2, :])
                total_squares(work[:, 5, 0:MT], MT)
                if layer == 0:
                    project(12, "dve_freed", ready=h_tile)
                else:
                    for i in range(12):
                        project(1, "rope_copied", ready=h_tile if i == 0 else None)
                        if i:
                            swap(i - 1)
                    swap(11)
                for i in range(6):
                    project(1, "v_copied")
                    if i:
                        turn_values(i - 1, T, layer)
                turn_values(5, T, layer)
                project(3 if layer == 0 else 2, "dve_freed")
                mem = (lambda k: mn(g_hi, k), lambda k: mn(g_lo, k))
                project(2, "dve_freed", operand=mem, width=MT, ready=lambda k: need("mem_ready"))
                for i in range(2):
                    project(1, "v_copied", operand=mem, width=MT)
                    if i:
                        turn_values(6, MT, layer)
                turn_values(7, MT, layer)
                attention(layer)
                pe.wait_ge(S("heads"), 16 * (layer + 1))
                project(8, "x_done", operand=g)
                total_squares(work[:, 2, :])
                for group, pairs in enumerate(FF2_GROUPS):
                    project(2 * pairs, "conv_summed", ready=h_tile if group == 0 else None)
                    project(8, "x_done", operand=g, blocks=pairs, ready=hidden)
            total_squares(work[:, 2, :])


def pieces_of(w):
    k = w.shape[0] // P
    out = np.zeros((w.shape[1] // P, P, D), w.dtype)
    out[:, :, :k * P] = w.reshape(k, P, -1, P).transpose(2, 1, 0, 3).reshape(-1, P, k * P)
    return out


def small_pieces_of(w):
    return w.reshape(2, P, -1, 4, P).transpose(2, 1, 3, 0, 4).reshape(-1, P, D)


def columns(v):
    return v.reshape(-1, P).T


def constants():
    i, j = np.arange(P)[:, None], np.arange(64)[None, :]
    same = (i // C % 2) == (j // C)
    rot = np.zeros((P, P))
    for k in range(P):
        if k % HD < HD // 2:
            rot[k, k + HD // 2] = 1
        else:
            rot[k, k - HD // 2] = -1
    con = {"ident": np.eye(P), "ones": np.ones((P, P)), "hsum": np.kron(np.eye(2), np.ones((HD, HD))),
           "lt": same & (j % C < i % C), "gt": same & (j % C > i % C), "ge": same & (j % C >= i % C),
           "stack": (i % HD) == j, "sum32": (i % C) == np.arange(C)[None, :], "hm": (i // C % 2) == np.arange(2)[None, :],
           "rot": rot}
    con = np.concatenate([con[name] for name in CON], axis=1).astype(np.float32)
    c = np.arange(C // 2)[None, :, None] + (C // 2) * (np.arange(P)[:, None, None] // 64)
    eye = (c == np.arange(C)[None, None, :]).reshape(P, -1).astype(np.float32)
    q, k = np.arange(T)[:, None], np.arange(T)[None, :]
    fox = np.where(k <= q, 0.0, NEG)
    d = q - k
    count = ((d >= 0) & (d <= P)).astype(int) + ((d >= 0) & (d % 4 == 0)) + ((d >= 0) & (d % 16 == 0))
    dil = np.where(count > 0, np.log(np.maximum(count, 1)), NEG)
    by_block = lambda m: np.concatenate([m[b * P:b * P + P, 0:(b + 1) * P] for b in range(QB)], axis=1).astype(np.float32)
    inv = (np.float32(1.0) / np.float32(10000.0) ** (np.arange(0, HD, 2, dtype=np.float32) / np.float32(HD))).astype(np.float32)
    ang = np.arange(T, dtype=np.float32)[:, None] * inv[None, :]
    rope = np.stack([np.tile(np.cos(ang).T, (4, 1)), np.tile(np.sin(ang).T, (4, 1))], axis=1).astype(np.float32)
    m8 = np.zeros((P, S5T, 8), np.float32)
    for s in range(S5T):
        for g in range(2):
            m8[64 * g:64 * g + 64, s, (2 * s + g) % 8] = 1
    caus = (np.arange(P)[:, None] <= np.arange(P)[None, :]).astype(np.float32)
    return dict(con=con, eye=eye, mask_fox=by_block(fox), mask_dil=by_block(dil), rope=rope, s5_m8=m8, caus=caus)


def layout(i):
    i = {k: np.asarray(v) for k, v in i.items()}
    first = {k: v[0] for k, v in i.items() if not k.endswith("_2") and v.ndim > 1 and v.shape[0] == 1}
    w_in = first["w_in"]
    a_cols = 3 * DM + 128
    off_c, off_d, off_g = a_cols + 2 * DM, a_cols + 5 * DM, a_cols + 6 * DM
    stream = [pieces_of(w_in[:, off_c:off_d]), pieces_of(w_in[:, a_cols:off_c]), pieces_of(w_in[:, off_d:off_g]),
              pieces_of(w_in[:, :a_cols])]
    glu = first["s5_glu_w"].reshape(DM, 2, KT, P).transpose(0, 2, 1, 3).reshape(DM, 2 * D)
    outs = {"conv": (2, small_pieces_of(first["conv_out"])), "sg": (1, small_pieces_of(first["sg_out"])),
            "s5": (3, small_pieces_of(glu)), "rwkv": (0, small_pieces_of(first["rwkv_out"]))}
    for branch, per in branch_pieces():
        gate, w = outs[branch]
        gates = pieces_of(w_in[:, off_g + gate * D:off_g + gate * D + D])
        for half in range(2):
            stream += [gates[4 * half:4 * half + 4], w[per * half:per * half + per]]
    stream.append(pieces_of(first["w_o"]))
    for g in range(FF_GROUPS):
        cut = slice(g * D, g * D + D)
        stream += [pieces_of(first["ffn_w1"][:, cut]), pieces_of(first["ffn_w2"][cut])]
    dmix = NH * HD
    for layer, w in ((0, i["w_in_fox_2"][0]), (1, i["w_in_dil_2"][0])):
        if layer == 0:
            forget = np.zeros((D, P), w.dtype)
            forget[:, :NH] = w[:, 3 * dmix:3 * dmix + NH]
            w = np.concatenate([w[:, :3 * dmix], forget, w[:, 3 * dmix + NH:]], axis=1)
        up, down = i["w_up_2"][layer], i["w_down_2"][layer]
        stream += [pieces_of(w), pieces_of(i["w_mem_kv_2"][layer]), pieces_of(i["w_out_2"][layer])]
        pairs = pieces_of(up.reshape(D, 2, FF2, P).transpose(0, 2, 1, 3).reshape(D, -1))
        at = 0
        for n in FF2_GROUPS:
            stream += [pairs[2 * at:2 * at + 2 * n], pieces_of(down[at * P:(at + n) * P])]
            at += n
    f = first
    vec = {"c": columns(i["c"][0]), "ada_b": columns(f["ada_b"]), "g_mix": columns(f["norm_mix_g"]), "mu": columns(f["rwkv_mu"]),
           "w0": columns(f["rwkv_w0"]), "a0": columns(f["rwkv_a0"]), "kk": columns(f["rwkv_kk"]), "ka": columns(f["rwkv_ka"]),
           "rk": columns(f["rwkv_rk"].reshape(-1)), "sg_w": columns(f["sg_ln_w"]), "sg_b": columns(f["sg_ln_b"]),
           "conv_w": columns(f["conv_w"].reshape(-1)), "s5_d": columns(f["s5_d"]),
           "a_re": columns(f["s5_a_re"].reshape(-1)), "a_im": columns(f["s5_a_im"].reshape(-1)),
           "log_dt": columns(np.repeat(f["s5_log_dt"], 64)), "g_ffn": columns(f["norm_ffn_g"]), "g_final1": columns(i["final_g"]),
           "g_mix2": columns(i["norm_mix_2"].reshape(-1)), "g_mem2": columns(i["norm_mem_2"].reshape(-1)),
           "g_ffn2": columns(i["norm_ffn_2"].reshape(-1)),
           "b_f": np.concatenate([i["b_forget_2"][0], np.zeros(P - NH, np.float32)])[:, None],
           "cw2": columns(i["conv_w_2"].reshape(-1)), "cb2": columns(i["conv_b_2"].reshape(-1)),
           "g_final": columns(i["norm_final_2"]),
           "lnx_w": np.repeat(f["rwkv_lnx_w"].reshape(H_A, HD), C, axis=0), "lnx_b": np.repeat(f["rwkv_lnx_b"].reshape(H_A, HD), C, axis=0)}
    b = np.stack([f["s5_b_re"], f["s5_b_im"]])
    c = np.stack([f["s5_c_re"], f["s5_c_im"]])
    arrays = dict(
        w=np.concatenate(stream), ada=pieces_of(f["ada_w"]), vec=np.concatenate([vec[name] for name in VEC], axis=1),
        xT=i["x"][0].reshape(T, KT, P).transpose(2, 1, 0), memT=i["mem_2"][0].reshape(MT, KT, P).transpose(2, 1, 0),
        sg_ws=f["sg_ws"].transpose(2, 0, 1), sg_bs=np.repeat(f["sg_bs"].reshape(2, 2, 1, P), 64, axis=2).transpose(1, 2, 0, 3).reshape(P, 2, P),
        s5_b=b.reshape(2, S5T, P, 16).transpose(2, 0, 1, 3),
        s5_c=np.concatenate([c, c], axis=3).reshape(2, 2, P, P).transpose(2, 0, 1, 3),
        lora=np.concatenate([f["rwkv_w2"], f["rwkv_a2"], f["rwkv_g2"]]), **constants())
    return {k: np.ascontiguousarray(v) for k, v in arrays.items()}


def kernel(**inputs):
    import concourse.bacc as bacc
    from concourse.bass_utils import run_bass_kernel_spmd

    nc = bacc.Bacc("TRN2", target_bir_lowering=False, num_devices=1)
    arrays = layout(inputs)
    aps = {k: nc.dram_tensor(f"in_{k}", v.shape, mybir.dt.from_np(v.dtype), kind="ExternalInput").ap() for k, v in arrays.items()}
    out = nc.dram_tensor("out_y", (P, KT, T), F32, kind="ExternalOutput").ap()
    build(nc, aps, out)
    r = run_bass_kernel_spmd(nc, [{f"in_{k}": v for k, v in arrays.items()}], core_ids=[0])
    y = r.results[0]["out_y"]
    return np.ascontiguousarray(y.transpose(2, 1, 0)).reshape(1, T, D)
```

```python
from contextlib import ExitStack

import numpy as np

import concourse.bass as bass
from concourse import mybir
from concourse.alu_op_type import AluOpType as ALU

F32 = mybir.dt.float32
F32R = mybir.dt.float32r
ACT = mybir.ActivationFunctionType
AX = mybir.AxisListType

P = 128
T = 512
D = 1024
KT = D // P
DM = 256
H_A, HD = 4, 64
C = 32
NCK = T // C
NB = 4
FF_GROUPS = 4096 // D
FF2 = 2816 // P
FF2_GROUPS = [8, 8, 6]
NH, NMH = 12, 4
MT = 256
QB = T // P
S5T = 8

RAW, SPLIT, BANKS, ADA = 2, 2, 4, 4

N_FOX, N_DIL = 21, 20
N_KV = 4

EPS, LN_EPS, LNX_EPS = 1e-6, 1e-5, 64e-5
NEG = -1e30
PI = float(np.pi)
PI_IN = 3.1415925
TWO_PI = [6.28125, 0.0019350051879882812, 3.019916e-07]
ROUND = 1.5 * 2.0 ** 23


def mixer_pieces():
    order = [("conv_in", 6), ("sg_in", 4), ("s5_in", 2)]
    for branch in ("conv", "sg"):
        order += [(branch + "_gate", 4), (branch + "_out", 1)] * 2
    order += [("rwkv_in", 7)] + [("s5_gate", 4), ("s5_out", 2)] * 2
    return order + [("rwkv_gate", 4), ("rwkv_gate", 4), ("rwkv_out", 1), ("rwkv_out", 1)]


def vec_columns():
    sizes = [("c", 8), ("ada_b", 48), ("g_mix", 8), ("mu", 7), ("w0", 2), ("a0", 2), ("kk", 2), ("ka", 2), ("rk", 2),
             ("sg_w", 2), ("sg_b", 2), ("conv_w", 6), ("s5_d", 2), ("a_re", 8), ("a_im", 8), ("log_dt", 8),
             ("g_ffn", 8), ("g_final1", 8), ("g_mix2", 16), ("g_mem2", 16), ("g_ffn2", 16), ("b_f", 1),
             ("cw2", 2 * 3 * 44), ("cb2", 2 * 44), ("g_final", 8), ("lnx_w", 64), ("lnx_b", 64)]
    at, cols = 0, {}
    for name, n in sizes:
        cols[name] = (at, n)
        at += n
    return cols, at


VEC, NVEC = vec_columns()


def const_columns():
    sizes = [("ident", 128), ("ones", 128), ("hsum", 128), ("lt", 64), ("gt", 64), ("ge", 64),
             ("stack", 64), ("sum32", 32), ("hm", 2), ("rot", 128)]
    at, cols = 0, {}
    for name, n in sizes:
        cols[name] = (at, n)
        at += n
    return cols, at


CON, NCON = const_columns()


X_DONE = [8 + 8 * FF_GROUPS + 8, 8 + 8 * FF_GROUPS + 8 + 8 + 24]

UNITS = [(h, b, (b + 1) * P, b * (b + 1) // 2 * P) for h in range(NH) for b in range(QB)] + \
        [(NH + h, b, MT, 0) for h in range(NMH) for b in range(QB)]


class Counts:

    def __init__(self):
        self.value = {}

    def next(self, name, by=1):
        self.value[name] = self.value.get(name, 0) + by
        return self.value[name]

    def turn(self, i, per):
        self.start = dict(self.value)
        for name, n in per.items():
            self.value[name] = self.value.get(name, 0) + i * n

    def leave(self, turns, per):
        for name, n in per.items():
            self.value[name] = self.start.get(name, 0) + turns * n


def build(nc, A, out):
    n_mixer = sum(n for _, n in mixer_pieces())
    n_block1 = n_mixer + 8 + 2 * 8 * FF_GROUPS
    n_early = 12 + 2 * 10 + 7 + 2 * 6
    pieces = n_block1 + sum(n + N_KV + 8 + 2 * FF2 + 8 * len(FF2_GROUPS) for n in (N_FOX, N_DIL))
    with ExitStack() as ctx:
        def sb(name, shape, dt=F32):
            return ctx.enter_context(nc.sbuf_tensor(name, shape, dt))

        sems = {}

        def S(name):
            if name not in sems:
                sems[name] = ctx.enter_context(nc.semaphore(name))
            return sems[name]

        raw = sb("raw", [P, RAW, D])
        w_hi = sb("w_hi", [P, SPLIT, D], F32R)
        w_lo = sb("w_lo", [P, SPLIT, D], F32R)
        zero = sb("zero", [P, 1])
        x = sb("x", [P, KT, T])
        h_hi = sb("h_hi", [P, KT, T], F32R)
        h_lo = sb("h_lo", [P, KT, T], F32R)
        g_hi = sb("g_hi", [P, KT, T], F32R)
        g_lo = sb("g_lo", [P, KT, T], F32R)
        work = sb("work", [P, 6, T])
        vec = sb("vec", [P, NVEC])
        con = sb("con", [P, NCON])
        mod = sb("mod", [P, 48])
        small = sb("small", [P, 40, 8])
        ARENA = 21504
        arena = sb("arena", [P, ARENA])
        ps = [ctx.enter_context(nc.psum_tensor(f"ps{i}", [P, T], F32)) for i in range(8)]
        PA, PB, PC, PD = ps[4:]

        a_dram = nc.dram_tensor("pair_scores", (H_A, C, NCK, C), F32, kind="Internal").ap()
        t_dram = nc.dram_tensor("pair_inverse", (2, H_A, NCK, C // 2, C), F32, kind="Internal").ap()

        def V(name, i=0, n=None):
            at, size = VEC[name]
            return vec[:, at + i:at + i + (n or 1)]

        def K(name):
            at, size = CON[name]
            return con[:, at:at + size]

        def place(sizes, at=0):
            parts = {}
            for name, shape in sizes:
                n = int(np.prod(shape))
                assert at + n <= ARENA, (name, at + n)
                flat = arena[:, at:at + n]
                if len(shape) == 2:
                    flat = flat.rearrange("p (a b) -> p a b", a=shape[0])
                elif len(shape) == 3:
                    flat = flat.rearrange("p (a b c) -> p a b c", a=shape[0], b=shape[1])
                elif len(shape) == 4:
                    flat = flat.rearrange("p (a b c d) -> p a b c d", a=shape[0], b=shape[1], c=shape[2])
                parts[name] = flat
                at += n
            parts["end"] = at
            return parts

        def gate_room(p):
            at = (ARENA - 4 * T, ARENA - 4 * T, ARENA - 5 * T, 2048 if p < 28 else 4096)[p // 8] + p % 4 * T
            return arena[:, at:at + T]

        merged, product, glu = x, work[:, 0, :], work[:, 1, :]
        ada_m = place([("ada", (ADA, D))], at=ARENA - ADA * D)
        conv_m = place([("bg", (2, T)), ("cg", (2, T)), ("z", (2, T)), ("y", (2, T))])
        sg_m = place([("z", (4, T)), ("mu", (T,)), ("d", (2, T)), ("sq", (2, T)), ("std", (T,)), ("rstd", (T,)),
                      ("vn", (2, T)), ("vt", (2, 4, P)), ("ws", (4, P)), ("wsm", (4, P)), ("bs", (2, P)),
                      ("mix", (2, T)), ("caus", (P,))], at=4096)
        s5_m = place([("ct", (8, T)), ("st", (8, T)), ("w", (6, T)), ("bt", (2, 8, P)), ("bpad", (2, 8, P)),
                      ("bb", (2, 8, 16)), ("b_in", (2, 8, 16)), ("m8", (8, 8)), ("c_in", (2, 2, P)), ("u", (2, T))])
        s5_m["cc"] = s5_m["bpad"]
        assert s5_m["end"] <= ARENA - 4 * T
        rw_pad = place([("a", (2, NCK, 2, C)), ("b", (2, NCK, 2, C)), ("k", (2, NCK, 2, C)), ("r", (2, NCK, 2, C)),
                        ("g", (2, T)), ("bonus", (2, T))])
        rw_pad["all"] = arena[:, 0:4 * 2 * NCK * 2 * C]
        base_at = rw_pad["end"]
        rw_in = place([("r", (2, T)), ("k", (2, T)), ("v", (2, T)), ("m", (T,)), ("lw", (2, T)), ("a", (2, T)),
                       ("kk", (2, T)), ("cum", (2, T)), ("e", (2, T))], at=base_at)
        rw_bd = place([("ab", (NCK, 64)), ("akT", (NCK, 64)), ("vt", (NCK, 64)), ("rbT", (NCK, 64)),
                       ("rkT", (NCK, 64)), ("tT", (NCK, 64)), ("kt", (NCK, P))], at=base_at)
        rw_sol = place([("as", (C, C)), ("z", (C // 2, C)), ("o", (NCK, 64))],
                       at=max(rw_in["end"], rw_bd["end"]))
        at_m = place([("q", (NH + NMH, T)), ("k", (NH, T)), ("km", (NMH, MT)), ("v", (QB, NH * HD)), 
                      ("p", (2, T)), ("pt", (QB, T))])
        rw_sol["prod"] = work[:, 4, :]
        at_m["vm"] = work[:, 5, :].rearrange("p (a b) -> p a b", a=2)
        probs = [at_m["p"][:, 0, :], at_m["p"][:, 1, :], work[:, 3, :], work[:, 4, :]]
        mem_in = at_m["pt"].rearrange("p a b -> p (a b)").rearrange("p (k t) -> p k t", k=KT)
        rope_t = arena[:, at_m["end"] - 4 * T - 2 * T:at_m["end"] - 4 * T].rearrange("p (a b) -> p a b", a=2)
        cv_m = place([("cv", (2, T)), ("cg", (2, T)), ("sg", (2, T)), ("t", (2, T))])
        ff_m = place([("r", (2, T)), ("s", (2, T))])
        rw_bt = rw_pad["k"].rearrange("p a n h c -> p (a n h c)").rearrange("p (n c) -> p n c", n=NCK)
        state = work[:, 2, 0:6 * HD].rearrange("p (a b c) -> p a b c", a=3, b=2)
        chain_y = work[:, 3, 0:2 * HD].rearrange("p (a b) -> p a b", a=2)


        block = ctx.enter_context(nc.Block())
        lora = work[:, 5, 0:DM]
        masks = work[:, 0:3, :].rearrange("p a b -> p (a b)")[:, 0:(QB * (QB + 1) // 2) * P]

        def mn(pair, k):
            return pair[:, k // 2, MT * (k % 2):MT * (k % 2) + MT]


        @block.sync
        def _(sp):
            sp.dma_start(vec[:], A["vec"]).then_inc(S("vec_in"), 16)
            sp.dma_start(con[:], A["con"]).then_inc(S("con_in"), 16)
            ada = ada_m["ada"]
            for q in range(ADA):
                sp.dma_start(ada[:, q, :], A["ada"][q]).then_inc(S(f"ada_in{q}"), 16)
            sp.dma_start(x[:], A["xT"]).then_inc(S("x_in"), 16)
            for q in range(RAW):
                if q < pieces:
                    sp.dma_start(raw[:, q, :], A["w"][q]).then_inc(S(f"raw_in{q}"), 16)
            for q in range(ADA, 16):
                sp.wait_ge(S("ada_used"), q - ADA + 1)
                sp.dma_start(ada[:, q % ADA, :], A["ada"][q]).then_inc(S(f"ada_in{q % ADA}"), 16)
            def stream_to(a, b):
                def one(q, n, slot):
                    sp.wait_ge(S("w_split"), q - RAW + 1)
                    sp.dma_start(raw[:, slot, :], n).then_inc(S(f"raw_in{slot}"), 16)
                while a < b and (a % RAW or b - a < RAW):
                    one(a, A["w"][a], a % RAW)
                    a += 1
                turns = (b - a) // RAW
                if turns == 1:
                    for k in range(RAW):
                        one(a + k, A["w"][a + k], k)
                elif turns > 1:
                    w = A["w"][0:pieces // RAW * RAW].rearrange("(g s) p n -> g s p n", s=RAW)
                    with sp.Fori(a // RAW, a // RAW + turns) as g:
                        for k in range(RAW):
                            one(g * RAW + k, w[bass.ds(g, 1), k].rearrange("a p n -> (a p) n"), k)
                a += turns * RAW
                while a < b:
                    one(a, A["w"][a], a % RAW)
                    a += 1

            stream_to(RAW, 8)
            sp.wait_ge(S("ada_used"), 16)
            sp.dma_start(sg_m["ws"], A["sg_ws"]).then_inc(S("sg_in"), 16)
            sp.dma_start(sg_m["bs"], A["sg_bs"]).then_inc(S("sg_in"), 16)
            sp.dma_start(sg_m["caus"], A["caus"]).then_inc(S("sg_in"), 16)
            for name, key in (("b_in", "s5_b"), ("m8", "s5_m8"), ("c_in", "s5_c")):
                sp.dma_start(s5_m[name], A[key]).then_inc(S("s5_in"), 16)
            stream_to(8, 32)
            stream_to(32, 34)
            sp.wait_ge(S("s5_y"), 2)
            sp.dma_start(lora, A["lora"]).then_inc(S("lora_in"), 16)
            stream_to(34, n_early)
            sp.wait_ge(S("ab_scores"), 1)
            ab = rw_bd["ab"]
            for h in range(H_A):
                sp.dma_start(a_dram[h], ab[C * h:C * h + C, :, C * (h % 2):C * (h % 2) + C]).then_inc(S("a_out"), 16)
            sp.wait_ge(S("a_out"), 16 * H_A)
            for half in range(2):
                for h in range(H_A):
                    at = 64 * half + NCK * h
                    sp.dma_start(rw_sol["as"][at:at + NCK], a_dram[h].rearrange("t n s -> n t s")).then_inc(S("a_in"), 16)
            sp.dma_start(rw_sol["z"], A["eye"].rearrange("p (c t) -> p c t", t=C)).then_inc(S("a_in"), 16)
            stream_to(n_early, n_early + 4)
            sp.wait_ge(S("solved"), C - 1)
            sp.dma_start(t_dram.rearrange("a h n c t -> (a h n) (c t)"),
                         rw_sol["z"].rearrange("p c t -> p (c t)")).then_inc(S("t_out"), 16)
            sp.wait_ge(S("t_out"), 16)
            sp.wait_ge(S("tT_clear"), 1)
            for half in range(2):
                for h in range(H_A):
                    at = C * h + C // 2 * half
                    sp.dma_start(rw_bd["tT"][at:at + C // 2, :, C * (h % 2):C * (h % 2) + C],
                                 t_dram[half, h].rearrange("n c t -> c n t")).then_inc(S("tT_in"), 16)
            stream_to(n_early + 4, n_early + 6)
            sp.wait_ge(S("rw_out"), 2)
            for q in range(16, 48):
                if q >= 16 + ADA:
                    sp.wait_ge(S("ada_used"), q - ADA + 1)
                sp.dma_start(ada_m["ada"][:, q % ADA, :], A["ada"][q]).then_inc(S(f"ada_in{q % ADA}"), 16)
                if q == 23:
                    stream_to(n_early + 6, n_early + 8)
                if q == 31:
                    stream_to(n_early + 8, n_mixer)
            sp.wait_ge(S("merged"), 8)
            sp.dma_start(x[:], A["xT"]).then_inc(S("x_in"), 16)
            stream_to(n_mixer, n_block1)
            first = n_block1
            for layer, n_in in ((0, N_FOX), (1, N_DIL)):
                sp.wait_ge(S("x_done"), X_DONE[layer])
                sp.dma_start(mem_in, A["memT"]).then_inc(S("mem_in"), 16)
                stream_to(first, first + 2)
                if layer:
                    sp.wait_ge(S("h_ready"), 8 * 5)
                    sp.dma_start(work[:, 2:4, :], A["rope"]).then_inc(S("rope_in"), 16)
                    stream_to(first + 2, first + 14)
                    sp.wait_ge(S("rope_done"), 12)
                    sp.dma_start(masks, A["mask_dil"]).then_inc(S("mask_in"), 16)
                    stream_to(first + 14, first + n_in + N_KV)
                else:
                    stream_to(first + 2, first + n_in + N_KV)
                    sp.wait_ge(S("forget_sum"), 1)
                    sp.dma_start(at_m["k"][HD:HD + 1, :, :], work[0:NH, 4, :]).then_inc(S("forget_in"), 16)
                    sp.wait_ge(S("forget_in"), 16)
                    sp.dma_start(masks, A["mask_fox"]).then_inc(S("mask_in"), 16)
                last = first + n_in + N_KV + 8 + 2 * FF2 + 24
                stream_to(first + n_in + N_KV, last)
                first = last
            sp.wait_ge(S("result"), KT)
            sp.dma_start(out, arena[:, 0:KT * T].rearrange("p (k t) -> p k t", k=KT)).then_inc(S("stored"), 16)
            sp.wait_ge(S("stored"), 16)

        @block.gpsimd
        def _(pool):
            pool.memset(zero[:], 0.0).then_inc(S("zero_set"), 1)
            pool.wait_ge(S("zero_set"), 1)

            def split(q, slot, landed, free):
                pool.wait_ge(S(f"raw_in{slot}"), landed)
                if free is not None:
                    pool.wait_ge(S("w_used"), free)
                pool.tensor_tensor(w_hi[:, slot % SPLIT, :], raw[:, slot, :], zero[:].broadcast_to((P, D)), ALU.add).then_inc(S("w_high"), 1)
                pool.wait_ge(S("w_high"), q + 1)
                pool.tensor_tensor(w_lo[:, slot % SPLIT, :], raw[:, slot, :], w_hi[:, slot % SPLIT, :].bitcast(F32),
                                   ALU.subtract).then_inc(S("w_split"), 1)

            for q in range(min(RAW, pieces)):
                split(q, q, 16, None if q < SPLIT else q - SPLIT + 1)
            turns = pieces // RAW
            if turns > 1:
                with pool.Fori(1, turns) as g:
                    for k in range(RAW):
                        split(g * RAW + k, k, g * 16 + 16, g * RAW + (k - SPLIT + 1))
            for q in range(max(turns, 1) * RAW, pieces):
                split(q, q % RAW, 16 * (q // RAW + 1), q - SPLIT + 1)

        @block.vector
        def _(dve):
            n = Counts()

            def do(ins, name="dve_step"):
                ins.then_inc(S(name), 1)
                dve.wait_ge(S(name), n.next(name))

            def need(name, by=1):
                dve.wait_ge(S(name), n.next(name, by))

            def both_parts(hi, lo, src, name):
                do(dve.tensor_copy(hi, src))
                do(dve.tensor_tensor(lo, src, hi.bitcast(F32), ALU.subtract), name)

            def add_square(k, sq, acc):
                need("square")
                if k == 0:
                    do(dve.tensor_copy(acc, sq(k)), "square_used")
                else:
                    do(dve.tensor_tensor(acc, acc, sq(k), ALU.add), "square_used")

            def add_square_x(k):
                add_square(k, lambda k: work[:, k % 2, :], work[:, 2, :])

            def last_terms(update):
                for k in range(KT):
                    update(k)
                    if k:
                        add_square_x(k - 1)
                add_square_x(KT - 1)

            def norm(gain, shift=None):
                need("rms_ready")
                do(dve.reciprocal(work[:, 3, :], work[:, 3, :]))
                for k in range(KT):
                    t = work[:, 4 + k % 2, :]
                    do(dve.scalar_tensor_tensor(t, x[:, k, :], gain(k), work[:, 3, :], ALU.mult, ALU.mult))
                    if shift is not None:
                        do(dve.tensor_scalar(t, t, shift(k), None, ALU.add))
                    both_parts(h_hi[:, k, :], h_lo[:, k, :], t, "h_ready")

            def add_to_x(k, gate=None):
                need("tile")
                bank = ps[n.value["bank"] % BANKS]
                if gate is None:
                    do(dve.tensor_tensor(x[:, k, :], bank[:], x[:, k, :], ALU.add), "dve_freed")
                else:
                    do(dve.scalar_tensor_tensor(x[:, k, :], bank[:], gate, x[:, k, :], ALU.mult, ALU.add), "dve_freed")
                n.value["bank"] += 1

            n.value["bank"] = 0

            def tile():
                need("tile")
                n.value["bank"] += 1
                return ps[(n.value["bank"] - 1) % BANKS]

            def skip(tiles):
                n.next("tile", tiles)
                n.value["bank"] += tiles


            def vector_recurrence():
                v, bd, sol = rw_in, rw_bd, rw_sol
                keep = small[:, 24, 0:7]
                do(dve.tensor_scalar(keep, V("mu", 0, 7), -1.0, 1.0, ALU.mult, ALU.add))
                for i, dst in enumerate([v["r"][:, 0], v["r"][:, 1], v["k"][:, 0], v["k"][:, 1], v["v"][:, 0], v["v"][:, 1], v["m"]]):
                    bank = tile()
                    do(dve.tensor_scalar(dst, bank[:], keep[:, i:i + 1], None, ALU.mult))
                    do(dve.scalar_tensor_tensor(dst[:, 1:], bank[:, :T - 1], V("mu", i), dst[:, 1:], ALU.mult, ALU.add), "dve_freed")
                do(dve.memset(rw_pad["all"], 0.0), "rw_shifted")
                e, cum, lw, kk = v["e"], v["cum"], v["lw"], v["kk"]
                reset = e[:, 1, :]
                do(dve.memset(reset, 1.0))
                do(dve.memset(reset.rearrange("p (n t) -> p n t", t=C)[:, :, 0:1], 0.0))
                for k in range(2):
                    need("rw_decay")
                    do(dve.tensor_scalar(lw[:, k], lw[:, k], -float(np.exp(-0.5)), None, ALU.mult))
                    do(dve.tensor_tensor_scan(cum[:, k], reset, lw[:, k], 0.0, ALU.mult, ALU.add), "rw_cum")
                for k in range(2):
                    do(dve.tensor_scalar(kk[:, k], v["k"][:, k], V("kk", k), None, ALU.mult))
                    do(dve.tensor_tensor(e[:, k], kk[:, k], kk[:, k], ALU.mult), "rw_kk_square")
                skip(4)
                for f in range(4):
                    gated(f, glu_tiles=True)
                for k in range(2):
                    need("rw_kk_sum")
                    do(dve.tensor_scalar(e[:, k], PA[:] if k == 0 else PB[:], 1e-24, None, ALU.max), "rw_kk_floor")
                for k in range(2):
                    need("rw_kk_norm")
                    do(dve.reciprocal(e[:, k], e[:, k]))
                    do(dve.tensor_tensor(kk[:, k], kk[:, k], e[:, k], ALU.mult))
                drop = small[:, 24, 0:2]
                do(dve.tensor_scalar(drop, V("ka", 0, 2), -1.0, 1.0, ALU.mult, ALU.add))
                for k in range(2):
                    need("rw_a")
                    do(dve.tensor_scalar(e[:, k], v["a"][:, k], V("ka", k), drop[:, k:k + 1], ALU.mult, ALU.add))
                    do(dve.tensor_tensor(v["k"][:, k], v["k"][:, k], e[:, k], ALU.mult))
                    do(dve.scalar_tensor_tensor(e[:, k], v["r"][:, k], V("rk", k), v["k"][:, k], ALU.mult, ALU.mult), "rw_rk")
                    do(dve.tensor_tensor(v["a"][:, k], v["a"][:, k], kk[:, k], ALU.mult))
                for k in range(2):
                    need("rw_rk_sum")
                    do(dve.tensor_tensor(rw_pad["bonus"][:, k], (PC if k == 0 else PD)[:], v["v"][:, k], ALU.mult))
                do(dve.memset(small[:, 39, :], 0.0), "rw_exp_go")
                skip(4)
                for f in range(4):
                    gated(4 + f, glu_tiles=True)
                half = lambda ap, g: ap[64 * g:64 * g + 64].rearrange("p (n t) -> p n t", t=C)
                pad = lambda name, k, g: rw_pad[name][64 * g:64 * g + 64, k, :, g, :]
                pc = small[:, 25:29, :].rearrange("p a b -> p (a b)").rearrange("p (k n) -> p k n", k=2)
                for k in range(2):
                    need("rw_exp")
                    for g in range(2):
                        do(dve.tensor_tensor(pad("r", k, g), half(v["r"][:, k], g), half(e[:, 0], g), ALU.mult))
                    do(dve.tensor_copy(pc[:, k, :], e[:, 0].rearrange("p (n t) -> p n t", t=C)[:, :, C - 1]))
                    do(dve.tensor_tensor(lw[:, k], cum[:, k], lw[:, k], ALU.subtract), "rw_before")
                    need("rw_exp")
                    for g in range(2):
                        do(dve.scalar_tensor_tensor(pad("a", k, g), half(kk[:, k], g), -1.0, half(e[:, 1], g), ALU.mult, ALU.mult))
                    need("rw_exp")
                    for g in range(2):
                        do(dve.tensor_tensor(pad("b", k, g), half(v["a"][:, k], g), half(e[:, 0], g), ALU.mult))
                        do(dve.tensor_tensor(pad("k", k, g), half(v["k"][:, k], g), half(e[:, 0], g), ALU.mult), "rw_padded")

                def bd_copy(dst, mask=None, per=8, name=None):
                    for q in range(NCK // per):
                        need("bd")
                        i = n.value["bd"] - 1
                        src = ps[4 + i % 4][:, 0:per * (T // per)].rearrange("p (n c) -> p n c", n=per)
                        d = dst[:, per * q:per * q + per, :]
                        if mask is None:
                            ins = dve.tensor_copy(d, src)
                        else:
                            ins = dve.tensor_tensor(d, src, mask.unsqueeze(1).broadcast_to((P, per, 64)), ALU.mult)
                        do(ins, "bd_used")

                bd_copy(bd["ab"], K("lt"))
                do(dve.memset(small[:, 39, :], 0.0), "ab_scores")
                bd_copy(bd["akT"], K("gt"))
                bd_copy(bd["rkT"], K("ge"))
                bd_copy(bd["rbT"], K("ge"))
                do(dve.memset(bd["tT"], 0.0), "tT_clear")
                bd_copy(bd["kt"], per=4)
                do(dve.memset(rw_pad["k"].rearrange("p a n h c -> p (a n h c)"), 0.0))
                for k in range(2):
                    for g in range(2):
                        do(dve.tensor_copy(pad("k", k, g), half(v["v"][:, k], g)), "v_padded")
                bd_copy(bd["vt"])
                bd_copy(rw_bt, per=4)
                dve.wait_ge(S("a_in"), 16 * 9)
                a_m, z, prod = sol["as"], sol["z"], sol["prod"]
                do(dve.memset(a_m.rearrange("p t s -> p (t s)")[:, 0:C * C:C + 1], 1.0))
                for i in range(1, C):
                    pr = prod[:, 0:C // 2 * (i + 1)].rearrange("p (c j) -> p c j", j=i + 1)
                    do(dve.tensor_tensor(pr, z[:, :, 0:i + 1], a_m[:, i, 0:i + 1].unsqueeze(1).broadcast_to((P, C // 2, i + 1)), ALU.mult))
                    do(dve.tensor_reduce(z[:, :, i], pr, AX.X, ALU.add), "solved")
                do(dve.memset(state, 0.0), "state_set")
                for c in range(NCK):
                    now, then = c % 2, 1 - c % 2
                    for p in range(2):
                        do(dve.tensor_scalar(state[:, 2, p, :], state[:, now, p, :], pc[:, p, c:c + 1], None, ALU.mult))
                    need("rec_y", 2)
                    do(dve.tensor_copy(chain_y[0:64, 0, :], ps[0][0:64, 0:HD]), "rec_y_copied")
                    need("rec_sa", 2)
                    do(dve.tensor_copy(chain_y[0:64, 1, :], ps[6][0:64, 0:HD]), "rec_sa_copied")
                    for p in range(2):
                        need("rec_state")
                        if p == 0 and c:
                            need("rec_o")
                        do(dve.scalar_tensor_tensor(state[:, then, p, :], ps[4 + p][:, P:P + HD], pc[:, p, c:c + 1], state[:, 2, p, :],
                                                    ALU.mult, ALU.add), "state_set")
                need("rec_o")
                need("rec_o_copied", 2 * NCK)
                o, sq = sol["o"], bd["ab"]
                mean, var = small[:, 29:31, :].rearrange("p a b -> p (a b)"), small[:, 31:33, :].rearrange("p a b -> p (a b)")
                spread = lambda s: s.unsqueeze(2).broadcast_to((P, NCK, HD))
                do(dve.tensor_reduce(mean, o, AX.X, ALU.add))
                do(dve.tensor_scalar(mean, mean, 1.0 / HD, None, ALU.mult))
                do(dve.tensor_tensor(o, o, spread(mean), ALU.subtract))
                do(dve.tensor_tensor(sq, o, o, ALU.mult))
                do(dve.tensor_reduce(var, sq, AX.X, ALU.add))
                do(dve.tensor_scalar(var, var, 1.0 / HD, LNX_EPS, ALU.mult, ALU.add), "rw_var")
                need("rw_std")
                do(dve.reciprocal(var, var))
                do(dve.tensor_tensor(o, o, spread(var), ALU.mult))
                at_w, at_b = VEC["lnx_w"][0], VEC["lnx_b"][0]
                over = lambda at: vec[:, at:at + HD].unsqueeze(1).broadcast_to((P, NCK, HD))
                do(dve.tensor_tensor(o, o, over(at_w), ALU.mult))
                do(dve.tensor_tensor(o, o, over(at_b), ALU.add))
                opad = rw_pad["a"].rearrange("p a n h c -> p (a n h c)").rearrange("p (n h i) -> p n h i", n=NCK, h=2)
                for g in range(2):
                    do(dve.tensor_scalar(opad[:, :, g, :], o, K("hm")[:, g:g + 1], None, ALU.mult), "o_padded")
                for k in range(2):
                    need("rw_o")
                    do(dve.tensor_tensor(rw_pad["bonus"][:, k], rw_pad["bonus"][:, k], ps[4 + k][:], ALU.add))
                    do(dve.tensor_tensor(rw_pad["bonus"][:, k], rw_pad["bonus"][:, k], rw_pad["g"][:, k], ALU.mult))
                    both_parts(g_hi[:, 6 + k, :], g_lo[:, 6 + k, :], rw_pad["bonus"][:, k], "rw_out")
                skip(8)

            def vector_layer(layer):
                gm = lambda k: V("g_mix2", 8 * layer + k)
                norm(gm)
                dve.wait_ge(S("mem_in"), 16 * (layer + 1))
                for k in range(KT):
                    add_square(k, lambda k: work[:, 4, MT * (k % 2):MT * (k % 2) + MT], work[:, 5, 0:MT])
                need("rms_ready")
                do(dve.reciprocal(work[:, 5, MT:], work[:, 5, MT:]))
                for k in range(KT):
                    t = work[:, 4, MT * (k % 2):MT * (k % 2) + MT]
                    do(dve.scalar_tensor_tensor(t, mem_in[:, k, :], V("g_mem2", 8 * layer + k), work[:, 5, MT:], ALU.mult, ALU.mult))
                    both_parts(mn(g_hi, k), mn(g_lo, k), t, "mem_ready")
                q, km, kk = at_m["q"], at_m["km"], at_m["k"]
                do(dve.memset(q[HD:HD + 1, :, :], 1.0))
                for name, dst in (("q", q), ("k", kk)):
                    for i in range(NH // 2):
                        if layer == 0:
                            bank = tile()
                            for g in range(2):
                                do(dve.tensor_scalar(dst[0:HD, 2 * i + g, :], bank[64 * g:64 * g + 64, :],
                                                     HD ** -0.5 if name == "q" else 1.0, None, ALU.mult),
                                   "dve_freed" if g else "dve_step")
                        else:
                            skip(1)
                            if name == "q" and i == 0:
                                dve.wait_ge(S("rope_in"), 16)
                            need("rope_copied")
                            t, sw = rope_t[:, i % 2, :], ps[6 + i % 2]
                            need("rope_swapped")
                            u = work[:, 4, :]
                            do(dve.tensor_tensor(u, sw[:], work[:, 3, :], ALU.mult))
                            do(dve.tensor_tensor(t, t, work[:, 2, :], ALU.mult))
                            for g in range(2):
                                do(dve.tensor_tensor(dst[0:HD, 2 * i + g, :], t[64 * g:64 * g + 64, :], u[64 * g:64 * g + 64, :], ALU.add),
                                   "rope_done" if g else "dve_step")
                for i in range(NH // 2):
                    skip(1)
                    need("v_turned")
                    do(dve.tensor_copy(at_m["v"][:, :, P * i:P * i + P], ps[6 + i % 2][:].rearrange("p (a b) -> p a b", a=QB)), "v_taken")
                if layer == 0:
                    bank = tile()
                    f = lambda i: work[0:NH, i, :]
                    do(dve.tensor_scalar(f(0), bank[0:NH, :], V("b_f")[0:NH], None, ALU.add), "dve_freed")
                    do(dve.tensor_scalar(f(1), f(0), -1.0, None, ALU.mult))
                    do(dve.tensor_tensor(f(1), f(1), f(0), ALU.min), "forget_in_abs")
                    need("forget_log")
                    do(dve.tensor_scalar(f(0), f(0), 0.0, None, ALU.min))
                    do(dve.tensor_tensor(f(0), f(1), f(0), ALU.subtract))
                    do(dve.memset(f(2), 1.0))
                    do(dve.tensor_tensor_scan(f(4), f(2), f(0), 0.0, ALU.mult, ALU.add), "forget_sum")
                for i in range(NMH // 2):
                    bank = tile()
                    for g in range(2):
                        do(dve.tensor_scalar(q[0:HD, NH + 2 * i + g, :], bank[64 * g:64 * g + 64, :], HD ** -0.5, None, ALU.mult),
                           "dve_freed" if g else "dve_step")
                for i in range(NMH // 2):
                    bank = tile()
                    for g in range(2):
                        do(dve.tensor_copy(km[0:HD, 2 * i + g, :], bank[64 * g:64 * g + 64, 0:MT]), "dve_freed" if g else "dve_step")
                for i in range(NMH // 2):
                    skip(1)
                    need("v_turned")
                    do(dve.tensor_copy(at_m["vm"][:, :, P * i:P * i + P],
                                       ps[6 + i % 2][:, 0:MT].rearrange("p (a b) -> p a b", a=2)), "v_taken")
                dve.wait_ge(S("mask_in"), 16 * (layer + 1))
                before = len(UNITS) * layer

                def head_low(head):
                    rows = slice(64 * (head % 2), 64 * (head % 2) + 64)
                    need("head_hi")
                    do(dve.tensor_tensor(g_lo[rows, head // 2, :], ps[6 + head % 2][rows, :], g_hi[rows, head // 2, :].bitcast(F32),
                                         ALU.subtract), "heads")

                for s in range(len(UNITS) + 1):
                    if s < len(UNITS):
                        head, qb, width, at = UNITS[s]
                        if s >= 4:
                            dve.wait_ge(S("probs_turned"), before + s - 3)
                        need("scores")
                        src, pr, top = ps[s % BANKS][:, 0:width], probs[s % 4][:, 0:width], small[:, 33 + s % 4, 0:1]
                        if head < NH and layer == 1:
                            do(dve.tensor_tensor(pr, src, masks[:, at:at + width], ALU.add))
                            src = pr
                        do(dve.tensor_reduce(top, src, AX.X, ALU.max, negate=True), "score_top")
                    if s:
                        u = s - 1
                        head, qb, width, at = UNITS[u]
                        pr, rec = probs[u % 4][:, 0:width], small[:, 33 + u % 4, 1:2]
                        need("exped")
                        do(dve.reciprocal(rec, small[:, 33 + u % 4, 2:3]))
                        do(dve.tensor_scalar(pr, pr, rec, None, ALU.mult), "probs")
                        if qb == QB - 1 and head:
                            head_low(head - 1)
                head_low(NH + NMH - 1)
                last_terms(lambda k: do(dve.tensor_tensor(x[:, k, :], tile()[:], x[:, k, :], ALU.add), "x_done"))
                norm(lambda k: V("g_ffn2", 8 * layer + k))
                for group in range(len(FF2_GROUPS)):
                    vector_ffn2(layer, group)

            def vector_ffn2(layer, group):
                j0 = sum(FF2_GROUPS[:group])
                for j in range(FF2_GROUPS[group]):
                    for side, c in ((0, cv_m["cv"]), (1, cv_m["cg"])):
                        bank = tile()
                        need("conv_first")
                        dst, w = c[:, j % 2, :], lambda tap: V("cw2", (3 * layer + tap) * 44 + 22 * side + j0 + j)
                        do(dve.scalar_tensor_tensor(dst[:, 1:], bank[:, :T - 1], w(1), dst[:, 1:], ALU.mult, ALU.add))
                        do(dve.scalar_tensor_tensor(dst[:, 2:], bank[:, :T - 2], w(0), dst[:, 2:], ALU.mult, ALU.add), "conv_summed")
                    need("conv_gate")
                    t = cv_m["t"][:, j % 2, :]
                    do(dve.tensor_tensor(t, cv_m["cv"][:, j % 2, :], cv_m["sg"][:, j % 2, :], ALU.mult), "conv_used")
                    both_parts(g_hi[:, j, :], g_lo[:, j, :], t, "hidden")
                update = lambda k: do(dve.tensor_tensor(x[:, k, :], tile()[:], x[:, k, :], ALU.add), "x_done")
                if group == len(FF2_GROUPS) - 1:
                    last_terms(update)
                else:
                    for k in range(KT):
                        update(k)

            do(dve.memset(small[:, 38, 0:1], EPS), "eps_set")
            do(dve.memset(small[:, 38, 1:2], LN_EPS), "eps_set")
            dve.wait_ge(S("vec_in"), 16)
            dve.wait_ge(S("con_in"), 16)
            c_act = small[:, 0, :]
            need("silu_c")
            do(dve.tensor_tensor(c_act, V("c", 0, 8), small[:, 1, :], ALU.mult), "c_act")
            dve.wait_ge(S("ada_used"), 16)
            do(dve.tensor_tensor(mod[:, 0:16], PA[:, 0:16], V("ada_b", 0, 16), ALU.add))
            gain1 = small[:, 2, :]
            do(dve.scalar_tensor_tensor(gain1, mod[:, 8:16], 1.0, V("g_mix", 0, 8), ALU.add, ALU.mult))
            for k in range(KT):
                add_square_x(k)
            norm(lambda k: gain1[:, k:k + 1], lambda k: mod[:, k:k + 1])

            bg, cg, z, y = (conv_m[k] for k in ("bg", "cg", "z", "y"))
            for dst in (bg, cg):
                for k in range(2):
                    do(dve.tensor_copy(dst[:, k, :], tile()[:]), "dve_freed")
            for k in range(2):
                do(dve.tensor_tensor(z[:, k, :], tile()[:], cg[:, k, :], ALU.mult), "dve_freed")
            for k in range(2):
                cw = lambda j: V("conv_w", 2 * j + k)
                do(dve.tensor_scalar(y[:, k, :], z[:, k, :], cw(2), None, ALU.mult))
                for lag in (1, 2):
                    do(dve.scalar_tensor_tensor(y[:, k, lag:], z[:, k, :T - lag], cw(2 - lag), y[:, k, lag:], ALU.mult, ALU.add))
                do(dve.tensor_tensor(y[:, k, :], y[:, k, :], bg[:, k, :], ALU.mult))
                both_parts(g_hi[:, k, :], g_lo[:, k, :], y[:, k, :], "conv_y")

            skip(4)
            m = sg_m
            dve.wait_ge(S("sg_in"), 48)
            do(dve.tensor_tensor(m["wsm"], m["ws"], m["caus"].unsqueeze(1).broadcast_to((P, 4, P)), ALU.mult), "sg_w_masked")
            need("sg_mean")
            do(dve.tensor_scalar(m["mu"], PA[:], 1.0 / DM, None, ALU.mult))
            for k in range(2):
                do(dve.tensor_tensor(m["d"][:, k, :], m["z"][:, 2 + k, :], m["mu"], ALU.subtract))
                do(dve.tensor_tensor(m["sq"][:, k, :], m["d"][:, k, :], m["d"][:, k, :], ALU.mult), "sg_square")
            need("sg_std")
            do(dve.reciprocal(m["rstd"], m["std"]))
            for k in range(2):
                do(dve.tensor_tensor(m["d"][:, k, :], m["d"][:, k, :], m["rstd"], ALU.mult))
                do(dve.tensor_scalar(m["vn"][:, k, :], m["d"][:, k, :], V("sg_w", k), V("sg_b", k), ALU.mult, ALU.add), "sg_normed")
            for k in range(2):
                need("sg_mixed")
                mix = m["mix"][:, k, :].rearrange("p (n t) -> p n t", t=P)
                do(dve.tensor_tensor(mix, ps[4 + k][:].rearrange("p (n t) -> p n t", t=P),
                                     m["bs"][:, k, :].unsqueeze(1).broadcast_to((P, QB, P)), ALU.add))
                do(dve.tensor_tensor(m["mix"][:, k, :], m["mix"][:, k, :], m["z"][:, k, :], ALU.mult))
                both_parts(g_hi[:, 2 + k, :], g_lo[:, 2 + k, :], m["mix"][:, k, :], "sg_y")

            count = [0]

            def gated(f, glu_tiles=False):
                first = count[0] < 8
                bank = tile()
                need("gate")
                do(dve.tensor_tensor(merged[:, f, :] if first else product, bank[:], gate_room(count[0]), ALU.mult), "gated")
                count[0] += 1
                if glu_tiles:
                    skip(1)
                    need("glu_gate")
                    do(dve.tensor_tensor(product, product, glu, ALU.mult), "glu_used")
                if not first:
                    do(dve.tensor_tensor(merged[:, f, :], merged[:, f, :], product, ALU.add))

            skip(2)
            m = s5_m
            row = lambda i: small[:, i, :]
            lam, dt, e1, mag, th, kq, sn, sh, cs, ar, ai, den, am, qr, qi, t1, t2, pr, pi, t3 = (row(i) for i in range(3, 23))
            do(dve.tensor_scalar(lam, V("a_re", 0, 8), -1e-4, None, ALU.min))
            need("s5_dt")
            do(dve.tensor_tensor(e1, lam, dt, ALU.mult), "s5_e1")
            do(dve.tensor_tensor(th, V("a_im", 0, 8), dt, ALU.mult))
            do(dve.tensor_scalar(kq, th, 1.0 / (2 * PI), ROUND, ALU.mult, ALU.add))
            do(dve.tensor_scalar(kq, kq, ROUND, None, ALU.subtract))
            for part in TWO_PI:
                do(dve.scalar_tensor_tensor(th, kq, -part, th, ALU.mult, ALU.add))
            do(dve.tensor_scalar(th, th, PI_IN, -PI_IN, ALU.min, ALU.max), "s5_angle")
            need("s5_sines")
            do(dve.tensor_tensor(cs, sh, sh, ALU.mult))
            do(dve.tensor_scalar(cs, cs, -2.0, 1.0, ALU.mult, ALU.add))
            do(dve.tensor_tensor(ar, mag, cs, ALU.mult))
            do(dve.tensor_tensor(ai, mag, sn, ALU.mult))
            do(dve.tensor_tensor(den, lam, lam, ALU.mult))
            do(dve.tensor_tensor(t1, V("a_im", 0, 8), V("a_im", 0, 8), ALU.mult))
            do(dve.tensor_tensor(den, den, t1, ALU.add))
            do(dve.reciprocal(den, den))
            do(dve.tensor_scalar(am, ar, 1.0, None, ALU.subtract))
            do(dve.tensor_tensor(qr, am, lam, ALU.mult))
            do(dve.tensor_tensor(t1, ai, V("a_im", 0, 8), ALU.mult))
            do(dve.tensor_tensor(qr, qr, t1, ALU.add))
            do(dve.tensor_tensor(qr, qr, den, ALU.mult))
            do(dve.tensor_tensor(qi, ai, lam, ALU.mult))
            do(dve.tensor_tensor(t1, am, V("a_im", 0, 8), ALU.mult))
            do(dve.tensor_tensor(qi, qi, t1, ALU.subtract))
            do(dve.tensor_tensor(qi, qi, den, ALU.mult))
            dve.wait_ge(S("s5_in"), 48)
            wide = lambda v: v.unsqueeze(2).broadcast_to((P, S5T, 16))
            bb, b_in, tmp = m["bb"], m["b_in"], m["w"][:, 5, 0:128].rearrange("p (s c) -> p s c", s=S5T)
            for out_part, (qa, qb), op in ((0, (qr, qi), ALU.subtract), (1, (qi, qr), ALU.add)):
                do(dve.tensor_tensor(bb[:, out_part], b_in[:, 0], wide(qa), ALU.mult))
                do(dve.tensor_tensor(tmp, b_in[:, 1], wide(qb), ALU.mult))
                do(dve.tensor_tensor(bb[:, out_part], bb[:, out_part], tmp, op))
            m8 = m["m8"].unsqueeze(3).broadcast_to((P, S5T, 8, 16))
            for part in range(2):
                do(dve.tensor_tensor(m["bpad"][:, part].rearrange("p s (g c) -> p s g c", g=8),
                                     bb[:, part].unsqueeze(2).broadcast_to((P, S5T, 8, 16)), m8, ALU.mult), "s5_bpad")
            need("s5_cT", 4)
            need("s5_bT", 4)
            for s in range(S5T):
                for part, sign in ((0, 1.0), (1, -1.0)):
                    src = ps[6 + part][:, (s // 4) * P:(s // 4) * P + P]
                    do(dve.scalar_tensor_tensor(m["cc"][:, part, s].rearrange("p (g c) -> p g c", g=8),
                                                src.rearrange("p (g c) -> p g c", g=8), sign,
                                                m["m8"][:, s].unsqueeze(2).broadcast_to((P, 8, 16)), ALU.mult, ALU.mult), "s5_cc")
            ct, st = m["ct"], m["st"]
            do(dve.memset(ct[:, :, 0:1], 1.0))
            do(dve.memset(st[:, :, 0:1], 0.0))
            do(dve.tensor_copy(pr, cs))
            do(dve.tensor_copy(pi, sn))
            L = 1
            while L < T:
                cr = pr.unsqueeze(2).broadcast_to((P, S5T, L))
                ci = pi.unsqueeze(2).broadcast_to((P, S5T, L))
                tmp = m["w"].rearrange("p a b -> p (a b)")[:, 0:S5T * L].rearrange("p (s l) -> p s l", s=S5T)
                do(dve.tensor_tensor(ct[:, :, L:2 * L], ct[:, :, 0:L], cr, ALU.mult))
                do(dve.tensor_tensor(tmp, st[:, :, 0:L], ci, ALU.mult))
                do(dve.tensor_tensor(ct[:, :, L:2 * L], ct[:, :, L:2 * L], tmp, ALU.subtract))
                do(dve.tensor_tensor(st[:, :, L:2 * L], st[:, :, 0:L], cr, ALU.mult))
                do(dve.tensor_tensor(tmp, ct[:, :, 0:L], ci, ALU.mult))
                do(dve.tensor_tensor(st[:, :, L:2 * L], st[:, :, L:2 * L], tmp, ALU.add))
                do(dve.tensor_tensor(t1, pr, pr, ALU.mult))
                do(dve.tensor_tensor(t2, pi, pi, ALU.mult))
                do(dve.tensor_tensor(t3, pr, pi, ALU.mult))
                do(dve.tensor_tensor(pr, t1, t2, ALU.subtract))
                do(dve.tensor_scalar(pi, t3, 2.0, None, ALU.mult))
                L *= 2
            w = m["w"]
            for s in range(S5T):
                need("s5_bu", 2)
                re, im = ps[4][:], ps[5][:]
                cos, sin = ct[:, s, :], st[:, s, :]
                do(dve.tensor_tensor(w[:, 0, :], re, cos, ALU.mult))
                do(dve.tensor_tensor(w[:, 1, :], im, sin, ALU.mult))
                do(dve.tensor_tensor(w[:, 2, :], im, cos, ALU.mult))
                do(dve.tensor_tensor(w[:, 3, :], re, sin, ALU.mult), "s5_bu_used")
                do(dve.tensor_tensor(w[:, 0, :], w[:, 0, :], w[:, 1, :], ALU.add))
                do(dve.tensor_tensor(w[:, 1, :], w[:, 2, :], w[:, 3, :], ALU.subtract))
                decay = mag[:, s:s + 1].broadcast_to((P, T))
                do(dve.tensor_tensor_scan(w[:, 2, :], decay, w[:, 0, :], 0.0, ALU.mult, ALU.add))
                do(dve.tensor_tensor_scan(w[:, 3, :], decay, w[:, 1, :], 0.0, ALU.mult, ALU.add))
                if s > 0:
                    need("s5_read")
                do(dve.tensor_tensor(w[:, 0, :], w[:, 2, :], cos, ALU.mult))
                do(dve.tensor_tensor(w[:, 1, :], w[:, 3, :], sin, ALU.mult))
                do(dve.tensor_tensor(w[:, 4, :], w[:, 0, :], w[:, 1, :], ALU.subtract))
                do(dve.tensor_tensor(w[:, 0, :], w[:, 2, :], sin, ALU.mult))
                do(dve.tensor_tensor(w[:, 1, :], w[:, 3, :], cos, ALU.mult))
                do(dve.tensor_tensor(w[:, 5, :], w[:, 0, :], w[:, 1, :], ALU.add), "s5_states")
                skip(2)
                if s % 2:
                    for f in range(4):
                        gated(4 * (s // 2 % 2) + f)
            for k in range(2):
                if k == 0:
                    need("s5_read")
                do(dve.scalar_tensor_tensor(w[:, k, :], m["u"][:, k, :], V("s5_d", k), ps[6 + k][:], ALU.mult, ALU.add), "s5_sum")
                need("s5_gelu")
                both_parts(g_hi[:, 4 + k, :], g_lo[:, 4 + k, :], w[:, 2 + k, :], "s5_y")
            vector_recurrence()

            for f in range(KT):
                gated(f)
                both_parts(h_hi[:, f, :], h_lo[:, f, :], merged[:, f, :], "merged")
            dve.wait_ge(S("ada_used"), 48)
            do(dve.tensor_tensor(mod[:, 16:48], PA[:, 16:48], V("ada_b", 16, 32), ALU.add))
            dve.wait_ge(S("x_in"), 32)
            gain2 = small[:, 23, :]
            do(dve.scalar_tensor_tensor(gain2, mod[:, 32:40], 1.0, V("g_ffn", 0, 8), ALU.add, ALU.mult))
            last_terms(lambda k: do(dve.scalar_tensor_tensor(x[:, k, :], tile()[:], mod[:, 16 + k:17 + k], x[:, k, :], ALU.mult, ALU.add), "x_done"))

            norm(lambda k: gain2[:, k:k + 1], lambda k: mod[:, 24 + k:25 + k])

            def ffn_group(last):
                for j in range(8):
                    skip(1)
                    need("hidden_relu")
                    r, s = ff_m["r"][:, j % 2, :], ff_m["s"][:, j % 2, :]
                    do(dve.tensor_tensor(s, r, r, ALU.mult), "relu_used")
                    both_parts(g_hi[:, j, :], g_lo[:, j, :], s, "hidden")
                update = lambda k: do(dve.scalar_tensor_tensor(x[:, k, :], tile()[:], mod[:, 40 + k:41 + k], x[:, k, :],
                                                               ALU.mult, ALU.add), "x_done")
                if last:
                    last_terms(update)
                else:
                    for k in range(KT):
                        update(k)

            for g in range(FF_GROUPS):
                ffn_group(g == FF_GROUPS - 1)
            need("rms_ready")
            do(dve.reciprocal(work[:, 3, :], work[:, 3, :]))
            last_terms(lambda k: do(dve.scalar_tensor_tensor(x[:, k, :], x[:, k, :], V("g_final1", k), work[:, 3, :], ALU.mult, ALU.mult), "x_done"))
            for layer in range(2):
                vector_layer(layer)
            need("rms_ready")
            do(dve.reciprocal(work[:, 3, :], work[:, 3, :]))
            for k in range(KT):
                do(dve.scalar_tensor_tensor(arena[:, k * T:k * T + T], x[:, k, :], V("g_final", k), work[:, 3, :], ALU.mult, ALU.mult), "result")

        @block.scalar
        def _(act):
            n = Counts()
            n.value["bank"] = 0

            def do(ins, name="act_step"):
                ins.then_inc(S(name), 1)
                act.wait_ge(S(name), n.next(name))

            def need(name, by=1):
                act.wait_ge(S(name), n.next(name, by))

            def tile():
                need("tile")
                n.value["bank"] += 1
                return ps[(n.value["bank"] - 1) % BANKS]

            def skip(tiles):
                n.next("tile", tiles)
                n.value["bank"] += tiles

            def rms(tiles, src, sq, bank, dst, width, ready=None):
                for k in range(tiles):
                    if ready is not None:
                        act.wait_ge(S("x_done"), ready + k + 1)
                    done = n.value.get("square", 0)
                    if done >= 2:
                        act.wait_ge(S("square_used"), done - 1)
                    do(act.activation(sq(k), src(k), ACT.Square), "square")
                need("squares_total")
                do(act.activation(dst, bank[:, 0:width], ACT.Sqrt, bias=small[:, 38, 0:1], scale=1.0 / D), "rms_ready")

            def rms_x(ready=None):
                rms(KT, lambda k: x[:, k, :], lambda k: work[:, k % 2, :], PB, work[:, 3, :], T, ready)

            def values(i, width, layer):
                bank = tile()
                if i >= 2:
                    act.wait_ge(S("v_turned"), 8 * layer + i - 1)
                elif layer:
                    act.wait_ge(S("rope_done"), 12)
                do(act.activation(rope_t[:, i % 2, 0:width], bank[:, 0:width], ACT.Copy), "v_copied")

            act.wait_ge(S("vec_in"), 16)
            do(act.activation(small[:, 1, :], V("c", 0, 8), ACT.Sigmoid), "silu_c")
            act.wait_ge(S("eps_set"), 2)
            act.wait_ge(S("x_in"), 16)
            rms_x()
            skip(6)
            m = sg_m
            for k in range(4):
                do(act.activation(m["z"][:, k, :], tile()[:], ACT.Gelu_apprx_tanh), "act_freed")
            need("sg_var")
            do(act.activation(m["std"], PB[:], ACT.Sqrt, bias=small[:, 38, 1:2], scale=1.0 / DM), "sg_std")
            for k in range(2):
                need("sg_turned")
                do(act.activation(m["vt"][:, k].rearrange("p n c -> p (n c)"), ps[6 + k][:], ACT.Copy), "sg_vt")
            m = s5_m
            row = lambda i: small[:, i, :]
            lam, dt, e1, mag, th, kq, sn, sh, cs = (row(i) for i in range(3, 12))
            for k in range(2):
                do(act.activation(m["u"][:, k, :], tile()[:], ACT.Copy), "act_freed")
            do(act.activation(dt, V("log_dt", 0, 8), ACT.Exp), "s5_dt")
            need("s5_e1")
            do(act.activation(mag, e1, ACT.Exp))
            need("s5_angle")
            do(act.activation(sn, th, ACT.Sin))
            do(act.activation(sh, th, ACT.Sin, scale=0.5), "s5_sines")
            for part in range(2):
                need("s5_bT", 2)
                for half in range(2):
                    do(act.activation(m["bt"][:, part, 4 * half:4 * half + 4].rearrange("p s c -> p (s c)"), ps[4 + half][:], ACT.Copy),
                       "s5_bt")
            count = [0, 0]

            def gate():
                bank = tile()
                if 4 <= count[0] < 28:
                    act.wait_ge(S("gated"), count[0] - 3)
                do(act.activation(gate_room(count[0]), bank[:], ACT.Sigmoid), "gate")
                count[0] += 1

            def glu_gate():
                skip(1)
                bank = tile()
                if count[1]:
                    act.wait_ge(S("glu_used"), count[1])
                do(act.activation(glu, bank[:], ACT.Sigmoid), "glu_gate")
                count[1] += 1

            for s in range(S5T):
                gate()
                gate()
                if s % 2:
                    skip(4)
            for k in range(2):
                need("s5_sum")
                do(act.activation(m["w"][:, 2 + k, :], m["w"][:, k, :], ACT.Gelu_apprx_tanh), "s5_gelu")
            v = rw_in
            act.wait_ge(S("lora_in"), 16)
            skip(7)
            need("rw_shifted")
            do(act.activation(v["m"][0:32, :], v["m"][0:32, :], ACT.Tanh), "rw_m")
            do(act.activation(v["m"][64:128, :], v["m"][64:128, :], ACT.Sigmoid), "rw_m")
            for k in range(2):
                need("rw_z")
                do(act.activation(v["lw"][:, k], ps[4 + k][:], ACT.Sigmoid, bias=V("w0", k)), "rw_decay")
            for k in range(2):
                need("rw_az")
                do(act.activation(v["a"][:, k], ps[6 + k][:], ACT.Sigmoid, bias=V("a0", k)), "rw_a")
            for k in range(2):
                need("rw_gz")
                do(act.activation(rw_pad["g"][:, k], ps[4 + k][:], ACT.Copy), "rw_g")
            for f in range(4):
                gate()
            for f in range(4):
                glu_gate()
            for k in range(2):
                need("rw_kk_floor")
                do(act.activation(v["e"][:, k], v["e"][:, k], ACT.Sqrt), "rw_kk_norm")
            for f in range(4):
                gate()
            for f in range(4):
                glu_gate()
            need("rw_exp_go")
            for k in range(2):
                if k:
                    act.wait_ge(S("rw_padded"), 2)
                do(act.activation(v["e"][:, 0], v["cum"][:, k], ACT.Exp), "rw_exp")
                need("rw_before")
                do(act.activation(v["e"][:, 1], v["lw"][:, k], ACT.Exp), "rw_exp")
                do(act.activation(v["e"][:, 0], v["cum"][:, k], ACT.Exp, scale=-1.0), "rw_exp")
            act.wait_ge(S("bd_used"), 18)
            for f in range(4):
                gate()

            def outputs(c):
                need("rec_o")
                for p in range(2):
                    rows = slice(64 * p, 64 * p + 64)
                    at = P + HD
                    do(act.activation(rw_sol["o"][rows, c, :], ps[6 + p][rows, at:at + HD], ACT.Copy), "rec_o_copied")

            for c in range(NCK):
                need("rec_y", 2)
                do(act.activation(chain_y[64:128, 0, :], ps[1][64:128, 0:HD], ACT.Copy), "rec_y_copied1")
                need("rec_sa", 2)
                do(act.activation(chain_y[64:128, 1, :], ps[7][64:128, 0:HD], ACT.Copy), "rec_sa_copied1")
                outputs(c)
            need("rw_var")
            do(act.activation(small[:, 31:33, :].rearrange("p a b -> p (a b)"), small[:, 31:33, :].rearrange("p a b -> p (a b)"),
                              ACT.Sqrt), "rw_std")
            act.wait_ge(S("rw_out"), 2)
            for f in range(4):
                gate()
            skip(8)
            skip(8)
            rms_x(0)
            for g in range(FF_GROUPS):
                for j in range(8):
                    bank = tile()
                    if 8 * g + j >= 2:
                        act.wait_ge(S("relu_used"), 8 * g + j - 1)
                    do(act.activation(ff_m["r"][:, j % 2, :], bank[:], ACT.Relu), "hidden_relu")
                skip(8)
            rms_x(8 * FF_GROUPS)
            for layer in range(2):
                rms_x(X_DONE[layer] - 8)
                act.wait_ge(S("mem_in"), 16 * (layer + 1))
                act.wait_ge(S("h_ready"), (16, 16 + 16)[layer] + 8)
                rms(KT, lambda k: mem_in[:, k, :], lambda k: work[:, 4, MT * (k % 2):MT * (k % 2) + MT], PB, work[:, 5, MT:], MT)
                if layer == 0:
                    skip(12)
                else:
                    for i in range(12):
                        bank = tile()
                        if i >= 2:
                            act.wait_ge(S("rope_done"), i - 1)
                        do(act.activation(rope_t[:, i % 2, :], bank[:], ACT.Copy, scale=HD ** -0.5 if i < 6 else 1.0), "rope_copied")
                for i in range(6):
                    values(i, T, layer)
                if layer == 0:
                    skip(1)
                    need("forget_in_abs")
                    f = lambda i: work[0:NH, i, :]
                    do(act.activation(f(3), f(1), ACT.Exp))
                    do(act.activation(f(1), f(3), ACT.Ln, bias=1.0), "forget_log")
                skip(4)
                for i in range(2):
                    values(6 + i, MT, layer)
                def head_high(head):
                    rows = slice(64 * (head % 2), 64 * (head % 2) + 64)
                    do(act.activation(g_hi[rows, head // 2, :], ps[6 + head % 2][rows, :], ACT.Copy), "head_hi")

                for s in range(len(UNITS) + 2):
                    if s < len(UNITS):
                        head, qb, width, at = UNITS[s]
                        pr, small_u = probs[s % 4][:, 0:width], small[:, 33 + s % 4, :]
                        need("score_top")
                        src = pr if head < NH and layer == 1 else ps[s % BANKS][:, 0:width]
                        do(act.activation(pr, src, ACT.Exp, bias=small_u[:, 0:1], accum_out=small_u[:, 2:3]), "exped")
                    if s >= 2:
                        u = s - 2
                        head, qb, width, at = UNITS[u]
                        if qb == 0 and head:
                            need("head_out")
                        need("probs_turned")
                        blocks = width // P
                        do(act.activation(at_m["pt"][:, 0:blocks, P * qb:P * qb + P],
                                          ps[4 + u % 2][:, 0:width].rearrange("p (a b) -> p a b", a=blocks), ACT.Copy), "probs_kept")
                        if qb == 0 and head:
                            head_high(head - 1)
                need("head_out")
                head_high(NH + NMH - 1)
                skip(8)
                rms_x(X_DONE[layer])
                for group, width in enumerate(FF2_GROUPS):
                    j0 = sum(FF2_GROUPS[:group])
                    for j in range(width):
                        for side, c in ((0, cv_m["cv"]), (1, cv_m["cg"])):
                            bank = tile()
                            done = 22 * layer + j0 + j
                            if done >= 2:
                                act.wait_ge(S("conv_used"), done - 1)
                            at = (3 * layer + 2) * 44 + 22 * side + j0 + j
                            do(act.activation(c[:, j % 2, :], bank[:], ACT.Identity, scale=V("cw2", at),
                                              bias=V("cb2", 44 * layer + 22 * side + j0 + j)), "conv_first")
                        need("conv_summed", 2)
                        do(act.activation(cv_m["sg"][:, j % 2, :], cv_m["cg"][:, j % 2, :], ACT.Silu), "conv_gate")
                    skip(8)
            rms_x(X_DONE[1] + 8 + 16)

        @block.tensor
        def _(pe):
            n = Counts()
            piece, t = [0], [0]
            squares = [0]
            freed = []

            def need(name, by=1):
                pe.wait_ge(S(name), n.next(name, by))

            def open_piece():
                pe.wait_ge(S("w_split"), piece[0] + 1)
                slot = piece[0] % SPLIT
                piece[0] += 1
                return slot

            def product(slot, blocks, hi, lo, owner, width=T, first_block=0, ready=None, first=True, close=True):
                if len(freed) >= BANKS:
                    pe.wait_ge(S(freed[-BANKS][0]), freed[-BANKS][1])
                bank = ps[t[0] % BANKS][:, 0:width]
                for k in range(blocks):
                    if ready is not None:
                        ready(k)
                    cols = slice(P * (first_block + k), P * (first_block + k) + P)
                    for i, (w, a) in enumerate(((w_hi, hi), (w_hi, lo), (w_lo, hi))):
                        mm = pe.matmul(bank, w[:, slot, cols], a(k), start=(k == 0 and i == 0), stop=(k == blocks - 1 and i == 2))
                        if first and k == 0 and i == 0 and piece[0] > 1:
                            mm.then_inc(S("w_used"), 1)
                mm.then_inc(S("tile"), 1)
                t[0] += 1
                freed.append((owner, n.next(owner)))

            of = lambda pair: (lambda k: pair[:, k, :])
            h = (of(h_hi), of(h_lo))

            def project(tiles, owner, operand=h, width=T, blocks=8, ready=None):
                for i in range(tiles):
                    slot = open_piece()
                    product(slot, blocks, *operand, owner if isinstance(owner, str) else owner[i], width,
                            ready=ready if i == 0 else None)

            def h_tile(k):
                need("h_ready")

            def modulation(a, b, bank):
                for q in range(a, b):
                    pe.wait_ge(S(f"ada_in{q % ADA}"), 16 * (q // ADA + 1))
                    for k in range(8):
                        mm = pe.matmul(bank[:, q:q + 1], ada_m["ada"][:, q % ADA, P * k:P * k + P], small[:, 0, k:k + 1],
                                       start=(k == 0), stop=(k == 7))
                    mm.then_inc(S("ada_used"), 1)

            def total_squares(acc, width=T):
                squares[0] += KT
                pe.wait_ge(S("square_used"), squares[0])
                pe.matmul(PB[:, 0:width], K("ones"), acc, start=True, stop=True).then_inc(S("squares_total"), 1)

            def swap(i):
                pe.wait_ge(S("rope_copied"), i + 1)
                if i >= 2:
                    pe.wait_ge(S("rope_done"), i - 1)
                pe.matmul(ps[6 + i % 2][:], K("rot"), rope_t[:, i % 2, :], start=True, stop=True).then_inc(S("rope_swapped"), 1)

            def turn_values(i, width, layer):
                pe.wait_ge(S("v_copied"), 8 * layer + i + 1)
                if i >= 2:
                    pe.wait_ge(S("v_taken"), 8 * layer + i - 1)
                elif layer:
                    pe.wait_ge(S("rope_done"), 12)
                for b in range(width // P):
                    mm = pe.transpose(ps[6 + i % 2][:, P * b:P * b + P], rope_t[:, i % 2, P * b:P * b + P], K("ident"))
                mm.then_inc(S("v_turned"), 1)

            def attention(layer):
                before, heads = len(UNITS) * layer, (NH + NMH) * layer
                pe.wait_ge(S("v_taken"), 8 * (layer + 1))
                if layer == 0:
                    pe.wait_ge(S("forget_in"), 16)

                def scores(u):
                    head, qb, width, _ = UNITS[u]
                    if u >= BANKS:
                        pe.wait_ge(S("exped"), before + u - BANKS + 1)
                    mixing = head < NH
                    rows = HD + 1 if layer == 0 and mixing else HD
                    keys = at_m["k"][0:rows, head, 0:width] if mixing else at_m["km"][0:rows, head - NH, :]
                    masked = layer == 0 and mixing
                    mm = pe.matmul(ps[u % BANKS][:, 0:width], at_m["q"][0:rows, head, P * qb:P * qb + P], keys,
                                   start=True, stop=not masked)
                    if masked:
                        mm = pe.matmul(ps[u % BANKS][:, P * qb:P * qb + P], K("ident"), masks[:, 0:P], start=False, stop=True)
                    mm.then_inc(S("scores"), 1)

                def head_output(head):
                    pe.wait_ge(S("probs_kept"), before + QB * head + QB)
                    if head >= 2:
                        pe.wait_ge(S("heads"), heads + head - 1)
                    out_rows = slice(64 * (head % 2), 64 * (head % 2) + 64)
                    blocks = QB if head < NH else MT // P
                    for b in range(blocks):
                        q0 = P * b if head < NH else 0
                        values = at_m["v"][:, b, HD * head:HD * head + HD] if head < NH else \
                            at_m["vm"][:, b, HD * (head - NH):HD * (head - NH) + HD]
                        mm = pe.matmul(ps[6 + head % 2][out_rows, q0:T], values, at_m["pt"][:, b, q0:T],
                                       start=(b == 0), stop=(b == blocks - 1))
                    mm.then_inc(S("head_out"), 1)

                pe.wait_ge(S("mask_in"), 16 * (layer + 1))
                scores(0)
                scores(1)
                for u, (head, qb, width, _) in enumerate(UNITS):
                    if u + 2 < len(UNITS):
                        scores(u + 2)
                    pe.wait_ge(S("probs"), before + u + 1)
                    if u >= 2:
                        pe.wait_ge(S("probs_kept"), before + u - 1)
                    for b in range(width // P):
                        mm = pe.transpose(ps[4 + u % 2][:, P * b:P * b + P], probs[u % 4][:, P * b:P * b + P], K("ident"))
                    mm.then_inc(S("probs_turned"), 1)
                    if qb == 0 and head:
                        head_output(head - 1)
                head_output(NH + NMH - 1)

            pe.wait_ge(S("con_in"), 16)
            need("c_act")
            modulation(0, 16, PA)
            total_squares(work[:, 2, :])
            project(10, ["dve_freed"] * 6 + ["act_freed"] * 4, ready=h_tile)
            project(2, "act_freed")

            m = sg_m
            pe.wait_ge(S("act_freed"), 4)
            for k in range(2):
                mm = pe.matmul(PA[:], K("ones"), m["z"][:, 2 + k, :], start=(k == 0), stop=(k == 1))
            mm.then_inc(S("sg_mean"), 1)
            for k in range(2):
                need("sg_square")
                mm = pe.matmul(PB[:], K("ones"), m["sq"][:, k, :], start=(k == 0), stop=(k == 1))
            mm.then_inc(S("sg_var"), 1)
            for k in range(2):
                need("sg_normed")
                for b in range(QB):
                    mm = pe.transpose(ps[6 + k][:, P * b:P * b + P], m["vn"][:, k, P * b:P * b + P], K("ident"))
                mm.then_inc(S("sg_turned"), 1)
            need("sg_w_masked")
            for k in range(2):
                need("sg_vt")
                for g in range(2):
                    for b in range(QB):
                        mm = pe.matmul(ps[4 + k][64 * g:64 * g + 64, P * b:P * b + P], m["vt"][:, k, b, 64 * g:64 * g + 64],
                                       m["wsm"][:, 2 * k + g, :], start=True, stop=True)
                mm.then_inc(S("sg_mixed"), 1)

            m = s5_m
            pe.wait_ge(S("s5_in"), 48)
            for k in range(2):
                for part in range(2):
                    pe.transpose(ps[6 + part][:, P * k:P * k + P], m["c_in"][:, part, k, :], K("ident")).then_inc(S("s5_cT"), 1)
            for part in range(2):
                need("s5_bpad")
                if part == 1:
                    pe.wait_ge(S("s5_bt"), 2)
                pe.wait_ge(S("sg_y"), 2)
                for half in range(2):
                    for s in range(4):
                        mm = pe.transpose(ps[4 + half][:, P * s:P * s + P], m["bpad"][:, part, 4 * half + s, :], K("ident"))
                    mm.then_inc(S("s5_bT"), 1)
            pe.wait_ge(S("s5_bt"), 4)
            pe.wait_ge(S("act_freed"), 6)
            pe.wait_ge(S("s5_cc"), 16)
            def inputs(s):
                for part in range(2):
                    pe.matmul(ps[4 + part][:], m["bt"][:, part, s, :], m["u"][:, s // 4, :], start=True, stop=True).then_inc(S("s5_bu"), 1)

            def branch_out(b, tiles, glu_tiles=False):
                y = (lambda k: g_hi[:, 2 * b + k, :], lambda k: g_lo[:, 2 * b + k, :])
                for q in range(tiles // 4):
                    slot = open_piece()
                    for i in range(4):
                        product(slot, 2, *y, "glu_gate" if glu_tiles and i % 2 else "gated", first_block=2 * i, first=(i == 0))

            inputs(0)
            for s in range(S5T):
                project(2, "gate")
                if s < S5T - 1:
                    need("s5_bu_used")
                    inputs(s + 1)
                if s % 2:
                    pe.wait_ge(S("conv_y" if s < 4 else "sg_y"), 2)
                    branch_out(s // 4, 4)
                need("s5_states")
                for part in range(2):
                    mm = pe.matmul(ps[6 + s // 4][:], m["cc"][:, part, s, :], m["w"][:, 4 + part, :],
                                   start=(s % 4 == 0 and part == 0), stop=(s % 4 == 3 and part == 1))
                mm.then_inc(S("s5_read"), 1)

            project(7, "dve_freed")
            v, bd = rw_in, rw_bd
            project(4, "gate")
            pe.wait_ge(S("lora_in"), 16)
            pe.wait_ge(S("rw_m"), 2)
            for rows, names, banks in ((slice(0, 32), "rw_z", (4, 5)), (slice(32, 64), "rw_az", (6, 7)), (slice(64, 128), "rw_gz", (4, 5))):
                for k in range(2):
                    if names == "rw_gz":
                        pe.wait_ge(S("rw_decay"), k + 1)
                    elif names == "rw_z":
                        pe.wait_ge(S("s5_sum"), 2)
                    pe.matmul(ps[banks[k]][:], lora[rows, P * k:P * k + P], v["m"][rows, :], start=True, stop=True).then_inc(S(names), 1)
            pe.wait_ge(S("s5_y"), 2)
            branch_out(2, 8, glu_tiles=True)
            for k in range(2):
                need("rw_kk_square")
                pe.wait_ge(S("rw_g"), k + 1)
                pe.matmul(ps[4 + k][:], K("hsum"), v["e"][:, k], start=True, stop=True).then_inc(S("rw_kk_sum"), 1)
            project(4, "gate")
            for k in range(2):
                need("rw_rk")
                pe.wait_ge(S("rw_a"), k + 1)
                pe.matmul(ps[6 + k][:], K("hsum"), v["e"][:, k], start=True, stop=True).then_inc(S("rw_rk_sum"), 1)
            branch_out(2, 8, glu_tiles=True)
            pe.wait_ge(S("rw_padded"), 4)
            banks = [0]

            def blocks(lhs, rhs, width, per):
                for q in range(NCK // per):
                    i = banks[0]
                    if i >= 4:
                        pe.wait_ge(S("bd_used"), i - 3)
                    banks[0] += 1
                    for c in range(per):
                        for p in range(2):
                            mm = pe.matmul(ps[4 + i % 4][64 * p:64 * p + 64, width * c:width * c + width], lhs(p, per * q + c),
                                           rhs(p, per * q + c), start=True, stop=True)
                    mm.then_inc(S("bd"), 1)

            pad = lambda name: (lambda p, c: rw_pad[name][:, p, c].rearrange("a h t -> a (h t)"))
            blocks(pad("a"), pad("b"), 64, 8)
            blocks(pad("k"), pad("a"), 64, 8)
            blocks(pad("k"), pad("r"), 64, 8)
            blocks(pad("b"), pad("r"), 64, 8)
            blocks(pad("k"), lambda p, c: K("ident"), P, 4)
            pe.wait_ge(S("v_padded"), 4)
            blocks(pad("k"), lambda p, c: K("stack"), 64, 8)
            blocks(pad("b"), lambda p, c: K("ident"), P, 4)
            project(4, "gate")
            pe.wait_ge(S("tT_in"), 16 * 8)
            pe.wait_ge(S("bd_used"), 18)
            pe.wait_ge(S("gate"), 28)
            need("state_set")
            rows = [slice(0, 64), slice(64, 128)]
            at_s, at_o = slice(P, P + HD), slice(P + HD, P + 2 * HD)
            for c in range(NCK):
                now = c % 2
                for p in range(2):
                    pe.matmul(ps[p][rows[p], 0:HD], bd["akT"][rows[p], c, :], bd["vt"][rows[p], c, :], start=True, stop=False)
                for p in range(2):
                    if c:
                        need("state_set")
                    pe.matmul(ps[p][rows[p], 0:HD], pad("a")(p, c), state[:, now, p, :], start=False, stop=True).then_inc(S("rec_y"), 1)
                if c:
                    need("rec_o_copied", 2)
                for p in range(2):
                    need("rec_y_copied1" if p else "rec_y_copied")
                    pe.matmul(ps[6 + p][rows[p], 0:HD], bd["tT"][rows[p], c, :], chain_y[rows[p], 0, :],
                              start=True, stop=True).then_inc(S("rec_sa"), 1)
                for p in range(2):
                    pe.matmul(ps[4 + p][:, at_s], bd["kt"][rows[p], c, :], bd["vt"][rows[p], c, :], start=True, stop=False)
                for p in range(2):
                    need("rec_sa_copied1" if p else "rec_sa_copied")
                    pe.matmul(ps[4 + p][:, at_s], rw_bt[rows[p], c, :], chain_y[rows[p], 1, :], start=False, stop=True).then_inc(S("rec_state"), 1)
                for p in range(2):
                    pe.matmul(ps[6 + p][rows[p], at_o], pad("r")(p, c), state[:, now, p, :], start=True, stop=False)
                    pe.matmul(ps[6 + p][rows[p], at_o], bd["rbT"][rows[p], c, :], chain_y[rows[p], 1, :], start=False, stop=False)
                    mm = pe.matmul(ps[6 + p][rows[p], at_o], bd["rkT"][rows[p], c, :], bd["vt"][rows[p], c, :], start=False, stop=True)
                mm.then_inc(S("rec_o"), 1)
            pe.wait_ge(S("o_padded"), 2)
            opad = rw_pad["a"].rearrange("p a n h c -> p (a n h c)").rearrange("p (n x) -> p n x", n=NCK)
            for p in range(2):
                rows = slice(64 * p, 64 * p + 64)
                for c in range(NCK):
                    mm = pe.matmul(ps[4 + p][:, C * c:C * c + C], opad[rows, c, :], K("sum32")[rows, :], start=True, stop=True)
                mm.then_inc(S("rw_o"), 1)

            pe.wait_ge(S("rw_out"), 2)
            for i in range(4):
                project(1, "gate")
                if i % 2:
                    modulation(16 + 8 * (i // 2), 24 + 8 * (i // 2), PA)
            for half in range(2):
                branch_out(3, 4)
            modulation(32, 48, PA)
            project(8, "x_done", ready=lambda k: need("merged"))
            g = (of(g_hi), of(g_lo))
            hidden = lambda k: need("hidden")
            total_squares(work[:, 2, :])
            for group in range(FF_GROUPS):
                project(8, "hidden_relu", ready=h_tile if group == 0 else None)
                project(8, "x_done", operand=g, ready=hidden)
            total_squares(work[:, 2, :])
            n.next("x_done", 8)
            for layer in range(2):
                total_squares(work[:, 2, :])
                total_squares(work[:, 5, 0:MT], MT)
                if layer == 0:
                    project(12, "dve_freed", ready=h_tile)
                else:
                    for i in range(12):
                        project(1, "rope_copied", ready=h_tile if i == 0 else None)
                        if i:
                            swap(i - 1)
                    swap(11)
                for i in range(6):
                    project(1, "v_copied")
                    if i:
                        turn_values(i - 1, T, layer)
                turn_values(5, T, layer)
                project(3 if layer == 0 else 2, "dve_freed")
                mem = (lambda k: mn(g_hi, k), lambda k: mn(g_lo, k))
                project(2, "dve_freed", operand=mem, width=MT, ready=lambda k: need("mem_ready"))
                for i in range(2):
                    project(1, "v_copied", operand=mem, width=MT)
                    if i:
                        turn_values(6, MT, layer)
                turn_values(7, MT, layer)
                attention(layer)
                pe.wait_ge(S("heads"), 16 * (layer + 1))
                project(8, "x_done", operand=g)
                total_squares(work[:, 2, :])
                for group, pairs in enumerate(FF2_GROUPS):
                    project(2 * pairs, "conv_summed", ready=h_tile if group == 0 else None)
                    project(8, "x_done", operand=g, blocks=pairs, ready=hidden)
            total_squares(work[:, 2, :])


def pieces_of(w):
    k = w.shape[0] // P
    out = np.zeros((w.shape[1] // P, P, D), w.dtype)
    out[:, :, :k * P] = w.reshape(k, P, -1, P).transpose(2, 1, 0, 3).reshape(-1, P, k * P)
    return out


def small_pieces_of(w):
    return w.reshape(2, P, -1, 4, P).transpose(2, 1, 3, 0, 4).reshape(-1, P, D)


def columns(v):
    return v.reshape(-1, P).T


def constants():
    i, j = np.arange(P)[:, None], np.arange(64)[None, :]
    same = (i // C % 2) == (j // C)
    rot = np.zeros((P, P))
    for k in range(P):
        if k % HD < HD // 2:
            rot[k, k + HD // 2] = 1
        else:
            rot[k, k - HD // 2] = -1
    con = {"ident": np.eye(P), "ones": np.ones((P, P)), "hsum": np.kron(np.eye(2), np.ones((HD, HD))),
           "lt": same & (j % C < i % C), "gt": same & (j % C > i % C), "ge": same & (j % C >= i % C),
           "stack": (i % HD) == j, "sum32": (i % C) == np.arange(C)[None, :], "hm": (i // C % 2) == np.arange(2)[None, :],
           "rot": rot}
    con = np.concatenate([con[name] for name in CON], axis=1).astype(np.float32)
    c = np.arange(C // 2)[None, :, None] + (C // 2) * (np.arange(P)[:, None, None] // 64)
    eye = (c == np.arange(C)[None, None, :]).reshape(P, -1).astype(np.float32)
    q, k = np.arange(T)[:, None], np.arange(T)[None, :]
    fox = np.where(k <= q, 0.0, NEG)
    d = q - k
    count = ((d >= 0) & (d <= P)).astype(int) + ((d >= 0) & (d % 4 == 0)) + ((d >= 0) & (d % 16 == 0))
    dil = np.where(count > 0, np.log(np.maximum(count, 1)), NEG)
    by_block = lambda m: np.concatenate([m[b * P:b * P + P, 0:(b + 1) * P] for b in range(QB)], axis=1).astype(np.float32)
    inv = (np.float32(1.0) / np.float32(10000.0) ** (np.arange(0, HD, 2, dtype=np.float32) / np.float32(HD))).astype(np.float32)
    ang = np.arange(T, dtype=np.float32)[:, None] * inv[None, :]
    rope = np.stack([np.tile(np.cos(ang).T, (4, 1)), np.tile(np.sin(ang).T, (4, 1))], axis=1).astype(np.float32)
    m8 = np.zeros((P, S5T, 8), np.float32)
    for s in range(S5T):
        for g in range(2):
            m8[64 * g:64 * g + 64, s, (2 * s + g) % 8] = 1
    caus = (np.arange(P)[:, None] <= np.arange(P)[None, :]).astype(np.float32)
    return dict(con=con, eye=eye, mask_fox=by_block(fox), mask_dil=by_block(dil), rope=rope, s5_m8=m8, caus=caus)


def layout(i):
    i = {k: np.asarray(v) for k, v in i.items()}
    first = {k: v[0] for k, v in i.items() if not k.endswith("_2") and v.ndim > 1 and v.shape[0] == 1}
    w_in = first["w_in"]
    a_cols = 3 * DM + 128
    off_c, off_d, off_g = a_cols + 2 * DM, a_cols + 5 * DM, a_cols + 6 * DM
    glu = first["s5_glu_w"].reshape(DM, 2, KT, P).transpose(0, 2, 1, 3).reshape(DM, 2 * D)
    gates = pieces_of(w_in[:, off_g:])
    sources = {"conv_in": pieces_of(w_in[:, off_c:off_d]), "sg_in": pieces_of(w_in[:, a_cols:off_c]),
               "s5_in": pieces_of(w_in[:, off_d:off_g]), "rwkv_in": pieces_of(w_in[:, :a_cols]),
               "rwkv_gate": gates[0:8], "sg_gate": gates[8:16], "conv_gate": gates[16:24], "s5_gate": gates[24:32],
               "rwkv_out": small_pieces_of(first["rwkv_out"]), "sg_out": small_pieces_of(first["sg_out"]),
               "conv_out": small_pieces_of(first["conv_out"]), "s5_out": small_pieces_of(glu)}
    stream = []
    for what, n in mixer_pieces():
        stream.append(sources[what][:n])
        sources[what] = sources[what][n:]
    stream.append(pieces_of(first["w_o"]))
    for g in range(FF_GROUPS):
        cut = slice(g * D, g * D + D)
        stream += [pieces_of(first["ffn_w1"][:, cut]), pieces_of(first["ffn_w2"][cut])]
    dmix = NH * HD
    for layer, w in ((0, i["w_in_fox_2"][0]), (1, i["w_in_dil_2"][0])):
        if layer == 0:
            forget = np.zeros((D, P), w.dtype)
            forget[:, :NH] = w[:, 3 * dmix:3 * dmix + NH]
            w = np.concatenate([w[:, :3 * dmix], forget, w[:, 3 * dmix + NH:]], axis=1)
        up, down = i["w_up_2"][layer], i["w_down_2"][layer]
        stream += [pieces_of(w), pieces_of(i["w_mem_kv_2"][layer]), pieces_of(i["w_out_2"][layer])]
        pairs = pieces_of(up.reshape(D, 2, FF2, P).transpose(0, 2, 1, 3).reshape(D, -1))
        at = 0
        for n in FF2_GROUPS:
            stream += [pairs[2 * at:2 * at + 2 * n], pieces_of(down[at * P:(at + n) * P])]
            at += n
    f = first
    vec = {"c": columns(i["c"][0]), "ada_b": columns(f["ada_b"]), "g_mix": columns(f["norm_mix_g"]), "mu": columns(f["rwkv_mu"]),
           "w0": columns(f["rwkv_w0"]), "a0": columns(f["rwkv_a0"]), "kk": columns(f["rwkv_kk"]), "ka": columns(f["rwkv_ka"]),
           "rk": columns(f["rwkv_rk"].reshape(-1)), "sg_w": columns(f["sg_ln_w"]), "sg_b": columns(f["sg_ln_b"]),
           "conv_w": columns(f["conv_w"].reshape(-1)), "s5_d": columns(f["s5_d"]),
           "a_re": columns(f["s5_a_re"].reshape(-1)), "a_im": columns(f["s5_a_im"].reshape(-1)),
           "log_dt": columns(np.repeat(f["s5_log_dt"], 64)), "g_ffn": columns(f["norm_ffn_g"]), "g_final1": columns(i["final_g"]),
           "g_mix2": columns(i["norm_mix_2"].reshape(-1)), "g_mem2": columns(i["norm_mem_2"].reshape(-1)),
           "g_ffn2": columns(i["norm_ffn_2"].reshape(-1)),
           "b_f": np.concatenate([i["b_forget_2"][0], np.zeros(P - NH, np.float32)])[:, None],
           "cw2": columns(i["conv_w_2"].reshape(-1)), "cb2": columns(i["conv_b_2"].reshape(-1)),
           "g_final": columns(i["norm_final_2"]),
           "lnx_w": np.repeat(f["rwkv_lnx_w"].reshape(H_A, HD), C, axis=0), "lnx_b": np.repeat(f["rwkv_lnx_b"].reshape(H_A, HD), C, axis=0)}
    b = np.stack([f["s5_b_re"], f["s5_b_im"]])
    c = np.stack([f["s5_c_re"], f["s5_c_im"]])
    arrays = dict(
        w=np.concatenate(stream), ada=pieces_of(f["ada_w"]), vec=np.concatenate([vec[name] for name in VEC], axis=1),
        xT=i["x"][0].reshape(T, KT, P).transpose(2, 1, 0), memT=i["mem_2"][0].reshape(MT, KT, P).transpose(2, 1, 0),
        sg_ws=f["sg_ws"].transpose(2, 0, 1), sg_bs=np.repeat(f["sg_bs"].reshape(2, 2, 1, P), 64, axis=2).transpose(1, 2, 0, 3).reshape(P, 2, P),
        s5_b=b.reshape(2, S5T, P, 16).transpose(2, 0, 1, 3),
        s5_c=np.concatenate([c, c], axis=3).reshape(2, 2, P, P).transpose(2, 0, 1, 3),
        lora=np.concatenate([f["rwkv_w2"], f["rwkv_a2"], f["rwkv_g2"]]), **constants())
    return {k: np.ascontiguousarray(v) for k, v in arrays.items()}


def kernel(**inputs):
    import concourse.bacc as bacc
    from concourse.bass_utils import run_bass_kernel_spmd

    nc = bacc.Bacc("TRN2", target_bir_lowering=False, num_devices=1)
    arrays = layout(inputs)
    aps = {k: nc.dram_tensor(f"in_{k}", v.shape, mybir.dt.from_np(v.dtype), kind="ExternalInput").ap() for k, v in arrays.items()}
    out = nc.dram_tensor("out_y", (P, KT, T), F32, kind="ExternalOutput").ap()
    build(nc, aps, out)
    r = run_bass_kernel_spmd(nc, [{f"in_{k}": v for k, v in arrays.items()}], core_ids=[0])
    y = r.results[0]["out_y"]
    return np.ascontiguousarray(y.transpose(2, 1, 0)).reshape(1, T, D)
```

```python
from contextlib import ExitStack

import numpy as np

import concourse.bass as bass
from concourse import mybir
from concourse.alu_op_type import AluOpType as ALU

F32 = mybir.dt.float32
F32R = mybir.dt.float32r
ACT = mybir.ActivationFunctionType
AX = mybir.AxisListType

P = 128
T = 512
D = 1024
KT = D // P
DM = 256
H_A, HD = 4, 64
C = 32
NCK = T // C
NB = 4
FF_GROUPS = 4096 // D
FF2 = 2816 // P
FF2_GROUPS = [8, 8, 6]
NH, NMH = 12, 4
MT = 256
QB = T // P
S5T = 8

RAW, SPLIT, BANKS, ADA = 2, 2, 4, 4

N_FOX, N_DIL = 21, 20
N_KV = 4

EPS, LN_EPS, LNX_EPS = 1e-6, 1e-5, 64e-5
NEG = -1e30
PI = float(np.pi)
PI_IN = 3.1415925
TWO_PI = [6.28125, 0.0019350051879882812, 3.019916e-07]
ROUND = 1.5 * 2.0 ** 23


def mixer_pieces():
    order = [("conv_in", 6), ("sg_in", 4), ("s5_in", 2)]
    for branch in ("conv", "sg"):
        order += [(branch + "_gate", 4), (branch + "_out", 1)] * 2
    order += [("rwkv_in", 7)] + [("s5_gate", 4), ("s5_out", 2)] * 2
    return order + [("rwkv_gate", 4), ("rwkv_gate", 4), ("rwkv_out", 1), ("rwkv_out", 1)]


BESIDE = [(2, None), (2, 0), (2, None), (2, 1), (1, None), (1, None), (1, None), (1, 1)]


def vec_columns():
    sizes = [("c", 8), ("ada_b", 48), ("g_mix", 8), ("mu", 7), ("w0", 2), ("a0", 2), ("kk", 2), ("ka", 2), ("rk", 2),
             ("sg_w", 2), ("sg_b", 2), ("conv_w", 6), ("s5_d", 2), ("a_re", 8), ("a_im", 8), ("log_dt", 8),
             ("g_ffn", 8), ("g_final1", 8), ("g_mix2", 16), ("g_mem2", 16), ("g_ffn2", 16), ("b_f", 1),
             ("cw2", 2 * 3 * 44), ("cb2", 2 * 44), ("g_final", 8), ("lnx_w", 64), ("lnx_b", 64)]
    at, cols = 0, {}
    for name, n in sizes:
        cols[name] = (at, n)
        at += n
    return cols, at


VEC, NVEC = vec_columns()


def const_columns():
    sizes = [("ident", 128), ("ones", 128), ("hsum", 128), ("lt", 64), ("gt", 64), ("ge", 64),
             ("stack", 64), ("sum32", 32), ("hm", 2), ("rot", 128)]
    at, cols = 0, {}
    for name, n in sizes:
        cols[name] = (at, n)
        at += n
    return cols, at


CON, NCON = const_columns()


X_DONE = [8 + 8 * FF_GROUPS + 8, 8 + 8 * FF_GROUPS + 8 + 8 + 24]

UNITS = [(h, b, (b + 1) * P, b * (b + 1) // 2 * P) for h in range(NH) for b in range(QB)] + \
        [(NH + h, b, MT, 0) for h in range(NMH) for b in range(QB)]


class Counts:

    def __init__(self):
        self.value = {}

    def next(self, name, by=1):
        self.value[name] = self.value.get(name, 0) + by
        return self.value[name]


def build(nc, A, out):
    n_mixer = sum(n for _, n in mixer_pieces())
    n_block1 = n_mixer + 8 + 2 * 8 * FF_GROUPS
    n_early = 12 + 2 * 10 + 7 + 2 * 6
    pieces = n_block1 + sum(n + N_KV + 8 + 2 * FF2 + 8 * len(FF2_GROUPS) for n in (N_FOX, N_DIL))
    with ExitStack() as ctx:
        def sb(name, shape, dt=F32):
            return ctx.enter_context(nc.sbuf_tensor(name, shape, dt))

        sems = {}

        def S(name):
            if name not in sems:
                sems[name] = ctx.enter_context(nc.semaphore(name))
            return sems[name]

        raw = sb("raw", [P, RAW, D])
        w_hi = sb("w_hi", [P, SPLIT, D], F32R)
        w_lo = sb("w_lo", [P, SPLIT, D], F32R)
        zero = sb("zero", [P, 1])
        x = sb("x", [P, KT, T])
        h_hi = sb("h_hi", [P, KT, T], F32R)
        h_lo = sb("h_lo", [P, KT, T], F32R)
        g_hi = sb("g_hi", [P, KT, T], F32R)
        g_lo = sb("g_lo", [P, KT, T], F32R)
        work = sb("work", [P, 6, T])
        vec = sb("vec", [P, NVEC])
        con = sb("con", [P, NCON])
        mod = sb("mod", [P, 48])
        small = sb("small", [P, 40, 8])
        ARENA = 21504
        arena = sb("arena", [P, ARENA])
        ps = [ctx.enter_context(nc.psum_tensor(f"ps{i}", [P, T], F32)) for i in range(8)]
        PA, PB, PC, PD = ps[4:]

        a_dram = nc.dram_tensor("pair_scores", (H_A, C, NCK, C), F32, kind="Internal").ap()
        t_dram = nc.dram_tensor("pair_inverse", (2, H_A, NCK, C // 2, C), F32, kind="Internal").ap()

        def V(name, i=0, n=None):
            at, size = VEC[name]
            return vec[:, at + i:at + i + (n or 1)]

        def K(name):
            at, size = CON[name]
            return con[:, at:at + size]

        def place(sizes, at=0):
            parts = {}
            for name, shape in sizes:
                n = int(np.prod(shape))
                assert at + n <= ARENA, (name, at + n)
                flat = arena[:, at:at + n]
                if len(shape) == 2:
                    flat = flat.rearrange("p (a b) -> p a b", a=shape[0])
                elif len(shape) == 3:
                    flat = flat.rearrange("p (a b c) -> p a b c", a=shape[0], b=shape[1])
                elif len(shape) == 4:
                    flat = flat.rearrange("p (a b c d) -> p a b c d", a=shape[0], b=shape[1], c=shape[2])
                parts[name] = flat
                at += n
            parts["end"] = at
            return parts

        def gate_room(p):
            at = (ARENA - 4 * T, ARENA - 4 * T, ARENA - 5 * T, 2048 if p < 28 else 4096)[p // 8] + p % 4 * T
            return arena[:, at:at + T]

        merged, product, glu = x, work[:, 0, :], work[:, 1, :]
        ada_m = place([("sum", (2, D)), ("ada", (ADA, D))], at=ARENA - (ADA + 2) * D)
        conv_m = place([("bg", (2, T)), ("cg", (2, T)), ("z", (2, T)), ("y", (2, T))])
        sg_m = place([("z", (4, T)), ("mu", (T,)), ("d", (2, T)), ("sq", (2, T)), ("std", (T,)), ("rstd", (T,)),
                      ("vn", (2, T)), ("vt", (2, 4, P)), ("ws", (4, P)), ("wsm", (4, P)), ("bs", (2, P)),
                      ("mix", (2, T)), ("caus", (P,))], at=4096)
        s5_m = place([("ct", (8, T)), ("st", (8, T)), ("w", (6, T)), ("bt", (2, 8, P)), ("bpad", (2, 8, P)),
                      ("bb", (2, 8, 16)), ("b_in", (2, 8, 16)), ("m8", (8, 8)), ("c_in", (2, 2, P)), ("u", (2, T))])
        s5_m["cc"] = s5_m["bpad"]
        assert s5_m["end"] <= ARENA - 4 * T
        rw_pad = place([("a", (2, NCK, 2, C)), ("b", (2, NCK, 2, C)), ("k", (2, NCK, 2, C)), ("r", (2, NCK, 2, C)),
                        ("g", (2, T)), ("bonus", (2, T))])
        rw_pad["all"] = arena[:, 0:4 * 2 * NCK * 2 * C]
        base_at = rw_pad["end"]
        rw_in = place([("r", (2, T)), ("k", (2, T)), ("v", (2, T)), ("m", (T,)), ("lw", (2, T)), ("a", (2, T)),
                       ("kk", (2, T)), ("cum", (2, T)), ("e", (2, T))], at=base_at)
        rw_bd = place([("ab", (NCK, 64)), ("akT", (NCK, 64)), ("vt", (NCK, 64)), ("rbT", (NCK, 64)),
                       ("rkT", (NCK, 64)), ("tT", (NCK, 64)), ("kt", (NCK, P))], at=base_at)
        rw_sol = place([("as", (C, C)), ("z", (C // 2, C)), ("o", (NCK, 64))],
                       at=max(rw_in["end"], rw_bd["end"]))
        at_m = place([("q", (NH + NMH, T)), ("k", (NH, T)), ("km", (NMH, MT)), ("v", (QB, NH * HD)), 
                      ("p", (2, T)), ("pt", (QB, T))])
        rw_sol["prod"] = work[:, 4, :]
        at_m["vm"] = work[:, 5, :].rearrange("p (a b) -> p a b", a=2)
        probs = [at_m["p"][:, 0, :], at_m["p"][:, 1, :], work[:, 3, :], work[:, 4, :]]
        mem_in = at_m["pt"].rearrange("p a b -> p (a b)").rearrange("p (k t) -> p k t", k=KT)
        rope_t = arena[:, at_m["end"] - 4 * T - 2 * T:at_m["end"] - 4 * T].rearrange("p (a b) -> p a b", a=2)
        cv_m = place([("cv", (2, T)), ("cg", (2, T)), ("sg", (2, T)), ("t", (2, T)), ("z", (2, T))])
        rstd = work[:, 5, :]
        room = at_m["v"].rearrange("p a b -> p (a b)")
        mem_sq = lambda k: room[:, MT * (k % 2):MT * (k % 2) + MT]
        mem_t = lambda k: room[:, MT * (2 + k % 2):MT * (2 + k % 2) + MT]
        mem_total, mem_rstd = room[:, 4 * MT:5 * MT], room[:, 5 * MT:6 * MT]
        mix_gain = small[:, 1, :]
        ff_m = place([("r", (2, T)), ("s", (2, T))])
        rw_bt = rw_pad["k"].rearrange("p a n h c -> p (a n h c)").rearrange("p (n c) -> p n c", n=NCK)
        state = work[:, 2, 0:6 * HD].rearrange("p (a b c) -> p a b c", a=3, b=2)
        chain_y = work[:, 3, 0:2 * HD].rearrange("p (a b) -> p a b", a=2)


        block = ctx.enter_context(nc.Block())
        lora = work[:, 5, 0:DM]
        masks = work[:, 0:3, :].rearrange("p a b -> p (a b)")[:, 0:(QB * (QB + 1) // 2) * P]

        def mn(pair, k):
            return pair[:, k // 2, MT * (k % 2):MT * (k % 2) + MT]


        @block.sync
        def _(sp):
            sp.dma_start(vec[:], A["vec"]).then_inc(S("vec_in"), 16)
            sp.dma_start(con[:], A["con"]).then_inc(S("con_in"), 16)
            ada = ada_m["ada"]
            for q in range(ADA):
                sp.dma_start(ada[:, q, :], A["ada"][q]).then_inc(S(f"ada_in{q}"), 16)
            sp.dma_start(x[:], A["xT"]).then_inc(S("x_in"), 16)
            for q in range(RAW):
                if q < pieces:
                    sp.dma_start(raw[:, q, :], A["w"][q]).then_inc(S(f"raw_in{q}"), 16)
            for q in range(ADA, 16):
                sp.wait_ge(S("ada_used"), q - ADA + 1)
                sp.dma_start(ada[:, q % ADA, :], A["ada"][q]).then_inc(S(f"ada_in{q % ADA}"), 16)
            def stream_to(a, b):
                def one(q, n, slot):
                    sp.wait_ge(S("w_split"), q - RAW + 1)
                    sp.dma_start(raw[:, slot, :], n).then_inc(S(f"raw_in{slot}"), 16)
                while a < b and (a % RAW or b - a < RAW):
                    one(a, A["w"][a], a % RAW)
                    a += 1
                turns = (b - a) // RAW
                if turns == 1:
                    for k in range(RAW):
                        one(a + k, A["w"][a + k], k)
                elif turns > 1:
                    w = A["w"][0:pieces // RAW * RAW].rearrange("(g s) p n -> g s p n", s=RAW)
                    with sp.Fori(a // RAW, a // RAW + turns) as g:
                        for k in range(RAW):
                            one(g * RAW + k, w[bass.ds(g, 1), k].rearrange("a p n -> (a p) n"), k)
                a += turns * RAW
                while a < b:
                    one(a, A["w"][a], a % RAW)
                    a += 1

            stream_to(RAW, 8)
            sp.wait_ge(S("ada_used"), 16)
            sp.dma_start(sg_m["ws"], A["sg_ws"]).then_inc(S("sg_in"), 16)
            sp.dma_start(sg_m["bs"], A["sg_bs"]).then_inc(S("sg_in"), 16)
            sp.dma_start(sg_m["caus"], A["caus"]).then_inc(S("sg_in"), 16)
            for name, key in (("b_in", "s5_b"), ("m8", "s5_m8"), ("c_in", "s5_c")):
                sp.dma_start(s5_m[name], A[key]).then_inc(S("s5_in"), 16)
            stream_to(8, 32)
            stream_to(32, 34)
            sp.wait_ge(S("s5_y"), 2)
            sp.dma_start(lora, A["lora"]).then_inc(S("lora_in"), 16)
            stream_to(34, n_early)
            sp.wait_ge(S("ab_scores"), 1)
            ab = rw_bd["ab"]
            for h in range(H_A):
                sp.dma_start(a_dram[h], ab[C * h:C * h + C, :, C * (h % 2):C * (h % 2) + C]).then_inc(S("a_out"), 16)
            sp.wait_ge(S("a_out"), 16 * H_A)
            for half in range(2):
                for h in range(H_A):
                    at = 64 * half + NCK * h
                    sp.dma_start(rw_sol["as"][at:at + NCK], a_dram[h].rearrange("t n s -> n t s")).then_inc(S("a_in"), 16)
            sp.dma_start(rw_sol["z"], A["eye"].rearrange("p (c t) -> p c t", t=C)).then_inc(S("a_in"), 16)
            stream_to(n_early, n_early + 4)
            sp.wait_ge(S("solved"), C - 1)
            sp.dma_start(t_dram.rearrange("a h n c t -> (a h n) (c t)"),
                         rw_sol["z"].rearrange("p c t -> p (c t)")).then_inc(S("t_out"), 16)
            sp.wait_ge(S("t_out"), 16)
            sp.wait_ge(S("tT_clear"), 1)
            for half in range(2):
                for h in range(H_A):
                    at = C * h + C // 2 * half
                    sp.dma_start(rw_bd["tT"][at:at + C // 2, :, C * (h % 2):C * (h % 2) + C],
                                 t_dram[half, h].rearrange("n c t -> c n t")).then_inc(S("tT_in"), 16)
            stream_to(n_early + 4, n_early + 9)
            sp.wait_ge(S("rw_out"), 2)
            for q in range(16, 48):
                if q >= 16 + ADA:
                    sp.wait_ge(S("ada_used"), q - ADA + 1)
                sp.dma_start(ada_m["ada"][:, q % ADA, :], A["ada"][q]).then_inc(S(f"ada_in{q % ADA}"), 16)
                if q == 19:
                    stream_to(n_early + 9, n_mixer)
                if q == 23:
                    stream_to(n_mixer, n_mixer + 3)
                    for k in range(0, KT, 2):
                        sp.wait_ge(S("merged"), k + 2)
                        sp.dma_start(x[:, k:k + 2, :], A["xT"][:, k:k + 2, :]).then_inc(S("x_in"), 16)
                if 24 < q < 34 and q % 2:
                    stream_to(n_mixer + 3 + (q - 25) // 2, n_mixer + 4 + (q - 25) // 2)
                if q == 43:
                    stream_to(n_mixer + 8, n_mixer + 12)
                if q > 43:
                    stream_to(n_mixer + q - 32, n_mixer + q - 31)
            stream_to(n_mixer + 16, n_mixer + 20)
            sp.wait_ge(S("ada_used"), 48)
            sp.dma_start(mem_in, A["memT"]).then_inc(S("mem_in"), 16)
            stream_to(n_mixer + 20, n_block1)
            first = n_block1
            for layer, n_in in ((0, N_FOX), (1, N_DIL)):
                stream_to(first, first + 2)
                if layer:
                    sp.wait_ge(S("rms_ready"), 7)
                    sp.dma_start(work[:, 2:4, :], A["rope"]).then_inc(S("rope_in"), 16)
                    stream_to(first + 2, first + 14)
                    sp.wait_ge(S("rope_done"), 12)
                    sp.dma_start(masks, A["mask_dil"]).then_inc(S("mask_in"), 16)
                    stream_to(first + 14, first + n_in + N_KV)
                else:
                    stream_to(first + 2, first + n_in + N_KV)
                    sp.wait_ge(S("forget_sum"), 1)
                    sp.dma_start(at_m["k"][HD:HD + 1, :, :], work[0:NH, 4, :]).then_inc(S("forget_in"), 16)
                    sp.wait_ge(S("forget_in"), 16)
                    sp.dma_start(masks, A["mask_fox"]).then_inc(S("mask_in"), 16)
                last = first + n_in + N_KV + 8 + 2 * FF2 + 24
                stream_to(first + n_in + N_KV, first + n_in + N_KV + 8)
                if layer == 0:
                    sp.wait_ge(S("heads"), NH + NMH)
                    sp.dma_start(mem_in, A["memT"]).then_inc(S("mem_in"), 16)
                stream_to(first + n_in + N_KV + 8, last)
                first = last
            sp.wait_ge(S("result"), KT)
            sp.dma_start(out, arena[:, 0:KT * T].rearrange("p (k t) -> p k t", k=KT)).then_inc(S("stored"), 16)
            sp.wait_ge(S("stored"), 16)

        @block.gpsimd
        def _(pool):
            pool.memset(zero[:], 0.0).then_inc(S("zero_set"), 1)
            pool.wait_ge(S("zero_set"), 1)

            def split(q, slot, landed, free):
                pool.wait_ge(S(f"raw_in{slot}"), landed)
                if free is not None:
                    pool.wait_ge(S("w_used"), free)
                pool.tensor_tensor(w_hi[:, slot % SPLIT, :], raw[:, slot, :], zero[:].broadcast_to((P, D)), ALU.add).then_inc(S("w_high"), 1)
                pool.wait_ge(S("w_high"), q + 1)
                pool.tensor_tensor(w_lo[:, slot % SPLIT, :], raw[:, slot, :], w_hi[:, slot % SPLIT, :].bitcast(F32),
                                   ALU.subtract).then_inc(S("w_split"), 1)

            for q in range(min(RAW, pieces)):
                split(q, q, 16, None if q < SPLIT else q - SPLIT + 1)
            turns = pieces // RAW
            if turns > 1:
                with pool.Fori(1, turns) as g:
                    for k in range(RAW):
                        split(g * RAW + k, k, g * 16 + 16, g * RAW + (k - SPLIT + 1))
            for q in range(max(turns, 1) * RAW, pieces):
                split(q, q % RAW, 16 * (q // RAW + 1), q - SPLIT + 1)

        @block.vector
        def _(dve):
            n = Counts()

            def do(ins, name="dve_step"):
                ins.then_inc(S(name), 1)
                dve.wait_ge(S(name), n.next(name))

            def need(name, by=1):
                dve.wait_ge(S(name), n.next(name, by))

            def both_parts(hi, lo, src, name):
                do(dve.tensor_copy(hi, src))
                do(dve.tensor_tensor(lo, src, hi.bitcast(F32), ALU.subtract), name)

            def add_square(k, sq, acc):
                need("square")
                if k == 0:
                    do(dve.tensor_copy(acc, sq(k)), "square_used")
                else:
                    do(dve.tensor_tensor(acc, acc, sq(k), ALU.add), "square_used")

            def add_square_x(k):
                add_square(k, lambda k: work[:, k % 2, :], work[:, 2, :])

            def last_terms(update, gain=None, after=add_square_x):
                def finish(k):
                    after(k)
                    if gain is not None:
                        need("h_high")
                        do(dve.scalar_tensor_tensor(h_lo[:, k, :], x[:, k, :], gain(k), h_hi[:, k, :].bitcast(F32),
                                                    ALU.mult, ALU.subtract), "h_ready")

                for k in range(KT):
                    update(k)
                    if k:
                        finish(k - 1)
                finish(KT - 1)

            def two_squares(k):
                for slot, acc in ((0, work[:, 2, :]), (1, work[:, 3, :])):
                    add_square(k, lambda _: work[:, slot, :], acc)

            def finish_rstd():
                need("rms_ready")
                do(dve.reciprocal(rstd, rstd))

            def norm_start():
                need("rms_ready")
                do(dve.reciprocal(work[:, 3, :], work[:, 3, :]))

            def norm(gain, shift=None):
                for k in range(KT):
                    t = work[:, 4 + k % 2, :]
                    do(dve.scalar_tensor_tensor(t, x[:, k, :], gain(k), work[:, 3, :], ALU.mult, ALU.mult))
                    if shift is not None:
                        do(dve.tensor_scalar(t, t, shift(k), None, ALU.add))
                    both_parts(h_hi[:, k, :], h_lo[:, k, :], t, "h_ready")

            def add_to_x(k, gate=None):
                need("tile")
                bank = ps[n.value["bank"] % BANKS]
                if gate is None:
                    do(dve.tensor_tensor(x[:, k, :], bank[:], x[:, k, :], ALU.add), "dve_freed")
                else:
                    do(dve.scalar_tensor_tensor(x[:, k, :], bank[:], gate, x[:, k, :], ALU.mult, ALU.add), "dve_freed")
                n.value["bank"] += 1

            n.value["bank"] = 0

            def tile():
                need("tile")
                n.value["bank"] += 1
                return ps[(n.value["bank"] - 1) % BANKS]

            def skip(tiles):
                n.next("tile", tiles)
                n.value["bank"] += tiles


            def modulate(group, a, b):
                for k in range(a, b):
                    q, acc = 8 * group + k, ada_m["sum"][:, group % 2, :]
                    dve.wait_ge(S(f"ada_in{q % ADA}"), 16 * (q // ADA + 1))
                    w = ada_m["ada"][:, q % ADA, :]
                    if k == 0:
                        do(dve.tensor_scalar(acc, w, c_act[:, k:k + 1], None, ALU.mult), "ada_used")
                    else:
                        do(dve.scalar_tensor_tensor(acc, w, c_act[:, k:k + 1], acc, ALU.mult, ALU.add), "ada_used")
                if b == 8:
                    do(dve.memset(small[:, 39, :], 0.0), "ada_sum")

            def modulation(group, groups=1):
                need("ada_total", groups)
                cols = slice(8 * group, 8 * (group + groups))
                do(dve.tensor_tensor(mod[:, cols], PA[:, cols], V("ada_b", 8 * group, 8 * groups), ALU.add))

            def vector_recurrence():
                v, bd, sol = rw_in, rw_bd, rw_sol
                keep = small[:, 24, 0:7]
                do(dve.tensor_scalar(keep, V("mu", 0, 7), -1.0, 1.0, ALU.mult, ALU.add))
                for i, dst in enumerate([v["r"][:, 0], v["r"][:, 1], v["k"][:, 0], v["k"][:, 1], v["v"][:, 0], v["v"][:, 1], v["m"]]):
                    bank = tile()
                    do(dve.tensor_scalar(dst, bank[:], keep[:, i:i + 1], None, ALU.mult))
                    do(dve.scalar_tensor_tensor(dst[:, 1:], bank[:, :T - 1], V("mu", i), dst[:, 1:], ALU.mult, ALU.add), "dve_freed")
                do(dve.memset(rw_pad["all"], 0.0), "rw_shifted")
                e, cum, lw, kk = v["e"], v["cum"], v["lw"], v["kk"]
                reset = e[:, 1, :]
                do(dve.memset(reset, 1.0))
                do(dve.memset(reset.rearrange("p (n t) -> p n t", t=C)[:, :, 0:1], 0.0))
                for k in range(2):
                    need("rw_decay")
                    do(dve.tensor_scalar(lw[:, k], lw[:, k], -float(np.exp(-0.5)), None, ALU.mult))
                    do(dve.tensor_tensor_scan(cum[:, k], reset, lw[:, k], 0.0, ALU.mult, ALU.add), "rw_cum")
                for k in range(2):
                    do(dve.tensor_scalar(kk[:, k], v["k"][:, k], V("kk", k), None, ALU.mult))
                    do(dve.tensor_tensor(e[:, k], kk[:, k], kk[:, k], ALU.mult), "rw_kk_square")
                skip(4)
                for f in range(4):
                    gated(f, glu_tiles=True)
                for k in range(2):
                    need("rw_kk_sum")
                    do(dve.tensor_scalar(e[:, k], PA[:] if k == 0 else PB[:], 1e-24, None, ALU.max), "rw_kk_floor")
                for k in range(2):
                    need("rw_kk_norm")
                    do(dve.reciprocal(e[:, k], e[:, k]))
                    do(dve.tensor_tensor(kk[:, k], kk[:, k], e[:, k], ALU.mult))
                drop = small[:, 24, 0:2]
                do(dve.tensor_scalar(drop, V("ka", 0, 2), -1.0, 1.0, ALU.mult, ALU.add))
                for k in range(2):
                    need("rw_a")
                    do(dve.tensor_scalar(e[:, k], v["a"][:, k], V("ka", k), drop[:, k:k + 1], ALU.mult, ALU.add))
                    do(dve.tensor_tensor(v["k"][:, k], v["k"][:, k], e[:, k], ALU.mult))
                    do(dve.scalar_tensor_tensor(e[:, k], v["r"][:, k], V("rk", k), v["k"][:, k], ALU.mult, ALU.mult), "rw_rk")
                    do(dve.tensor_tensor(v["a"][:, k], v["a"][:, k], kk[:, k], ALU.mult))
                for k in range(2):
                    need("rw_rk_sum")
                    do(dve.tensor_tensor(rw_pad["bonus"][:, k], (PC if k == 0 else PD)[:], v["v"][:, k], ALU.mult))
                do(dve.memset(small[:, 39, :], 0.0), "rw_exp_go")
                skip(4)
                for f in range(4):
                    gated(4 + f, glu_tiles=True)
                half = lambda ap, g: ap[64 * g:64 * g + 64].rearrange("p (n t) -> p n t", t=C)
                pad = lambda name, k, g: rw_pad[name][64 * g:64 * g + 64, k, :, g, :]
                pc = small[:, 25:29, :].rearrange("p a b -> p (a b)").rearrange("p (k n) -> p k n", k=2)
                for k in range(2):
                    need("rw_exp")
                    for g in range(2):
                        do(dve.tensor_tensor(pad("r", k, g), half(v["r"][:, k], g), half(e[:, 0], g), ALU.mult))
                    do(dve.tensor_copy(pc[:, k, :], e[:, 0].rearrange("p (n t) -> p n t", t=C)[:, :, C - 1]))
                    do(dve.tensor_tensor(lw[:, k], cum[:, k], lw[:, k], ALU.subtract), "rw_before")
                    need("rw_exp")
                    for g in range(2):
                        do(dve.scalar_tensor_tensor(pad("a", k, g), half(kk[:, k], g), -1.0, half(e[:, 1], g), ALU.mult, ALU.mult))
                    need("rw_exp")
                    for g in range(2):
                        do(dve.tensor_tensor(pad("b", k, g), half(v["a"][:, k], g), half(e[:, 0], g), ALU.mult))
                        do(dve.tensor_tensor(pad("k", k, g), half(v["k"][:, k], g), half(e[:, 0], g), ALU.mult), "rw_padded")

                def bd_copy(dst, mask=None, per=8, name=None):
                    for q in range(NCK // per):
                        need("bd")
                        i = n.value["bd"] - 1
                        src = ps[4 + i % 4][:, 0:per * (T // per)].rearrange("p (n c) -> p n c", n=per)
                        d = dst[:, per * q:per * q + per, :]
                        if mask is None:
                            ins = dve.tensor_copy(d, src)
                        else:
                            ins = dve.tensor_tensor(d, src, mask.unsqueeze(1).broadcast_to((P, per, 64)), ALU.mult)
                        do(ins, "bd_used")

                bd_copy(bd["ab"], K("lt"))
                do(dve.memset(small[:, 39, :], 0.0), "ab_scores")
                bd_copy(bd["akT"], K("gt"))
                bd_copy(bd["rkT"], K("ge"))
                bd_copy(bd["rbT"], K("ge"))
                do(dve.memset(bd["tT"], 0.0), "tT_clear")
                bd_copy(bd["kt"], per=4)
                do(dve.memset(rw_pad["k"].rearrange("p a n h c -> p (a n h c)"), 0.0))
                for k in range(2):
                    for g in range(2):
                        do(dve.tensor_copy(pad("k", k, g), half(v["v"][:, k], g)), "v_padded")
                bd_copy(bd["vt"])
                bd_copy(rw_bt, per=4)
                dve.wait_ge(S("a_in"), 16 * 9)
                a_m, z, prod = sol["as"], sol["z"], sol["prod"]
                do(dve.memset(a_m.rearrange("p t s -> p (t s)")[:, 0:C * C:C + 1], 1.0))
                for i in range(1, C):
                    pr = prod[:, 0:C // 2 * (i + 1)].rearrange("p (c j) -> p c j", j=i + 1)
                    do(dve.tensor_tensor(pr, z[:, :, 0:i + 1], a_m[:, i, 0:i + 1].unsqueeze(1).broadcast_to((P, C // 2, i + 1)), ALU.mult))
                    do(dve.tensor_reduce(z[:, :, i], pr, AX.X, ALU.add), "solved")
                do(dve.memset(state, 0.0), "state_set")
                for c in range(NCK):
                    now, then = c % 2, 1 - c % 2
                    for p in range(2):
                        do(dve.tensor_scalar(state[:, 2, p, :], state[:, now, p, :], pc[:, p, c:c + 1], None, ALU.mult))
                    need("rec_y", 2)
                    do(dve.tensor_copy(chain_y[0:64, 0, :], ps[0][0:64, 0:HD]), "rec_y_copied")
                    need("rec_sa", 2)
                    do(dve.tensor_copy(chain_y[0:64, 1, :], ps[6][0:64, 0:HD]), "rec_sa_copied")
                    for p in range(2):
                        need("rec_state")
                        if p == 0 and c:
                            need("rec_o")
                        do(dve.scalar_tensor_tensor(state[:, then, p, :], ps[4 + p][:, P:P + HD], pc[:, p, c:c + 1], state[:, 2, p, :],
                                                    ALU.mult, ALU.add), "state_set")
                need("rec_o")
                need("rec_o_copied", 2 * NCK)
                o, sq = sol["o"], bd["ab"]
                mean, var = small[:, 29:31, :].rearrange("p a b -> p (a b)"), small[:, 31:33, :].rearrange("p a b -> p (a b)")
                spread = lambda s: s.unsqueeze(2).broadcast_to((P, NCK, HD))
                do(dve.tensor_reduce(mean, o, AX.X, ALU.add))
                do(dve.tensor_scalar(mean, mean, 1.0 / HD, None, ALU.mult))
                do(dve.tensor_tensor(o, o, spread(mean), ALU.subtract))
                do(dve.tensor_tensor(sq, o, o, ALU.mult))
                do(dve.tensor_reduce(var, sq, AX.X, ALU.add))
                do(dve.tensor_scalar(var, var, 1.0 / HD, LNX_EPS, ALU.mult, ALU.add), "rw_var")
                need("rw_std")
                do(dve.reciprocal(var, var))
                do(dve.tensor_tensor(o, o, spread(var), ALU.mult))
                at_w, at_b = VEC["lnx_w"][0], VEC["lnx_b"][0]
                over = lambda at: vec[:, at:at + HD].unsqueeze(1).broadcast_to((P, NCK, HD))
                do(dve.tensor_tensor(o, o, over(at_w), ALU.mult))
                do(dve.tensor_tensor(o, o, over(at_b), ALU.add))
                opad = rw_pad["a"].rearrange("p a n h c -> p (a n h c)").rearrange("p (n h i) -> p n h i", n=NCK, h=2)
                for g in range(2):
                    do(dve.tensor_scalar(opad[:, :, g, :], o, K("hm")[:, g:g + 1], None, ALU.mult), "o_padded")
                for k in range(2):
                    need("rw_o")
                    do(dve.tensor_tensor(rw_pad["bonus"][:, k], rw_pad["bonus"][:, k], ps[4 + k][:], ALU.add))
                    do(dve.tensor_tensor(rw_pad["bonus"][:, k], rw_pad["bonus"][:, k], rw_pad["g"][:, k], ALU.mult))
                    both_parts(g_hi[:, 6 + k, :], g_lo[:, 6 + k, :], rw_pad["bonus"][:, k], "rw_out")
                skip(8)

            def vector_layer(layer):
                finish_rstd()
                if layer == 0:
                    again = work[:, 4, :]
                    do(dve.tensor_tensor(again, rstd, rstd, ALU.mult))
                    dve.wait_ge(S("squares_total"), 4)
                    do(dve.tensor_tensor(again, again, PA[:], ALU.mult), "second_square")
                    for k in range(KT):
                        do(dve.scalar_tensor_tensor(x[:, k, :], x[:, k, :], V("g_final1", k), rstd, ALU.mult, ALU.mult), "x_done")
                    need("rms_ready")
                    do(dve.reciprocal(again, again))
                    do(dve.tensor_tensor(rstd, rstd, again, ALU.mult))
                else:
                    dve.wait_ge(S("rope_in"), 16)
                    for i in (2, 3):
                        do(dve.tensor_tensor(work[:, i, :], work[:, i, :], rstd, ALU.mult))
                dve.wait_ge(S("mem_in"), 16 * (layer + 1))

                def memory_norm(i):
                    if i < KT:
                        add_square(i, mem_sq, mem_total)
                    elif i == 9:
                        need("rms_ready")
                        do(dve.reciprocal(mem_rstd, mem_rstd))
                    elif i > 9:
                        for k in range(4 * (i - 10), 4 * (i - 10) + 4):
                            do(dve.scalar_tensor_tensor(mem_t(k), mem_in[:, k, :], V("g_mem2", 8 * layer + k), mem_rstd,
                                                        ALU.mult, ALU.mult))
                            both_parts(mn(g_hi, k), mn(g_lo, k), mem_t(k), "mem_ready")

                q, km, kk = at_m["q"], at_m["km"], at_m["k"]
                scaled = lambda bank, g: (bank[64 * g:64 * g + 64, :], HD ** -0.5, rstd[64 * g:64 * g + 64, :], ALU.mult, ALU.mult)
                do(dve.memset(q[HD:HD + 1, :, :], 1.0))
                for name, dst in (("q", q), ("k", kk)):
                    for i in range(NH // 2):
                        if layer == 0:
                            bank = tile()
                            for g in range(2):
                                do(dve.scalar_tensor_tensor(dst[0:HD, 2 * i + g, :], bank[64 * g:64 * g + 64, :],
                                                            HD ** -0.5 if name == "q" else 1.0, rstd[64 * g:64 * g + 64, :],
                                                            ALU.mult, ALU.mult),
                                   "dve_freed" if g else "dve_step")
                        else:
                            skip(1)
                            need("rope_copied")
                            t, sw = rope_t[:, i % 2, :], ps[6 + i % 2]
                            need("rope_swapped")
                            u = work[:, 4, :]
                            do(dve.tensor_tensor(u, sw[:], work[:, 3, :], ALU.mult))
                            do(dve.tensor_tensor(t, t, work[:, 2, :], ALU.mult))
                            for g in range(2):
                                do(dve.tensor_tensor(dst[0:HD, 2 * i + g, :], t[64 * g:64 * g + 64, :], u[64 * g:64 * g + 64, :], ALU.add),
                                   "rope_done" if g else "dve_step")
                        memory_norm(i if name == "q" else NH // 2 + i)

                def take(i):
                    need("v_turned")
                    do(dve.tensor_copy(at_m["v"][:, :, P * i:P * i + P], ps[6 + i % 2][:].rearrange("p (a b) -> p a b", a=QB)), "v_taken")

                for i in range(NH // 2):
                    do(dve.tensor_tensor(rope_t[:, i % 2, :], tile()[:], rstd, ALU.mult), "v_scaled")
                    if i:
                        take(i - 1)
                take(NH // 2 - 1)
                if layer == 0:
                    bank = tile()
                    f = lambda i: work[0:NH, i, :]
                    do(dve.tensor_tensor(f(0), bank[0:NH, :], rstd[0:NH, :], ALU.mult), "dve_freed")
                    do(dve.tensor_scalar(f(0), f(0), V("b_f")[0:NH], None, ALU.add))
                    do(dve.tensor_scalar(f(1), f(0), -1.0, None, ALU.mult))
                    do(dve.tensor_tensor(f(1), f(1), f(0), ALU.min), "forget_in_abs")
                    need("forget_log")
                    do(dve.tensor_scalar(f(0), f(0), 0.0, None, ALU.min))
                    do(dve.tensor_tensor(f(0), f(1), f(0), ALU.subtract))
                    do(dve.memset(f(2), 1.0))
                    do(dve.tensor_tensor_scan(f(4), f(2), f(0), 0.0, ALU.mult, ALU.add), "forget_sum")
                for i in range(NMH // 2):
                    bank = tile()
                    for g in range(2):
                        do(dve.scalar_tensor_tensor(q[0:HD, NH + 2 * i + g, :], *scaled(bank, g)), "dve_freed" if g else "dve_step")
                for i in range(NMH // 2):
                    bank = tile()
                    for g in range(2):
                        do(dve.tensor_copy(km[0:HD, 2 * i + g, :], bank[64 * g:64 * g + 64, 0:MT]), "dve_freed" if g else "dve_step")
                for i in range(NMH // 2):
                    skip(1)
                    need("v_turned")
                    do(dve.tensor_copy(at_m["vm"][:, :, P * i:P * i + P],
                                       ps[6 + i % 2][:, 0:MT].rearrange("p (a b) -> p a b", a=2)), "v_taken")
                dve.wait_ge(S("mask_in"), 16 * (layer + 1))
                before = len(UNITS) * layer

                def head_low(head):
                    rows = slice(64 * (head % 2), 64 * (head % 2) + 64)
                    need("head_hi")
                    do(dve.tensor_tensor(g_lo[rows, head // 2, :], ps[6 + head % 2][rows, :], g_hi[rows, head // 2, :].bitcast(F32),
                                         ALU.subtract), "heads")

                for s in range(len(UNITS) + 1):
                    if s < len(UNITS):
                        head, qb, width, at = UNITS[s]
                        if s >= 4:
                            dve.wait_ge(S("probs_turned"), before + s - 3)
                        need("scores")
                        src, pr, top = ps[s % BANKS][:, 0:width], probs[s % 4][:, 0:width], small[:, 33 + s % 4, 0:1]
                        if head < NH and layer == 1:
                            do(dve.tensor_tensor(pr, src, masks[:, at:at + width], ALU.add))
                            src = pr
                        do(dve.tensor_reduce(top, src, AX.X, ALU.max, negate=True), "score_top")
                    if s:
                        u = s - 1
                        head, qb, width, at = UNITS[u]
                        pr, rec = probs[u % 4][:, 0:width], small[:, 33 + u % 4, 1:2]
                        need("exped")
                        do(dve.reciprocal(rec, small[:, 33 + u % 4, 2:3]))
                        do(dve.tensor_scalar(pr, pr, rec, None, ALU.mult), "probs")
                        if qb == QB - 1 and head:
                            head_low(head - 1)
                head_low(NH + NMH - 1)
                last_terms(lambda k: do(dve.tensor_tensor(x[:, k, :], tile()[:], x[:, k, :], ALU.add), "x_done"),
                           lambda k: V("g_ffn2", 8 * layer + k))
                finish_rstd()
                for group in range(len(FF2_GROUPS)):
                    vector_ffn2(layer, group)

            def vector_ffn2(layer, group):
                j0 = sum(FF2_GROUPS[:group])
                for j in range(FF2_GROUPS[group]):
                    for side in range(2):
                        do(dve.tensor_tensor(cv_m["z"][:, side, :], tile()[:], rstd, ALU.mult), "conv_scaled")
                    for side, c in ((0, cv_m["cv"]), (1, cv_m["cg"])):
                        z = cv_m["z"][:, side, :]
                        need("conv_first")
                        dst, w = c[:, j % 2, :], lambda tap: V("cw2", (3 * layer + tap) * 44 + 22 * side + j0 + j)
                        do(dve.scalar_tensor_tensor(dst[:, 1:], z[:, :T - 1], w(1), dst[:, 1:], ALU.mult, ALU.add))
                        do(dve.scalar_tensor_tensor(dst[:, 2:], z[:, :T - 2], w(0), dst[:, 2:], ALU.mult, ALU.add), "conv_summed")
                    need("conv_gate")
                    t = cv_m["t"][:, j % 2, :]
                    do(dve.tensor_tensor(t, cv_m["cv"][:, j % 2, :], cv_m["sg"][:, j % 2, :], ALU.mult), "conv_used")
                    both_parts(g_hi[:, j, :], g_lo[:, j, :], t, "hidden")
                update = lambda k: do(dve.tensor_tensor(x[:, k, :], tile()[:], x[:, k, :], ALU.add), "x_done")
                if group == len(FF2_GROUPS) - 1:
                    last_terms(update, None if layer else lambda k: V("g_mix2", 8 + k))
                else:
                    for k in range(KT):
                        update(k)

            do(dve.memset(small[:, 38, 0:1], EPS), "eps_set")
            do(dve.memset(small[:, 38, 1:2], LN_EPS), "eps_set")
            dve.wait_ge(S("vec_in"), 16)
            dve.wait_ge(S("con_in"), 16)
            c_act = small[:, 0, :]
            need("silu_c")
            do(dve.tensor_tensor(c_act, V("c", 0, 8), small[:, 1, :], ALU.mult), "c_act")
            row = lambda i: small[:, i, :]
            lam, dt, e1, mag, th, kq, sn, sh, cs, ar, ai, den, am, qr, qi, t1, t2, pr, pi, t3 = (row(i) for i in range(3, 23))
            do(dve.tensor_scalar(lam, V("a_re", 0, 8), -1e-4, None, ALU.min))
            need("s5_dt")
            do(dve.tensor_tensor(e1, lam, dt, ALU.mult), "s5_e1")
            do(dve.tensor_tensor(th, V("a_im", 0, 8), dt, ALU.mult))
            do(dve.tensor_scalar(kq, th, 1.0 / (2 * PI), ROUND, ALU.mult, ALU.add))
            do(dve.tensor_scalar(kq, kq, ROUND, None, ALU.subtract))
            for part in TWO_PI:
                do(dve.scalar_tensor_tensor(th, kq, -part, th, ALU.mult, ALU.add))
            do(dve.tensor_scalar(th, th, PI_IN, -PI_IN, ALU.min, ALU.max), "s5_angle")
            need("s5_sines")
            do(dve.tensor_tensor(cs, sh, sh, ALU.mult))
            do(dve.tensor_scalar(cs, cs, -2.0, 1.0, ALU.mult, ALU.add))
            do(dve.tensor_tensor(ar, mag, cs, ALU.mult))
            do(dve.tensor_tensor(ai, mag, sn, ALU.mult))
            do(dve.tensor_tensor(den, lam, lam, ALU.mult))
            do(dve.tensor_tensor(t1, V("a_im", 0, 8), V("a_im", 0, 8), ALU.mult))
            do(dve.tensor_tensor(den, den, t1, ALU.add))
            do(dve.reciprocal(den, den))
            do(dve.tensor_scalar(am, ar, 1.0, None, ALU.subtract))
            do(dve.tensor_tensor(qr, am, lam, ALU.mult))
            do(dve.tensor_tensor(t1, ai, V("a_im", 0, 8), ALU.mult))
            do(dve.tensor_tensor(qr, qr, t1, ALU.add))
            do(dve.tensor_tensor(qr, qr, den, ALU.mult))
            do(dve.tensor_tensor(qi, ai, lam, ALU.mult))
            do(dve.tensor_tensor(t1, am, V("a_im", 0, 8), ALU.mult))
            do(dve.tensor_tensor(qi, qi, t1, ALU.subtract))
            do(dve.tensor_tensor(qi, qi, den, ALU.mult))
            modulate(0, 0, 8)
            for k in range(KT):
                add_square_x(k)
            modulate(1, 0, 4)
            norm_start()
            modulate(1, 4, 8)
            modulation(0, 2)
            gain1 = small[:, 2, :]
            do(dve.scalar_tensor_tensor(gain1, mod[:, 8:16], 1.0, V("g_mix", 0, 8), ALU.add, ALU.mult))
            norm(lambda k: gain1[:, k:k + 1], lambda k: mod[:, k:k + 1])

            bg, cg, z, y = (conv_m[k] for k in ("bg", "cg", "z", "y"))
            for dst in (bg, cg):
                for k in range(2):
                    do(dve.tensor_copy(dst[:, k, :], tile()[:]), "dve_freed")
            for k in range(2):
                do(dve.tensor_tensor(z[:, k, :], tile()[:], cg[:, k, :], ALU.mult), "dve_freed")
            for k in range(2):
                cw = lambda j: V("conv_w", 2 * j + k)
                do(dve.tensor_scalar(y[:, k, :], z[:, k, :], cw(2), None, ALU.mult))
                for lag in (1, 2):
                    do(dve.scalar_tensor_tensor(y[:, k, lag:], z[:, k, :T - lag], cw(2 - lag), y[:, k, lag:], ALU.mult, ALU.add))
                do(dve.tensor_tensor(y[:, k, :], y[:, k, :], bg[:, k, :], ALU.mult))
                both_parts(g_hi[:, k, :], g_lo[:, k, :], y[:, k, :], "conv_y")

            skip(4)
            m = sg_m
            dve.wait_ge(S("sg_in"), 48)
            do(dve.tensor_tensor(m["wsm"], m["ws"], m["caus"].unsqueeze(1).broadcast_to((P, 4, P)), ALU.mult), "sg_w_masked")
            need("sg_mean")
            do(dve.tensor_scalar(m["mu"], PA[:], 1.0 / DM, None, ALU.mult))
            for k in range(2):
                do(dve.tensor_tensor(m["d"][:, k, :], m["z"][:, 2 + k, :], m["mu"], ALU.subtract))
                do(dve.tensor_tensor(m["sq"][:, k, :], m["d"][:, k, :], m["d"][:, k, :], ALU.mult), "sg_square")
            need("sg_std")
            do(dve.reciprocal(m["rstd"], m["std"]))
            for k in range(2):
                do(dve.tensor_tensor(m["d"][:, k, :], m["d"][:, k, :], m["rstd"], ALU.mult))
                do(dve.tensor_scalar(m["vn"][:, k, :], m["d"][:, k, :], V("sg_w", k), V("sg_b", k), ALU.mult, ALU.add), "sg_normed")
            for k in range(2):
                need("sg_mixed")
                mix = m["mix"][:, k, :].rearrange("p (n t) -> p n t", t=P)
                do(dve.tensor_tensor(mix, ps[4 + k][:].rearrange("p (n t) -> p n t", t=P),
                                     m["bs"][:, k, :].unsqueeze(1).broadcast_to((P, QB, P)), ALU.add))
                do(dve.tensor_tensor(m["mix"][:, k, :], m["mix"][:, k, :], m["z"][:, k, :], ALU.mult))
                both_parts(g_hi[:, 2 + k, :], g_lo[:, 2 + k, :], m["mix"][:, k, :], "sg_y")

            count = [0]

            def gated(f, glu_tiles=False):
                first = count[0] < 8
                bank = tile()
                need("gate")
                do(dve.tensor_tensor(merged[:, f, :] if first else product, bank[:], gate_room(count[0]), ALU.mult), "gated")
                count[0] += 1
                if glu_tiles:
                    skip(1)
                    need("glu_gate")
                    do(dve.tensor_tensor(product, product, glu, ALU.mult), "glu_used")
                if not first:
                    do(dve.tensor_tensor(merged[:, f, :], merged[:, f, :], product, ALU.add))

            skip(2)
            m = s5_m
            dve.wait_ge(S("s5_in"), 48)
            wide = lambda v: v.unsqueeze(2).broadcast_to((P, S5T, 16))
            bb, b_in, tmp = m["bb"], m["b_in"], m["w"][:, 5, 0:128].rearrange("p (s c) -> p s c", s=S5T)
            for out_part, (qa, qb), op in ((0, (qr, qi), ALU.subtract), (1, (qi, qr), ALU.add)):
                do(dve.tensor_tensor(bb[:, out_part], b_in[:, 0], wide(qa), ALU.mult))
                do(dve.tensor_tensor(tmp, b_in[:, 1], wide(qb), ALU.mult))
                do(dve.tensor_tensor(bb[:, out_part], bb[:, out_part], tmp, op))
            m8 = m["m8"].unsqueeze(3).broadcast_to((P, S5T, 8, 16))
            for part in range(2):
                do(dve.tensor_tensor(m["bpad"][:, part].rearrange("p s (g c) -> p s g c", g=8),
                                     bb[:, part].unsqueeze(2).broadcast_to((P, S5T, 8, 16)), m8, ALU.mult), "s5_bpad")
            need("s5_cT", 4)
            need("s5_bT", 4)
            for s in range(S5T):
                for part, sign in ((0, 1.0), (1, -1.0)):
                    src = ps[6 + part][:, (s // 4) * P:(s // 4) * P + P]
                    do(dve.scalar_tensor_tensor(m["cc"][:, part, s].rearrange("p (g c) -> p g c", g=8),
                                                src.rearrange("p (g c) -> p g c", g=8), sign,
                                                m["m8"][:, s].unsqueeze(2).broadcast_to((P, 8, 16)), ALU.mult, ALU.mult), "s5_cc")
            ct, st = m["ct"], m["st"]
            do(dve.memset(ct[:, :, 0:1], 1.0))
            do(dve.memset(st[:, :, 0:1], 0.0))
            do(dve.tensor_copy(pr, cs))
            do(dve.tensor_copy(pi, sn))
            L = 1
            while L < T:
                if 2 * L == T:
                    skip(4)
                    for f in range(4):
                        gated(f)
                cr = pr.unsqueeze(2).broadcast_to((P, S5T, L))
                ci = pi.unsqueeze(2).broadcast_to((P, S5T, L))
                tmp = m["w"].rearrange("p a b -> p (a b)")[:, 0:S5T * L].rearrange("p (s l) -> p s l", s=S5T)
                do(dve.tensor_tensor(ct[:, :, L:2 * L], ct[:, :, 0:L], cr, ALU.mult))
                do(dve.tensor_tensor(tmp, st[:, :, 0:L], ci, ALU.mult))
                do(dve.tensor_tensor(ct[:, :, L:2 * L], ct[:, :, L:2 * L], tmp, ALU.subtract))
                do(dve.tensor_tensor(st[:, :, L:2 * L], st[:, :, 0:L], cr, ALU.mult))
                do(dve.tensor_tensor(tmp, ct[:, :, 0:L], ci, ALU.mult))
                do(dve.tensor_tensor(st[:, :, L:2 * L], st[:, :, L:2 * L], tmp, ALU.add))
                do(dve.tensor_tensor(t1, pr, pr, ALU.mult))
                do(dve.tensor_tensor(t2, pi, pi, ALU.mult))
                do(dve.tensor_tensor(t3, pr, pi, ALU.mult))
                do(dve.tensor_tensor(pr, t1, t2, ALU.subtract))
                do(dve.tensor_scalar(pi, t3, 2.0, None, ALU.mult))
                L *= 2
            w = m["w"]
            for s in range(S5T):
                need("s5_bu", 2)
                re, im = ps[4][:], ps[5][:]
                cos, sin = ct[:, s, :], st[:, s, :]
                do(dve.tensor_tensor(w[:, 0, :], re, cos, ALU.mult))
                do(dve.tensor_tensor(w[:, 1, :], im, sin, ALU.mult))
                do(dve.tensor_tensor(w[:, 2, :], im, cos, ALU.mult))
                do(dve.tensor_tensor(w[:, 3, :], re, sin, ALU.mult), "s5_bu_used")
                do(dve.tensor_tensor(w[:, 0, :], w[:, 0, :], w[:, 1, :], ALU.add))
                do(dve.tensor_tensor(w[:, 1, :], w[:, 2, :], w[:, 3, :], ALU.subtract))
                decay = mag[:, s:s + 1].broadcast_to((P, T))
                do(dve.tensor_tensor_scan(w[:, 2, :], decay, w[:, 0, :], 0.0, ALU.mult, ALU.add))
                do(dve.tensor_tensor_scan(w[:, 3, :], decay, w[:, 1, :], 0.0, ALU.mult, ALU.add))
                if s > 0:
                    need("s5_read")
                do(dve.tensor_tensor(w[:, 0, :], w[:, 2, :], cos, ALU.mult))
                do(dve.tensor_tensor(w[:, 1, :], w[:, 3, :], sin, ALU.mult))
                do(dve.tensor_tensor(w[:, 4, :], w[:, 0, :], w[:, 1, :], ALU.subtract))
                do(dve.tensor_tensor(w[:, 0, :], w[:, 2, :], sin, ALU.mult))
                do(dve.tensor_tensor(w[:, 1, :], w[:, 3, :], cos, ALU.mult))
                do(dve.tensor_tensor(w[:, 5, :], w[:, 0, :], w[:, 1, :], ALU.add), "s5_states")
                gates, branch = BESIDE[s]
                skip(gates)
                if branch is not None:
                    for f in range(4):
                        gated((0 if s == 3 else 4) + f)
            for k in range(2):
                if k == 0:
                    need("s5_read")
                do(dve.scalar_tensor_tensor(w[:, k, :], m["u"][:, k, :], V("s5_d", k), ps[6 + k][:], ALU.mult, ALU.add), "s5_sum")
                need("s5_gelu")
                both_parts(g_hi[:, 4 + k, :], g_lo[:, 4 + k, :], w[:, 2 + k, :], "s5_y")
            vector_recurrence()

            modulate(2, 0, 8)
            for f in range(KT):
                gated(f)
                both_parts(h_hi[:, f, :], h_lo[:, f, :], merged[:, f, :], "merged")
            modulation(2)
            dve.wait_ge(S("x_in"), 16 * 5)

            def mixer_update(k):
                do(dve.scalar_tensor_tensor(x[:, k, :], tile()[:], mod[:, 16 + k:17 + k], x[:, k, :], ALU.mult, ALU.add), "x_done")
                modulate(3 + k // 4, 2 * (k % 4), 2 * (k % 4) + 2)

            last_terms(mixer_update)
            modulation(3, 2)
            gain2 = small[:, 23, :]
            do(dve.scalar_tensor_tensor(gain2, mod[:, 32:40], 1.0, V("g_ffn", 0, 8), ALU.add, ALU.mult))

            norm_start()
            norm(lambda k: gain2[:, k:k + 1], lambda k: mod[:, 24 + k:25 + k])

            def ffn_group(first, last):
                for j in range(8):
                    skip(1)
                    need("hidden_relu")
                    r, s = ff_m["r"][:, j % 2, :], ff_m["s"][:, j % 2, :]
                    do(dve.tensor_tensor(s, r, r, ALU.mult), "relu_used")
                    both_parts(g_hi[:, j, :], g_lo[:, j, :], s, "hidden")
                    if first:
                        modulate(5, j, j + 1)
                if first:
                    modulation(5)
                update = lambda k: do(dve.scalar_tensor_tensor(x[:, k, :], tile()[:], mod[:, 40 + k:41 + k], x[:, k, :],
                                                               ALU.mult, ALU.add), "x_done")
                if last:
                    last_terms(update, lambda k: mix_gain[:, k:k + 1], two_squares)
                else:
                    for k in range(KT):
                        update(k)

            do(dve.tensor_tensor(mix_gain, V("g_final1", 0, 8), V("g_mix2", 0, 8), ALU.mult), "mix_gain")
            for g in range(FF_GROUPS):
                ffn_group(g == 0, g == FF_GROUPS - 1)
            for layer in range(2):
                vector_layer(layer)
            need("rms_ready")
            do(dve.reciprocal(work[:, 3, :], work[:, 3, :]))
            for k in range(KT):
                do(dve.scalar_tensor_tensor(arena[:, k * T:k * T + T], x[:, k, :], V("g_final", k), work[:, 3, :], ALU.mult, ALU.mult), "result")

        @block.scalar
        def _(act):
            n = Counts()
            n.value["bank"] = 0

            def do(ins, name="act_step"):
                ins.then_inc(S(name), 1)
                act.wait_ge(S(name), n.next(name))

            def need(name, by=1):
                act.wait_ge(S(name), n.next(name, by))

            def tile():
                need("tile")
                n.value["bank"] += 1
                return ps[(n.value["bank"] - 1) % BANKS]

            def skip(tiles):
                n.next("tile", tiles)
                n.value["bank"] += tiles

            def rms(tiles, src, sq, bank, dst, width, ready=None):
                for k in range(tiles):
                    if ready is not None:
                        act.wait_ge(S("x_done"), ready + k + 1)
                    done = n.value.get("square", 0)
                    if done >= 2:
                        act.wait_ge(S("square_used"), done - 1)
                    do(act.activation(sq(k), src(k), ACT.Square), "square")
                need("squares_total")
                do(act.activation(dst, bank[:, 0:width], ACT.Sqrt, bias=small[:, 38, 0:1], scale=1.0 / D), "rms_ready")

            def rms_x(ready=None):
                rms(KT, lambda k: x[:, k, :], lambda k: work[:, k % 2, :], PB, work[:, 3, :], T, ready)

            def square(src, dst, gain=1.0):
                done = n.value.get("square", 0)
                if done >= 2:
                    act.wait_ge(S("square_used"), done - 1)
                do(act.activation(dst, src, ACT.Square, scale=gain), "square")

            def root(bank, dst, width=T):
                need("squares_total")
                do(act.activation(dst, bank[:, 0:width], ACT.Sqrt, bias=small[:, 38, 0:1], scale=1.0 / D), "rms_ready")

            def high_and_squares(ready, gain, first=None):
                for k in range(KT):
                    act.wait_ge(S("x_done"), ready + k + 1)
                    if first is None:
                        square(x[:, k, :], work[:, k % 2, :])
                    else:
                        square(x[:, k, :], work[:, 0, :])
                        square(x[:, k, :], work[:, 1, :], first(k))
                    do(act.activation(h_hi[:, k, :], x[:, k, :], ACT.Identity, scale=gain(k)), "h_high")
                root(PB, rstd)

            def values(i, width, layer):
                bank = tile()
                act.wait_ge(S("v_turned"), 8 * layer + i - 1)
                do(act.activation(rope_t[:, i % 2, 0:width], bank[:, 0:width], ACT.Copy), "v_copied")

            act.wait_ge(S("vec_in"), 16)
            do(act.activation(small[:, 1, :], V("c", 0, 8), ACT.Sigmoid), "silu_c")
            row = lambda i: small[:, i, :]
            lam, dt, e1, mag, th, kq, sn, sh, cs = (row(i) for i in range(3, 12))
            do(act.activation(dt, V("log_dt", 0, 8), ACT.Exp), "s5_dt")
            need("s5_e1")
            do(act.activation(mag, e1, ACT.Exp))
            need("s5_angle")
            do(act.activation(sn, th, ACT.Sin))
            do(act.activation(sh, th, ACT.Sin, scale=0.5), "s5_sines")
            act.wait_ge(S("eps_set"), 2)
            act.wait_ge(S("x_in"), 16)
            rms_x()
            skip(6)
            m = sg_m
            for k in range(4):
                do(act.activation(m["z"][:, k, :], tile()[:], ACT.Gelu_apprx_tanh), "act_freed")
            need("sg_var")
            do(act.activation(m["std"], PB[:], ACT.Sqrt, bias=small[:, 38, 1:2], scale=1.0 / DM), "sg_std")
            for k in range(2):
                need("sg_turned")
                do(act.activation(m["vt"][:, k].rearrange("p n c -> p (n c)"), ps[6 + k][:], ACT.Copy), "sg_vt")
            m = s5_m
            for k in range(2):
                do(act.activation(m["u"][:, k, :], tile()[:], ACT.Copy), "act_freed")
            for part in range(2):
                need("s5_bT", 2)
                for half in range(2):
                    do(act.activation(m["bt"][:, part, 4 * half:4 * half + 4].rearrange("p s c -> p (s c)"), ps[4 + half][:], ACT.Copy),
                       "s5_bt")
            count = [0, 0]

            def gate():
                bank = tile()
                if 4 <= count[0] < 28:
                    act.wait_ge(S("gated"), count[0] - 3)
                do(act.activation(gate_room(count[0]), bank[:], ACT.Sigmoid), "gate")
                count[0] += 1

            def glu_gate():
                skip(1)
                bank = tile()
                if count[1]:
                    act.wait_ge(S("glu_used"), count[1])
                do(act.activation(glu, bank[:], ACT.Sigmoid), "glu_gate")
                count[1] += 1

            for k in range(4):
                gate()
            skip(4)
            for gates, branch in BESIDE:
                for k in range(gates):
                    gate()
                if branch is not None:
                    skip(4)
            for k in range(2):
                need("s5_sum")
                do(act.activation(m["w"][:, 2 + k, :], m["w"][:, k, :], ACT.Gelu_apprx_tanh), "s5_gelu")
            v = rw_in
            act.wait_ge(S("lora_in"), 16)
            skip(7)
            need("rw_shifted")
            do(act.activation(v["m"][0:32, :], v["m"][0:32, :], ACT.Tanh), "rw_m")
            do(act.activation(v["m"][64:128, :], v["m"][64:128, :], ACT.Sigmoid), "rw_m")
            for k in range(2):
                need("rw_z")
                do(act.activation(v["lw"][:, k], ps[4 + k][:], ACT.Sigmoid, bias=V("w0", k)), "rw_decay")
            for k in range(2):
                need("rw_az")
                do(act.activation(v["a"][:, k], ps[6 + k][:], ACT.Sigmoid, bias=V("a0", k)), "rw_a")
            for k in range(2):
                need("rw_gz")
                do(act.activation(rw_pad["g"][:, k], ps[4 + k][:], ACT.Copy), "rw_g")
            for f in range(4):
                gate()
            for f in range(4):
                glu_gate()
            for k in range(2):
                need("rw_kk_floor")
                do(act.activation(v["e"][:, k], v["e"][:, k], ACT.Sqrt), "rw_kk_norm")
            for f in range(4):
                gate()
            for f in range(4):
                glu_gate()
            need("rw_exp_go")
            for k in range(2):
                if k:
                    act.wait_ge(S("rw_padded"), 2)
                do(act.activation(v["e"][:, 0], v["cum"][:, k], ACT.Exp), "rw_exp")
                need("rw_before")
                do(act.activation(v["e"][:, 1], v["lw"][:, k], ACT.Exp), "rw_exp")
                do(act.activation(v["e"][:, 0], v["cum"][:, k], ACT.Exp, scale=-1.0), "rw_exp")
            act.wait_ge(S("bd_used"), 18)
            for f in range(4):
                gate()

            def outputs(c):
                need("rec_o")
                for p in range(2):
                    rows = slice(64 * p, 64 * p + 64)
                    at = P + HD
                    do(act.activation(rw_sol["o"][rows, c, :], ps[6 + p][rows, at:at + HD], ACT.Copy), "rec_o_copied")

            for c in range(NCK):
                need("rec_y", 2)
                do(act.activation(chain_y[64:128, 0, :], ps[1][64:128, 0:HD], ACT.Copy), "rec_y_copied1")
                need("rec_sa", 2)
                do(act.activation(chain_y[64:128, 1, :], ps[7][64:128, 0:HD], ACT.Copy), "rec_sa_copied1")
                outputs(c)
            need("rw_var")
            do(act.activation(small[:, 31:33, :].rearrange("p a b -> p (a b)"), small[:, 31:33, :].rearrange("p a b -> p (a b)"),
                              ACT.Sqrt), "rw_std")
            for f in range(4):
                gate()
            skip(8)
            skip(8)
            rms_x(0)
            for g in range(FF_GROUPS):
                for j in range(8):
                    bank = tile()
                    if 8 * g + j >= 2:
                        act.wait_ge(S("relu_used"), 8 * g + j - 1)
                    do(act.activation(ff_m["r"][:, j % 2, :], bank[:], ACT.Relu), "hidden_relu")
                skip(8)
            need("mix_gain")
            for layer in range(2):
                if layer == 0:
                    high_and_squares(8 * FF_GROUPS, lambda k: mix_gain[:, k:k + 1], lambda k: V("g_final1", k))
                    n.next("squares_total")
                    need("second_square")
                    do(act.activation(work[:, 4, :], work[:, 4, :], ACT.Sqrt, bias=small[:, 38, 0:1], scale=1.0 / D), "rms_ready")
                else:
                    high_and_squares(X_DONE[1] - 8, lambda k: V("g_mix2", 8 + k))
                act.wait_ge(S("mem_in"), 16 * (layer + 1))
                if layer == 0:
                    for k in range(KT):
                        square(mem_in[:, k, :], mem_sq(k))
                    root(PB, mem_rstd, MT)
                    skip(12)
                else:
                    for i in range(12):
                        bank = tile()
                        if i >= 2:
                            act.wait_ge(S("rope_done"), i - 1)
                        do(act.activation(rope_t[:, i % 2, :], bank[:], ACT.Copy, scale=HD ** -0.5 if i < 6 else 1.0), "rope_copied")
                        if i < KT:
                            square(mem_in[:, i, :], mem_sq(i))
                        elif i == 9:
                            root(PB, mem_rstd, MT)
                skip(6)
                if layer == 0:
                    skip(1)
                    need("forget_in_abs")
                    f = lambda i: work[0:NH, i, :]
                    do(act.activation(f(3), f(1), ACT.Exp))
                    do(act.activation(f(1), f(3), ACT.Ln, bias=1.0), "forget_log")
                skip(4)
                for i in range(2):
                    values(6 + i, MT, layer)
                def head_high(head):
                    rows = slice(64 * (head % 2), 64 * (head % 2) + 64)
                    do(act.activation(g_hi[rows, head // 2, :], ps[6 + head % 2][rows, :], ACT.Copy), "head_hi")

                for s in range(len(UNITS) + 2):
                    if s < len(UNITS):
                        head, qb, width, at = UNITS[s]
                        pr, small_u = probs[s % 4][:, 0:width], small[:, 33 + s % 4, :]
                        need("score_top")
                        src = pr if head < NH and layer == 1 else ps[s % BANKS][:, 0:width]
                        do(act.activation(pr, src, ACT.Exp, bias=small_u[:, 0:1], accum_out=small_u[:, 2:3]), "exped")
                    if s >= 2:
                        u = s - 2
                        head, qb, width, at = UNITS[u]
                        if qb == 0 and head:
                            need("head_out")
                        need("probs_turned")
                        blocks = width // P
                        do(act.activation(at_m["pt"][:, 0:blocks, P * qb:P * qb + P],
                                          ps[4 + u % 2][:, 0:width].rearrange("p (a b) -> p a b", a=blocks), ACT.Copy), "probs_kept")
                        if qb == 0 and head:
                            head_high(head - 1)
                need("head_out")
                head_high(NH + NMH - 1)
                skip(8)
                high_and_squares(X_DONE[layer], lambda k: V("g_ffn2", 8 * layer + k))
                for group, width in enumerate(FF2_GROUPS):
                    j0 = sum(FF2_GROUPS[:group])
                    for j in range(width):
                        for side, c in ((0, cv_m["cv"]), (1, cv_m["cg"])):
                            skip(1)
                            need("conv_scaled")
                            done = 22 * layer + j0 + j
                            if done >= 2:
                                act.wait_ge(S("conv_used"), done - 1)
                            at = (3 * layer + 2) * 44 + 22 * side + j0 + j
                            do(act.activation(c[:, j % 2, :], cv_m["z"][:, side, :], ACT.Identity, scale=V("cw2", at),
                                              bias=V("cb2", 44 * layer + 22 * side + j0 + j)), "conv_first")
                        need("conv_summed", 2)
                        do(act.activation(cv_m["sg"][:, j % 2, :], cv_m["cg"][:, j % 2, :], ACT.Silu), "conv_gate")
                    skip(8)
            rms_x(X_DONE[1] + 8 + 16)

        @block.tensor
        def _(pe):
            n = Counts()
            piece, t = [0], [0]
            squares = [0]
            freed = []

            def need(name, by=1):
                pe.wait_ge(S(name), n.next(name, by))

            def open_piece():
                pe.wait_ge(S("w_split"), piece[0] + 1)
                slot = piece[0] % SPLIT
                piece[0] += 1
                return slot

            def product(slot, blocks, hi, lo, owner, width=T, first_block=0, ready=None, first=True, close=True):
                if len(freed) >= BANKS:
                    pe.wait_ge(S(freed[-BANKS][0]), freed[-BANKS][1])
                bank = ps[t[0] % BANKS][:, 0:width]
                for k in range(blocks):
                    if ready is not None:
                        ready(k)
                    cols = slice(P * (first_block + k), P * (first_block + k) + P)
                    for i, (w, a) in enumerate(((w_hi, hi), (w_hi, lo), (w_lo, hi))):
                        mm = pe.matmul(bank, w[:, slot, cols], a(k), start=(k == 0 and i == 0), stop=(k == blocks - 1 and i == 2))
                        if first and k == 0 and i == 0 and piece[0] > 1:
                            mm.then_inc(S("w_used"), 1)
                mm.then_inc(S("tile"), 1)
                t[0] += 1
                freed.append((owner, n.next(owner)))

            of = lambda pair: (lambda k: pair[:, k, :])
            h = (of(h_hi), of(h_lo))

            def project(tiles, owner, operand=h, width=T, blocks=8, ready=None):
                for i in range(tiles):
                    slot = open_piece()
                    product(slot, blocks, *operand, owner if isinstance(owner, str) else owner[i], width,
                            ready=ready if i == 0 else None)

            def h_tile(k):
                need("h_ready")

            def modulation(group):
                pe.wait_ge(S("ada_sum"), group + 1)
                for k in range(8):
                    mm = pe.matmul(PA[:, 8 * group + k:8 * group + k + 1], ada_m["sum"][:, group % 2, P * k:P * k + P], K("ones")[:, 0:1],
                                   start=True, stop=True)
                mm.then_inc(S("ada_total"), 1)

            def total_squares(acc, width=T, count=KT, bank=PB):
                squares[0] += count
                pe.wait_ge(S("square_used"), squares[0])
                pe.matmul(bank[:, 0:width], K("ones"), acc, start=True, stop=True).then_inc(S("squares_total"), 1)

            def swap(i):
                pe.wait_ge(S("rope_copied"), i + 1)
                if i >= 2:
                    pe.wait_ge(S("rope_done"), i - 1)
                pe.matmul(ps[6 + i % 2][:], K("rot"), rope_t[:, i % 2, :], start=True, stop=True).then_inc(S("rope_swapped"), 1)

            def turn_values(i, width, layer):
                if i < 6:
                    pe.wait_ge(S("v_scaled"), 6 * layer + i + 1)
                else:
                    pe.wait_ge(S("v_copied"), 2 * layer + i - 5)
                if i >= 2:
                    pe.wait_ge(S("v_taken"), 8 * layer + i - 1)
                elif layer:
                    pe.wait_ge(S("rope_done"), 12)
                for b in range(width // P):
                    mm = pe.transpose(ps[6 + i % 2][:, P * b:P * b + P], rope_t[:, i % 2, P * b:P * b + P], K("ident"))
                mm.then_inc(S("v_turned"), 1)

            def attention(layer):
                before, heads = len(UNITS) * layer, (NH + NMH) * layer
                pe.wait_ge(S("v_taken"), 8 * (layer + 1))
                if layer == 0:
                    pe.wait_ge(S("forget_in"), 16)

                def scores(u):
                    head, qb, width, _ = UNITS[u]
                    if u >= BANKS:
                        pe.wait_ge(S("exped"), before + u - BANKS + 1)
                    mixing = head < NH
                    rows = HD + 1 if layer == 0 and mixing else HD
                    keys = at_m["k"][0:rows, head, 0:width] if mixing else at_m["km"][0:rows, head - NH, :]
                    masked = layer == 0 and mixing
                    mm = pe.matmul(ps[u % BANKS][:, 0:width], at_m["q"][0:rows, head, P * qb:P * qb + P], keys,
                                   start=True, stop=not masked)
                    if masked:
                        mm = pe.matmul(ps[u % BANKS][:, P * qb:P * qb + P], K("ident"), masks[:, 0:P], start=False, stop=True)
                    mm.then_inc(S("scores"), 1)

                def head_output(head):
                    pe.wait_ge(S("probs_kept"), before + QB * head + QB)
                    if head >= 2:
                        pe.wait_ge(S("heads"), heads + head - 1)
                    out_rows = slice(64 * (head % 2), 64 * (head % 2) + 64)
                    blocks = QB if head < NH else MT // P
                    for b in range(blocks):
                        q0 = P * b if head < NH else 0
                        values = at_m["v"][:, b, HD * head:HD * head + HD] if head < NH else \
                            at_m["vm"][:, b, HD * (head - NH):HD * (head - NH) + HD]
                        mm = pe.matmul(ps[6 + head % 2][out_rows, q0:T], values, at_m["pt"][:, b, q0:T],
                                       start=(b == 0), stop=(b == blocks - 1))
                    mm.then_inc(S("head_out"), 1)

                pe.wait_ge(S("mask_in"), 16 * (layer + 1))
                scores(0)
                scores(1)
                for u, (head, qb, width, _) in enumerate(UNITS):
                    if u + 2 < len(UNITS):
                        scores(u + 2)
                    pe.wait_ge(S("probs"), before + u + 1)
                    if u >= 2:
                        pe.wait_ge(S("probs_kept"), before + u - 1)
                    for b in range(width // P):
                        mm = pe.transpose(ps[4 + u % 2][:, P * b:P * b + P], probs[u % 4][:, P * b:P * b + P], K("ident"))
                    mm.then_inc(S("probs_turned"), 1)
                    if qb == 0 and head:
                        head_output(head - 1)
                head_output(NH + NMH - 1)

            pe.wait_ge(S("con_in"), 16)
            total_squares(work[:, 2, :])
            modulation(0)
            modulation(1)
            project(10, ["dve_freed"] * 6 + ["act_freed"] * 4, ready=h_tile)
            project(2, "act_freed")

            m = sg_m
            pe.wait_ge(S("act_freed"), 4)
            for k in range(2):
                mm = pe.matmul(PA[:], K("ones"), m["z"][:, 2 + k, :], start=(k == 0), stop=(k == 1))
            mm.then_inc(S("sg_mean"), 1)
            for k in range(2):
                need("sg_square")
                mm = pe.matmul(PB[:], K("ones"), m["sq"][:, k, :], start=(k == 0), stop=(k == 1))
            mm.then_inc(S("sg_var"), 1)
            for k in range(2):
                need("sg_normed")
                for b in range(QB):
                    mm = pe.transpose(ps[6 + k][:, P * b:P * b + P], m["vn"][:, k, P * b:P * b + P], K("ident"))
                mm.then_inc(S("sg_turned"), 1)
            need("sg_w_masked")
            for k in range(2):
                need("sg_vt")
                for g in range(2):
                    for b in range(QB):
                        mm = pe.matmul(ps[4 + k][64 * g:64 * g + 64, P * b:P * b + P], m["vt"][:, k, b, 64 * g:64 * g + 64],
                                       m["wsm"][:, 2 * k + g, :], start=True, stop=True)
                mm.then_inc(S("sg_mixed"), 1)

            m = s5_m
            pe.wait_ge(S("s5_in"), 48)
            for k in range(2):
                for part in range(2):
                    pe.transpose(ps[6 + part][:, P * k:P * k + P], m["c_in"][:, part, k, :], K("ident")).then_inc(S("s5_cT"), 1)
            for part in range(2):
                need("s5_bpad")
                if part == 1:
                    pe.wait_ge(S("s5_bt"), 2)
                pe.wait_ge(S("sg_y"), 2)
                for half in range(2):
                    for s in range(4):
                        mm = pe.transpose(ps[4 + half][:, P * s:P * s + P], m["bpad"][:, part, 4 * half + s, :], K("ident"))
                    mm.then_inc(S("s5_bT"), 1)
            pe.wait_ge(S("s5_bt"), 4)
            pe.wait_ge(S("act_freed"), 6)
            pe.wait_ge(S("s5_cc"), 16)
            def inputs(s):
                for part in range(2):
                    pe.matmul(ps[4 + part][:], m["bt"][:, part, s, :], m["u"][:, s // 4, :], start=True, stop=True).then_inc(S("s5_bu"), 1)

            def branch_out(b, tiles, glu_tiles=False):
                y = (lambda k: g_hi[:, 2 * b + k, :], lambda k: g_lo[:, 2 * b + k, :])
                for q in range(tiles // 4):
                    slot = open_piece()
                    for i in range(4):
                        product(slot, 2, *y, "glu_gate" if glu_tiles and i % 2 else "gated", first_block=2 * i, first=(i == 0))

            inputs(0)
            project(4, "gate")
            pe.wait_ge(S("conv_y"), 2)
            branch_out(0, 4)
            for s, (gates, branch) in enumerate(BESIDE):
                project(gates, "gate")
                if s < S5T - 1:
                    need("s5_bu_used")
                    inputs(s + 1)
                if branch is not None:
                    pe.wait_ge(S("sg_y" if branch else "conv_y"), 2)
                    branch_out(branch, 4)
                need("s5_states")
                for part in range(2):
                    mm = pe.matmul(ps[6 + s // 4][:], m["cc"][:, part, s, :], m["w"][:, 4 + part, :],
                                   start=(s % 4 == 0 and part == 0), stop=(s % 4 == 3 and part == 1))
                mm.then_inc(S("s5_read"), 1)

            project(7, "dve_freed")
            v, bd = rw_in, rw_bd
            project(4, "gate")
            pe.wait_ge(S("lora_in"), 16)
            pe.wait_ge(S("rw_m"), 2)
            for rows, names, banks in ((slice(0, 32), "rw_z", (4, 5)), (slice(32, 64), "rw_az", (6, 7)), (slice(64, 128), "rw_gz", (4, 5))):
                for k in range(2):
                    if names == "rw_gz":
                        pe.wait_ge(S("rw_decay"), k + 1)
                    elif names == "rw_z":
                        pe.wait_ge(S("s5_sum"), 2)
                    pe.matmul(ps[banks[k]][:], lora[rows, P * k:P * k + P], v["m"][rows, :], start=True, stop=True).then_inc(S(names), 1)
            pe.wait_ge(S("s5_y"), 2)
            branch_out(2, 8, glu_tiles=True)
            for k in range(2):
                need("rw_kk_square")
                pe.wait_ge(S("rw_g"), k + 1)
                pe.matmul(ps[4 + k][:], K("hsum"), v["e"][:, k], start=True, stop=True).then_inc(S("rw_kk_sum"), 1)
            project(4, "gate")
            for k in range(2):
                need("rw_rk")
                pe.wait_ge(S("rw_a"), k + 1)
                pe.matmul(ps[6 + k][:], K("hsum"), v["e"][:, k], start=True, stop=True).then_inc(S("rw_rk_sum"), 1)
            branch_out(2, 8, glu_tiles=True)
            pe.wait_ge(S("rw_padded"), 4)
            banks = [0]

            def blocks(lhs, rhs, width, per):
                for q in range(NCK // per):
                    i = banks[0]
                    if i >= 4:
                        pe.wait_ge(S("bd_used"), i - 3)
                    banks[0] += 1
                    for c in range(per):
                        for p in range(2):
                            mm = pe.matmul(ps[4 + i % 4][64 * p:64 * p + 64, width * c:width * c + width], lhs(p, per * q + c),
                                           rhs(p, per * q + c), start=True, stop=True)
                    mm.then_inc(S("bd"), 1)

            pad = lambda name: (lambda p, c: rw_pad[name][:, p, c].rearrange("a h t -> a (h t)"))
            blocks(pad("a"), pad("b"), 64, 8)
            blocks(pad("k"), pad("a"), 64, 8)
            blocks(pad("k"), pad("r"), 64, 8)
            blocks(pad("b"), pad("r"), 64, 8)
            blocks(pad("k"), lambda p, c: K("ident"), P, 4)
            pe.wait_ge(S("v_padded"), 4)
            blocks(pad("k"), lambda p, c: K("stack"), 64, 8)
            blocks(pad("b"), lambda p, c: K("ident"), P, 4)
            project(4, "gate")
            pe.wait_ge(S("tT_in"), 16 * 8)
            pe.wait_ge(S("bd_used"), 18)
            pe.wait_ge(S("gate"), 28)
            need("state_set")
            rows = [slice(0, 64), slice(64, 128)]
            at_s, at_o = slice(P, P + HD), slice(P + HD, P + 2 * HD)
            for c in range(NCK):
                now = c % 2
                for p in range(2):
                    pe.matmul(ps[p][rows[p], 0:HD], bd["akT"][rows[p], c, :], bd["vt"][rows[p], c, :], start=True, stop=False)
                for p in range(2):
                    if c:
                        need("state_set")
                    pe.matmul(ps[p][rows[p], 0:HD], pad("a")(p, c), state[:, now, p, :], start=False, stop=True).then_inc(S("rec_y"), 1)
                if c:
                    need("rec_o_copied", 2)
                for p in range(2):
                    need("rec_y_copied1" if p else "rec_y_copied")
                    pe.matmul(ps[6 + p][rows[p], 0:HD], bd["tT"][rows[p], c, :], chain_y[rows[p], 0, :],
                              start=True, stop=True).then_inc(S("rec_sa"), 1)
                for p in range(2):
                    pe.matmul(ps[4 + p][:, at_s], bd["kt"][rows[p], c, :], bd["vt"][rows[p], c, :], start=True, stop=False)
                for p in range(2):
                    need("rec_sa_copied1" if p else "rec_sa_copied")
                    pe.matmul(ps[4 + p][:, at_s], rw_bt[rows[p], c, :], chain_y[rows[p], 1, :], start=False, stop=True).then_inc(S("rec_state"), 1)
                for p in range(2):
                    pe.matmul(ps[6 + p][rows[p], at_o], pad("r")(p, c), state[:, now, p, :], start=True, stop=False)
                    pe.matmul(ps[6 + p][rows[p], at_o], bd["rbT"][rows[p], c, :], chain_y[rows[p], 1, :], start=False, stop=False)
                    mm = pe.matmul(ps[6 + p][rows[p], at_o], bd["rkT"][rows[p], c, :], bd["vt"][rows[p], c, :], start=False, stop=True)
                mm.then_inc(S("rec_o"), 1)
            project(3, "gate")
            pe.wait_ge(S("o_padded"), 2)
            opad = rw_pad["a"].rearrange("p a n h c -> p (a n h c)").rearrange("p (n x) -> p n x", n=NCK)
            for p in range(2):
                rows = slice(64 * p, 64 * p + 64)
                for c in range(NCK):
                    mm = pe.matmul(ps[4 + p][:, C * c:C * c + C], opad[rows, c, :], K("sum32")[rows, :], start=True, stop=True)
                mm.then_inc(S("rw_o"), 1)

            project(1, "gate")
            pe.wait_ge(S("rw_out"), 2)
            for half in range(2):
                branch_out(3, 4)
            modulation(2)
            project(7, "x_done", ready=lambda k: need("merged"))
            modulation(3)
            project(1, "x_done")
            modulation(4)
            g = (of(g_hi), of(g_lo))
            hidden = lambda k: need("hidden")
            total_squares(work[:, 2, :])
            for group in range(FF_GROUPS):
                project(8, "hidden_relu", ready=h_tile if group == 0 else None)
                project(2, "x_done", operand=g, ready=hidden)
                if group == 0:
                    modulation(5)
                project(6, "x_done", operand=g)
            n.next("x_done", 8)
            for layer in range(2):
                if layer == 0:
                    project(1, "dve_freed", ready=h_tile)
                    total_squares(work[:, 2, :], count=2 * KT)
                    total_squares(work[:, 3, :], count=0, bank=PA)
                    project(9, "dve_freed")
                    total_squares(mem_total, MT)
                    project(2, "dve_freed")
                else:
                    for i in range(12):
                        project(1, "rope_copied", ready=h_tile if i == 0 else None)
                        if i == 0:
                            total_squares(work[:, 2, :])
                        else:
                            swap(i - 1)
                        if i == 9:
                            total_squares(mem_total, MT)
                    swap(11)
                for i in range(6):
                    project(1, "v_scaled")
                    if i:
                        turn_values(i - 1, T, layer)
                turn_values(5, T, layer)
                project(3 if layer == 0 else 2, "dve_freed")
                mem = (lambda k: mn(g_hi, k), lambda k: mn(g_lo, k))
                project(2, "dve_freed", operand=mem, width=MT, ready=lambda k: need("mem_ready"))
                for i in range(2):
                    project(1, "v_copied", operand=mem, width=MT)
                    if i:
                        turn_values(6, MT, layer)
                turn_values(7, MT, layer)
                attention(layer)
                pe.wait_ge(S("heads"), 16 * (layer + 1))
                project(8, "x_done", operand=g)
                for group, pairs in enumerate(FF2_GROUPS):
                    if group == 0:
                        project(1, "conv_scaled", ready=h_tile)
                        total_squares(work[:, 2, :])
                    project(2 * pairs - (group == 0), "conv_scaled")
                    project(8, "x_done", operand=g, blocks=pairs, ready=hidden)
            total_squares(work[:, 2, :])


def pieces_of(w):
    k = w.shape[0] // P
    out = np.zeros((w.shape[1] // P, P, D), w.dtype)
    out[:, :, :k * P] = w.reshape(k, P, -1, P).transpose(2, 1, 0, 3).reshape(-1, P, k * P)
    return out


def small_pieces_of(w):
    return w.reshape(2, P, -1, 4, P).transpose(2, 1, 3, 0, 4).reshape(-1, P, D)


def columns(v):
    return v.reshape(-1, P).T


def constants():
    i, j = np.arange(P)[:, None], np.arange(64)[None, :]
    same = (i // C % 2) == (j // C)
    rot = np.zeros((P, P))
    for k in range(P):
        if k % HD < HD // 2:
            rot[k, k + HD // 2] = 1
        else:
            rot[k, k - HD // 2] = -1
    con = {"ident": np.eye(P), "ones": np.ones((P, P)), "hsum": np.kron(np.eye(2), np.ones((HD, HD))),
           "lt": same & (j % C < i % C), "gt": same & (j % C > i % C), "ge": same & (j % C >= i % C),
           "stack": (i % HD) == j, "sum32": (i % C) == np.arange(C)[None, :], "hm": (i // C % 2) == np.arange(2)[None, :],
           "rot": rot}
    con = np.concatenate([con[name] for name in CON], axis=1).astype(np.float32)
    c = np.arange(C // 2)[None, :, None] + (C // 2) * (np.arange(P)[:, None, None] // 64)
    eye = (c == np.arange(C)[None, None, :]).reshape(P, -1).astype(np.float32)
    q, k = np.arange(T)[:, None], np.arange(T)[None, :]
    fox = np.where(k <= q, 0.0, NEG)
    d = q - k
    count = ((d >= 0) & (d <= P)).astype(int) + ((d >= 0) & (d % 4 == 0)) + ((d >= 0) & (d % 16 == 0))
    dil = np.where(count > 0, np.log(np.maximum(count, 1)), NEG)
    by_block = lambda m: np.concatenate([m[b * P:b * P + P, 0:(b + 1) * P] for b in range(QB)], axis=1).astype(np.float32)
    inv = (np.float32(1.0) / np.float32(10000.0) ** (np.arange(0, HD, 2, dtype=np.float32) / np.float32(HD))).astype(np.float32)
    ang = np.arange(T, dtype=np.float32)[:, None] * inv[None, :]
    rope = np.stack([np.tile(np.cos(ang).T, (4, 1)), np.tile(np.sin(ang).T, (4, 1))], axis=1).astype(np.float32)
    m8 = np.zeros((P, S5T, 8), np.float32)
    for s in range(S5T):
        for g in range(2):
            m8[64 * g:64 * g + 64, s, (2 * s + g) % 8] = 1
    caus = (np.arange(P)[:, None] <= np.arange(P)[None, :]).astype(np.float32)
    return dict(con=con, eye=eye, mask_fox=by_block(fox), mask_dil=by_block(dil), rope=rope, s5_m8=m8, caus=caus)


def layout(i):
    i = {k: np.asarray(v) for k, v in i.items()}
    first = {k: v[0] for k, v in i.items() if not k.endswith("_2") and v.ndim > 1 and v.shape[0] == 1}
    w_in = first["w_in"]
    a_cols = 3 * DM + 128
    off_c, off_d, off_g = a_cols + 2 * DM, a_cols + 5 * DM, a_cols + 6 * DM
    glu = first["s5_glu_w"].reshape(DM, 2, KT, P).transpose(0, 2, 1, 3).reshape(DM, 2 * D)
    gates = pieces_of(w_in[:, off_g:])
    sources = {"conv_in": pieces_of(w_in[:, off_c:off_d]), "sg_in": pieces_of(w_in[:, a_cols:off_c]),
               "s5_in": pieces_of(w_in[:, off_d:off_g]), "rwkv_in": pieces_of(w_in[:, :a_cols]),
               "rwkv_gate": gates[0:8], "sg_gate": gates[8:16], "conv_gate": gates[16:24], "s5_gate": gates[24:32],
               "rwkv_out": small_pieces_of(first["rwkv_out"]), "sg_out": small_pieces_of(first["sg_out"]),
               "conv_out": small_pieces_of(first["conv_out"]), "s5_out": small_pieces_of(glu)}
    stream = []
    for what, n in mixer_pieces():
        stream.append(sources[what][:n])
        sources[what] = sources[what][n:]
    stream.append(pieces_of(first["w_o"]))
    for g in range(FF_GROUPS):
        cut = slice(g * D, g * D + D)
        stream += [pieces_of(first["ffn_w1"][:, cut]), pieces_of(first["ffn_w2"][cut])]
    dmix = NH * HD
    for layer, w in ((0, i["w_in_fox_2"][0]), (1, i["w_in_dil_2"][0])):
        if layer == 0:
            forget = np.zeros((D, P), w.dtype)
            forget[:, :NH] = w[:, 3 * dmix:3 * dmix + NH]
            w = np.concatenate([w[:, :3 * dmix], forget, w[:, 3 * dmix + NH:]], axis=1)
        up, down = i["w_up_2"][layer], i["w_down_2"][layer]
        stream += [pieces_of(w), pieces_of(i["w_mem_kv_2"][layer]), pieces_of(i["w_out_2"][layer])]
        pairs = pieces_of(up.reshape(D, 2, FF2, P).transpose(0, 2, 1, 3).reshape(D, -1))
        at = 0
        for n in FF2_GROUPS:
            stream += [pairs[2 * at:2 * at + 2 * n], pieces_of(down[at * P:(at + n) * P])]
            at += n
    f = first
    vec = {"c": columns(i["c"][0]), "ada_b": columns(f["ada_b"]), "g_mix": columns(f["norm_mix_g"]), "mu": columns(f["rwkv_mu"]),
           "w0": columns(f["rwkv_w0"]), "a0": columns(f["rwkv_a0"]), "kk": columns(f["rwkv_kk"]), "ka": columns(f["rwkv_ka"]),
           "rk": columns(f["rwkv_rk"].reshape(-1)), "sg_w": columns(f["sg_ln_w"]), "sg_b": columns(f["sg_ln_b"]),
           "conv_w": columns(f["conv_w"].reshape(-1)), "s5_d": columns(f["s5_d"]),
           "a_re": columns(f["s5_a_re"].reshape(-1)), "a_im": columns(f["s5_a_im"].reshape(-1)),
           "log_dt": columns(np.repeat(f["s5_log_dt"], 64)), "g_ffn": columns(f["norm_ffn_g"]), "g_final1": columns(i["final_g"]),
           "g_mix2": columns(i["norm_mix_2"].reshape(-1)), "g_mem2": columns(i["norm_mem_2"].reshape(-1)),
           "g_ffn2": columns(i["norm_ffn_2"].reshape(-1)),
           "b_f": np.concatenate([i["b_forget_2"][0], np.zeros(P - NH, np.float32)])[:, None],
           "cw2": columns(i["conv_w_2"].reshape(-1)), "cb2": columns(i["conv_b_2"].reshape(-1)),
           "g_final": columns(i["norm_final_2"]),
           "lnx_w": np.repeat(f["rwkv_lnx_w"].reshape(H_A, HD), C, axis=0), "lnx_b": np.repeat(f["rwkv_lnx_b"].reshape(H_A, HD), C, axis=0)}
    b = np.stack([f["s5_b_re"], f["s5_b_im"]])
    c = np.stack([f["s5_c_re"], f["s5_c_im"]])
    arrays = dict(
        w=np.concatenate(stream), ada=f["ada_w"].reshape(KT, P, 6, D).transpose(2, 0, 1, 3).reshape(-1, P, D), vec=np.concatenate([vec[name] for name in VEC], axis=1),
        xT=i["x"][0].reshape(T, KT, P).transpose(2, 1, 0), memT=i["mem_2"][0].reshape(MT, KT, P).transpose(2, 1, 0),
        sg_ws=f["sg_ws"].transpose(2, 0, 1), sg_bs=np.repeat(f["sg_bs"].reshape(2, 2, 1, P), 64, axis=2).transpose(1, 2, 0, 3).reshape(P, 2, P),
        s5_b=b.reshape(2, S5T, P, 16).transpose(2, 0, 1, 3),
        s5_c=np.concatenate([c, c], axis=3).reshape(2, 2, P, P).transpose(2, 0, 1, 3),
        lora=np.concatenate([f["rwkv_w2"], f["rwkv_a2"], f["rwkv_g2"]]), **constants())
    return {k: np.ascontiguousarray(v) for k, v in arrays.items()}


def kernel(**inputs):
    import concourse.bacc as bacc
    from concourse.bass_utils import run_bass_kernel_spmd

    nc = bacc.Bacc("TRN2", target_bir_lowering=False, num_devices=1)
    arrays = layout(inputs)
    aps = {k: nc.dram_tensor(f"in_{k}", v.shape, mybir.dt.from_np(v.dtype), kind="ExternalInput").ap() for k, v in arrays.items()}
    out = nc.dram_tensor("out_y", (P, KT, T), F32, kind="ExternalOutput").ap()
    build(nc, aps, out)
    r = run_bass_kernel_spmd(nc, [{f"in_{k}": v for k, v in arrays.items()}], core_ids=[0])
    y = r.results[0]["out_y"]
    return np.ascontiguousarray(y.transpose(2, 1, 0)).reshape(1, T, D)
```
